# Optimizing a Trainium2 kernel written in Bass

```python
import jax, jax.numpy as jnp
from jax import lax
import numpy as np
import jax
import jax.numpy as jnp

D_MODEL = 1024
BATCH = 1
SEQ = 256
DEPTH = 1

HEAD_DIM = 64
RMS_EPS = 1e-6
NEG_INF = -1e30
ATTN_SCALE = HEAD_DIM ** -0.5

POOL_WIDTH = 512
POOL_GROUPS = 4
POOL_GROUP_DIM = POOL_WIDTH // POOL_GROUPS
POOL_WINDOWS = (2, 4, 8, 16)

SWA_Q_HEADS = 8
SWA_KV_HEADS = 2
SWA_GROUP = SWA_Q_HEADS // SWA_KV_HEADS
SWA_WINDOW = 128
SWA_BLOCK = 128
SWA_WIDTH = SWA_Q_HEADS * HEAD_DIM
SWA_KV_WIDTH = SWA_KV_HEADS * HEAD_DIM

MOBA_HEADS = 8
MOBA_BLOCK = 256
MOBA_TOPK = 3
MOBA_Q_CHUNK = 64
MOBA_WIDTH = MOBA_HEADS * HEAD_DIM

N_BRANCH = 3
IN_SIZES = (POOL_WIDTH, POOL_WIDTH,
            SWA_WIDTH, SWA_KV_WIDTH, SWA_KV_WIDTH, SWA_WIDTH,
            MOBA_WIDTH, MOBA_WIDTH, MOBA_WIDTH, MOBA_WIDTH,
            N_BRANCH * D_MODEL)
IN_WIDTH = sum(IN_SIZES)


def _rmsnorm(x, g):
    x32 = x.astype(jnp.float32)
    y = x32 * lax.rsqrt(jnp.mean(x32 * x32, axis=-1, keepdims=True) + RMS_EPS)
    return (y * g.astype(jnp.float32)).astype(x.dtype)

def _pool_mixer(xa, w_pool, scale):
    b, s, _ = xa.shape
    x32 = xa.astype(jnp.float32)
    cs = jnp.cumsum(x32, axis=1)
    t = jnp.arange(s)
    outs = []
    for gi, w in enumerate(POOL_WINDOWS):
        cg = cs[..., gi * POOL_GROUP_DIM:(gi + 1) * POOL_GROUP_DIM]
        lag = jnp.pad(cg, ((0, 0), (w, 0), (0, 0)))[:, :s]
        cnt = jnp.minimum(t + 1, w).astype(jnp.float32)
        outs.append((cg - lag) / cnt[None, :, None])
    pooled = (jnp.concatenate(outs, axis=-1) - x32).astype(xa.dtype)
    pooled = pooled.reshape(b, s, POOL_GROUPS, POOL_GROUP_DIM)
    mixed = jnp.einsum('bsgc,gcd->bsgd', pooled, w_pool).reshape(b, s, POOL_WIDTH)
    return mixed * scale

def _swa_attention(q, k, v, sinks):
    b, s = q.shape[0], q.shape[1]
    nb = s // SWA_BLOCK
    qb = q.reshape(b, nb, SWA_BLOCK, SWA_KV_HEADS, SWA_GROUP, HEAD_DIM)
    kb = k.reshape(b, nb, SWA_BLOCK, SWA_KV_HEADS, HEAD_DIM)
    vb = v.reshape(b, nb, SWA_BLOCK, SWA_KV_HEADS, HEAD_DIM)

    def with_prev(t):
        prev = jnp.pad(t[:, :-1], ((0, 0), (1, 0), (0, 0), (0, 0), (0, 0)))
        return jnp.concatenate([prev, t], axis=2)

    kk = with_prev(kb)
    vv = with_prev(vb)
    sc = jnp.einsum('bnqhgd,bnkhd->bnhgqk', qb, kk,
                    preferred_element_type=jnp.float32) * ATTN_SCALE
    qi = jnp.arange(SWA_BLOCK)[:, None] + SWA_BLOCK
    kj = jnp.arange(2 * SWA_BLOCK)[None, :]
    diff = qi - kj
    band = (diff >= 0) & (diff < SWA_WINDOW)
    kpos = jnp.arange(nb)[:, None, None] * SWA_BLOCK + kj[None] - SWA_BLOCK
    valid = band[None] & (kpos >= 0)
    sc = jnp.where(valid[None, :, None, None], sc, NEG_INF)
    sink = sinks.astype(jnp.float32).reshape(1, 1, SWA_KV_HEADS, SWA_GROUP, 1)
    m = jnp.maximum(jnp.max(sc, axis=-1), sink)
    p = jnp.exp(sc - m[..., None])
    denom = jnp.sum(p, axis=-1) + jnp.exp(sink - m)
    p = (p / denom[..., None]).astype(v.dtype)
    o = jnp.einsum('bnhgqk,bnkhd->bnqhgd', p, vv)
    return o.reshape(b, s, SWA_WIDTH)

def _moba_attention(q, k, v):
    b, s = q.shape[0], q.shape[1]
    nblk = -(-s // MOBA_BLOCK)
    s_pad = nblk * MOBA_BLOCK
    pad = ((0, 0), (0, s_pad - s), (0, 0), (0, 0))
    q = jnp.pad(q, pad)
    k = jnp.pad(k, pad)
    v = jnp.pad(v, pad)
    topk = min(MOBA_TOPK, nblk)
    kb = k.reshape(b, nblk, MOBA_BLOCK, MOBA_HEADS, HEAD_DIM)
    vb = v.reshape(b, nblk, MOBA_BLOCK, MOBA_HEADS, HEAD_DIM)
    k_mean = jnp.mean(kb.astype(jnp.float32), axis=2)
    k_bh = kb.transpose(0, 3, 1, 2, 4)
    v_bh = vb.transpose(0, 3, 1, 2, 4)
    bi = jnp.arange(b)[:, None, None, None]
    hi = jnp.arange(MOBA_HEADS)[None, None, :, None]
    n_chunks = s_pad // MOBA_Q_CHUNK

    def chunk_fn(c):
        q0 = c * MOBA_Q_CHUNK
        blk = q0 // MOBA_BLOCK
        qpos = q0 + jnp.arange(MOBA_Q_CHUNK)
        qc = lax.dynamic_slice_in_dim(q, q0, MOBA_Q_CHUNK, axis=1)
        gate = jnp.einsum('bqhd,bnhd->bqhn', qc.astype(jnp.float32), k_mean)
        past = jnp.arange(nblk) < blk
        gate = jnp.where(past[None, None, None, :], gate, NEG_INF)
        _, idx = lax.top_k(gate, topk)
        slot_valid = jnp.arange(topk) < blk
        k_sel = k_bh[bi, hi, idx]
        v_sel = v_bh[bi, hi, idx]
        s_sel = jnp.einsum('bqhd,bqhjkd->bqhjk', qc, k_sel,
                           preferred_element_type=jnp.float32) * ATTN_SCALE
        s_sel = jnp.where(slot_valid[:, None], s_sel, NEG_INF)
        s_sel = s_sel.reshape(b, MOBA_Q_CHUNK, MOBA_HEADS, topk * MOBA_BLOCK)
        k_own = lax.dynamic_slice_in_dim(kb, blk, 1, axis=1)[:, 0]
        v_own = lax.dynamic_slice_in_dim(vb, blk, 1, axis=1)[:, 0]
        s_own = jnp.einsum('bqhd,bkhd->bqhk', qc, k_own,
                           preferred_element_type=jnp.float32) * ATTN_SCALE
        kpos = blk * MOBA_BLOCK + jnp.arange(MOBA_BLOCK)
        causal = kpos[None, :] <= qpos[:, None]
        s_own = jnp.where(causal[None, :, None, :], s_own, NEG_INF)
        p = jax.nn.softmax(jnp.concatenate([s_sel, s_own], axis=-1), axis=-1).astype(v.dtype)
        p_sel = p[..., :topk * MOBA_BLOCK].reshape(b, MOBA_Q_CHUNK, MOBA_HEADS, topk, MOBA_BLOCK)
        p_own = p[..., topk * MOBA_BLOCK:]
        o = (jnp.einsum('bqhjk,bqhjkd->bqhd', p_sel, v_sel)
             + jnp.einsum('bqhk,bkhd->bqhd', p_own, v_own))
        return o.astype(q.dtype)

    outs = lax.map(chunk_fn, jnp.arange(n_chunks))
    o = outs.transpose(1, 0, 2, 3, 4).reshape(b, s_pad, MOBA_WIDTH)
    return o[:, :s]

def _layer(x, norm_g, w_in, pool_w, pool_scale, sinks, w_proj_a, w_proj_b, w_proj_c, w_out):
    b, s, _ = x.shape
    h = _rmsnorm(x, norm_g)
    u = h @ w_in
    offsets = np.cumsum(IN_SIZES)[:-1].tolist()
    (a_x, a_z, b_q, b_k, b_v, b_z, c_q, c_k, c_v, c_z, gate_logits) = jnp.split(u, offsets, axis=-1)
    ya = _pool_mixer(a_x, pool_w, pool_scale) * jax.nn.silu(a_z)
    yb = _swa_attention(b_q.reshape(b, s, SWA_Q_HEADS, HEAD_DIM),
                        b_k.reshape(b, s, SWA_KV_HEADS, HEAD_DIM),
                        b_v.reshape(b, s, SWA_KV_HEADS, HEAD_DIM), sinks) * jax.nn.silu(b_z)
    yc = _moba_attention(c_q.reshape(b, s, MOBA_HEADS, HEAD_DIM),
                         c_k.reshape(b, s, MOBA_HEADS, HEAD_DIM),
                         c_v.reshape(b, s, MOBA_HEADS, HEAD_DIM)) * jax.nn.silu(c_z)
    ga, gb, gc = jnp.split(jax.nn.sigmoid(gate_logits), N_BRANCH, axis=-1)
    merged = ga * (ya @ w_proj_a) + gb * (yb @ w_proj_b) + gc * (yc @ w_proj_c)
    return x + merged @ w_out

def first_inputs(seed: int = 0) -> dict:
    key = jax.random.key(seed)
    ks = jax.random.split(key, 11)
    nrm = jax.random.normal
    x = nrm(ks[0], (BATCH, SEQ, D_MODEL), jnp.float32)
    norm_g = 1.0 + 0.05 * nrm(ks[1], (DEPTH, D_MODEL), jnp.float32)
    w_in = nrm(ks[2], (DEPTH, D_MODEL, IN_WIDTH), jnp.float32) * D_MODEL ** -0.5
    pool_w = nrm(ks[3], (DEPTH, POOL_GROUPS, POOL_GROUP_DIM, POOL_GROUP_DIM), jnp.float32) * POOL_GROUP_DIM ** -0.5
    pool_scale = 1.0 + 0.1 * nrm(ks[4], (DEPTH, POOL_WIDTH), jnp.float32)
    sink_logits = 0.5 * nrm(ks[5], (DEPTH, SWA_Q_HEADS), jnp.float32)
    w_proj_a = nrm(ks[6], (DEPTH, POOL_WIDTH, D_MODEL), jnp.float32) * POOL_WIDTH ** -0.5
    w_proj_b = nrm(ks[7], (DEPTH, SWA_WIDTH, D_MODEL), jnp.float32) * SWA_WIDTH ** -0.5
    w_proj_c = nrm(ks[8], (DEPTH, MOBA_WIDTH, D_MODEL), jnp.float32) * MOBA_WIDTH ** -0.5
    w_out = nrm(ks[9], (DEPTH, D_MODEL, D_MODEL), jnp.float32) * D_MODEL ** -0.5
    final_norm_g = 1.0 + 0.05 * nrm(ks[10], (D_MODEL,), jnp.float32)
    return {"x": x, "norm_g": norm_g, "w_in": w_in, "pool_w": pool_w, "pool_scale": pool_scale,
            "sink_logits": sink_logits, "w_proj_a": w_proj_a, "w_proj_b": w_proj_b,
            "w_proj_c": w_proj_c, "w_out": w_out, "final_norm_g": final_norm_g}

def first_block(x, norm_g, w_in, pool_w, pool_scale, sink_logits, w_proj_a, w_proj_b, w_proj_c,
              w_out, final_norm_g):
    for l in range(DEPTH):
        x = _layer(x, norm_g[l], w_in[l], pool_w[l], pool_scale[l], sink_logits[l],
                   w_proj_a[l], w_proj_b[l], w_proj_c[l], w_out[l])
    return _rmsnorm(x, final_norm_g)


N_FOX_HEADS = 8
N_SB_HEADS = 8
FOX_WIDTH = N_FOX_HEADS * HEAD_DIM
SB_WIDTH = N_SB_HEADS * HEAD_DIM
N_GROUPS = 4
EXPERTS_PER_GROUP = 4
N_EXPERTS = N_GROUPS * EXPERTS_PER_GROUP
TOP_K_EXPERTS = 2
D_FF_EXPERT = D_MODEL // 2
Q_BLOCK = 128
N_MOD = 6
IN_SPLITS = (
    FOX_WIDTH, 2 * FOX_WIDTH, 3 * FOX_WIDTH,
    3 * FOX_WIDTH + N_FOX_HEADS,
    3 * FOX_WIDTH + N_FOX_HEADS + SB_WIDTH,
    3 * FOX_WIDTH + N_FOX_HEADS + 2 * SB_WIDTH,
    3 * FOX_WIDTH + N_FOX_HEADS + 3 * SB_WIDTH,
    3 * FOX_WIDTH + N_FOX_HEADS + 3 * SB_WIDTH + D_MODEL,
)
N_IN = 3 * FOX_WIDTH + N_FOX_HEADS + 3 * SB_WIDTH + 2 * D_MODEL


def rmsnorm(x, g):
    xf = x.astype(jnp.float32)
    xf = xf * lax.rsqrt(jnp.mean(xf * xf, axis=-1, keepdims=True) + RMS_EPS)
    return xf.astype(x.dtype) * g

def to_heads(t, n_heads):
    b, s, _ = t.shape
    return t.reshape(b, s, n_heads, HEAD_DIM).transpose(0, 2, 1, 3)

def from_heads(t):
    b, h, s, d = t.shape
    return t.transpose(0, 2, 1, 3).reshape(b, s, h * d)

def sweep_query_blocks(block_fn, seq):
    n_blocks = seq // Q_BLOCK
    out = lax.map(block_fn, jnp.arange(n_blocks))
    nb, b, h, qb, d = out.shape
    return out.transpose(1, 2, 0, 3, 4).reshape(b, h, nb * qb, d)

def forgetting_attention(q, k, v, log_f):
    seq = q.shape[2]
    scale = HEAD_DIM ** -0.5
    F = jnp.cumsum(log_f, axis=-1)
    kpos = jnp.arange(seq)

    def block(i):
        start = i * Q_BLOCK
        qs = lax.dynamic_slice_in_dim(q, start, Q_BLOCK, axis=2)
        Fq = lax.dynamic_slice_in_dim(F, start, Q_BLOCK, axis=2)
        logits = jnp.einsum("bhqd,bhkd->bhqk", qs, k).astype(jnp.float32) * scale
        logits = logits + Fq[..., :, None] - F[..., None, :]
        qpos = start + jnp.arange(Q_BLOCK)
        mask = kpos[None, :] <= qpos[:, None]
        logits = jnp.where(mask, logits, -jnp.inf)
        p = jax.nn.softmax(logits, axis=-1)
        return jnp.einsum("bhqk,bhkd->bhqd", p.astype(v.dtype), v)

    return sweep_query_blocks(block, seq)

def stick_breaking_attention(q, k, v):
    seq = q.shape[2]
    scale = HEAD_DIM ** -0.5
    kpos = jnp.arange(seq)

    def block(i):
        start = i * Q_BLOCK
        qs = lax.dynamic_slice_in_dim(q, start, Q_BLOCK, axis=2)
        z = jnp.einsum("bhqd,bhkd->bhqk", qs, k).astype(jnp.float32) * scale
        qpos = start + jnp.arange(Q_BLOCK)
        mask = kpos[None, :] < qpos[:, None]
        log_beta = jax.nn.log_sigmoid(z)
        log_one_minus = jnp.where(mask, jax.nn.log_sigmoid(-z), 0.0)
        suffix = lax.cumsum(log_one_minus, axis=3, reverse=True) - log_one_minus
        A = jnp.where(mask, jnp.exp(log_beta + suffix), 0.0)
        return jnp.einsum("bhqk,bhkd->bhqd", A.astype(v.dtype), v)

    return sweep_query_blocks(block, seq)

def hierarchical_moe(h, rg_w, rg_b, re_w, re_b, w_gate, w_up, w_down):
    b, s, d = h.shape
    hf = h.reshape(b * s, d)
    g_prob = jax.nn.softmax((hf @ rg_w + rg_b).astype(jnp.float32), axis=-1)
    g_top_p, g_idx = lax.top_k(g_prob, 1)
    e_logits = (hf @ re_w + re_b).astype(jnp.float32).reshape(b * s, N_GROUPS, EXPERTS_PER_GROUP)
    e_sel = jnp.take_along_axis(e_logits, g_idx[:, :, None], axis=1)[:, 0, :]
    e_prob = jax.nn.softmax(e_sel, axis=-1)
    e_top_p, e_idx = lax.top_k(e_prob, TOP_K_EXPERTS)
    e_top_p = e_top_p / jnp.sum(e_top_p, axis=-1, keepdims=True)
    within = jnp.sum(jax.nn.one_hot(e_idx, EXPERTS_PER_GROUP, dtype=jnp.float32)
                     * e_top_p[..., None], axis=1)
    combine = (jax.nn.one_hot(g_idx[:, 0], N_GROUPS, dtype=jnp.float32)[:, :, None]
               * within[:, None, :] * g_top_p[:, :, None])
    combine = combine.reshape(b * s, N_EXPERTS).astype(h.dtype)
    out = jnp.zeros_like(hf)
    for e in range(N_EXPERTS):
        act = jax.nn.silu(hf @ w_gate[e]) * (hf @ w_up[e])
        out = out + combine[:, e:e + 1] * (act @ w_down[e])
    return out.reshape(b, s, d)

def second_inputs(seed: int = 0) -> dict:
    key = jax.random.key(seed)
    ks = jax.random.split(key, 20)
    D, L = D_MODEL, DEPTH

    def nrm(k, shape, scale):
        return jax.random.normal(k, shape, jnp.float32) * scale

    return {
        "x": nrm(ks[0], (BATCH, SEQ, D), 1.0),
        "c": nrm(ks[1], (BATCH, D), 1.0),
        "ada_w": nrm(ks[2], (L, D, N_MOD * D), 0.5 * D ** -0.5),
        "ada_b": nrm(ks[3], (L, N_MOD * D), 0.02),
        "norm1_g": 1.0 + nrm(ks[4], (L, D), 0.02),
        "w_in": nrm(ks[5], (L, D, N_IN), D ** -0.5),
        "b_forget": 2.0 + nrm(ks[6], (L, N_FOX_HEADS), 0.1),
        "w_branch_fox": nrm(ks[7], (L, FOX_WIDTH, D), FOX_WIDTH ** -0.5),
        "w_branch_sb": nrm(ks[8], (L, SB_WIDTH, D), SB_WIDTH ** -0.5),
        "w_out": nrm(ks[9], (L, D, D), D ** -0.5),
        "norm2_g": 1.0 + nrm(ks[10], (L, D), 0.02),
        "router_group_w": nrm(ks[11], (L, D, N_GROUPS), D ** -0.5),
        "router_group_b": nrm(ks[12], (L, N_GROUPS), 0.01),
        "router_expert_w": nrm(ks[13], (L, D, N_EXPERTS), D ** -0.5),
        "router_expert_b": nrm(ks[14], (L, N_EXPERTS), 0.01),
        "expert_w_gate": nrm(ks[15], (L, N_EXPERTS, D, D_FF_EXPERT), D ** -0.5),
        "expert_w_up": nrm(ks[16], (L, N_EXPERTS, D, D_FF_EXPERT), D ** -0.5),
        "expert_w_down": nrm(ks[17], (L, N_EXPERTS, D_FF_EXPERT, D), D_FF_EXPERT ** -0.5),
        "final_g": 1.0 + nrm(ks[18], (D,), 0.02),
    }

def second_block(x, c, ada_w, ada_b, norm1_g, w_in, b_forget, w_branch_fox, w_branch_sb, w_out,
              norm2_g, router_group_w, router_group_b, router_expert_w, router_expert_b,
              expert_w_gate, expert_w_up, expert_w_down, final_g):
    c_act = jax.nn.silu(c)
    for l in range(DEPTH):
        mod = c_act @ ada_w[l] + ada_b[l]
        shift1, scale1, gate1, shift2, scale2, gate2 = [m[:, None, :] for m in jnp.split(mod, N_MOD, axis=-1)]

        h = rmsnorm(x, norm1_g[l]) * (1.0 + scale1) + shift1
        proj = h @ w_in[l]
        qa, ka, va, fa, qb, kb, vb, ga, gb = jnp.split(proj, IN_SPLITS, axis=-1)
        log_f = jax.nn.log_sigmoid((fa + b_forget[l]).astype(jnp.float32)).transpose(0, 2, 1)
        o_fox = forgetting_attention(to_heads(qa, N_FOX_HEADS), to_heads(ka, N_FOX_HEADS),
                                     to_heads(va, N_FOX_HEADS), log_f)
        o_sb = stick_breaking_attention(to_heads(qb, N_SB_HEADS), to_heads(kb, N_SB_HEADS),
                                        to_heads(vb, N_SB_HEADS))
        merged = (jax.nn.sigmoid(ga) * (from_heads(o_fox) @ w_branch_fox[l])
                  + jax.nn.sigmoid(gb) * (from_heads(o_sb) @ w_branch_sb[l]))
        x = x + gate1 * (merged @ w_out[l])

        h2 = rmsnorm(x, norm2_g[l]) * (1.0 + scale2) + shift2
        y = hierarchical_moe(h2, router_group_w[l], router_group_b[l], router_expert_w[l],
                             router_expert_b[l], expert_w_gate[l], expert_w_up[l], expert_w_down[l])
        x = x + gate2 * y
    return rmsnorm(x, final_g)


def setup_inputs(seed=0):
    out = dict(first_inputs(seed))
    for name, value in second_inputs(seed + 1).items():
        if name != "x":
            out[name + "_2"] = value
    return out


def reference(
    x, norm_g, w_in, pool_w, pool_scale, sink_logits, w_proj_a, w_proj_b, w_proj_c, w_out,
    final_norm_g, c_2, ada_w_2, ada_b_2, norm1_g_2, w_in_2, b_forget_2, w_branch_fox_2,
    w_branch_sb_2, w_out_2, norm2_g_2, router_group_w_2, router_group_b_2, router_expert_w_2,
    router_expert_b_2, expert_w_gate_2, expert_w_up_2, expert_w_down_2, final_g_2,
):
    x = first_block(
        x, norm_g, w_in, pool_w, pool_scale, sink_logits, w_proj_a, w_proj_b, w_proj_c, w_out,
        final_norm_g,
    )
    return second_block(
        x, c_2, ada_w_2, ada_b_2, norm1_g_2, w_in_2, b_forget_2, w_branch_fox_2, w_branch_sb_2,
        w_out_2, norm2_g_2, router_group_w_2, router_group_b_2, router_expert_w_2,
        router_expert_b_2, expert_w_gate_2, expert_w_up_2, expert_w_down_2, final_g_2,
    )


_drawn_inputs = setup_inputs


def setup_inputs(seed=0):
    import zlib

    import numpy as np

    out = dict(_drawn_inputs(seed))
    spreads = {}
    factors = {'sink_logits': 8.0,
     'ada_b_2': 3.33,
     'norm1_g_2': 8.0,
     'b_forget_2': 8.0,
     'norm2_g_2': 5.529,
     'router_group_b_2': 8.0,
     'router_expert_b_2': 8.0,
     'final_g_2': 2.802}
    for name, (base, spread) in spreads.items():
        noise = np.random.default_rng([zlib.crc32(name.encode()), seed]).standard_normal(out[name].shape)
        drawn = base * np.exp(spread * noise) if base else spread * noise
        out[name] = jnp.asarray(drawn.astype(out[name].dtype))
    for name, factor in factors.items():
        out[name] = (out[name] * factor).astype(out[name].dtype)
    return out
```

```python
from contextlib import ExitStack

import numpy as np
import concourse.bass as bass
from concourse import mybir

F32 = mybir.dt.float32
I32 = mybir.dt.int32
ALU = mybir.AluOpType
ACT = mybir.ActivationFunctionType
X = mybir.AxisListType.X

LN_EXP, LN, SILU_SET = "natural_log_exp_and_others", "natural_log", "silu_and_others"
P = 128
T = 256
TT = T // P
D = 1024
KD = D // P
HD = 64
W512 = 512
EPS = 1e-6
NEG = -1e30
N_MOD = 6
N_EXPERTS = 16
EXPERTS_PER_GROUP = 4
N_GROUPS = 4
FF = 512
SLOTS = 64
PAIRS = N_EXPERTS // 2
WINDOWS = (2, 4, 8, 16)
CHUNK = KD * W512
RING = 6

IN1 = dict(ax=0, az=512, bq=1024, bkv=1536, bz=1792, cq=2304, ck=2816, cv=3328, cz=3840, gate=4352)
IN2 = dict(qa=0, ka=512, va=1024, fa=1536, qb=1544, kb=2056, vb=2568, gate=3080)

VEC = {}
_at = 0
for _name, _n in (("eps", 1), ("norm_g", 8), ("norm1_g", 8), ("norm2_g", 8), ("c", 8), ("pool_scale", 4),
                  ("ada_b", 48), ("b_forget", 1), ("sink", 8), ("router_b", 20)):
    VEC[_name] = slice(_at, _at + _n)
    _at += _n
N_VEC = _at

CON = {}
_at = 0
for _name, _n in (("ident", 128), ("mask_causal", 384), ("mask_swa", 384), ("mask_strict", 384),
                  ("suffix", 128), ("before", 128), ("ones", 128), ("iota", 64), ("inv_count", 64),
                  ("tie", 16)):
    CON[_name] = slice(_at, _at + _n)
    _at += _n
N_CON = _at


def constants():
    c = np.zeros((P, N_CON), np.float32)
    i, j = np.arange(P)[:, None], np.arange(P)[None, :]
    causal = np.where(j <= i, 0.0, NEG)
    c[:, CON["ident"]] = i == j
    c[:, CON["mask_causal"]] = np.concatenate([causal, np.zeros((P, P)), causal], 1)
    c[:, CON["mask_swa"]] = np.concatenate([causal, np.where(j > i, 0.0, NEG), causal], 1)
    strict = np.where(i < j, 0.0, NEG)
    c[:, CON["mask_strict"]] = np.concatenate([strict, np.zeros((P, P)), strict], 1)
    c[:, CON["suffix"]] = i >= j
    c[:, CON["before"]] = i < j
    c[:, CON["ones"]] = 1.0
    c[:, CON["iota"]] = np.arange(SLOTS)
    c[:, CON["inv_count"]] = np.concatenate([1.0 / np.minimum(np.arange(16) + 1, w) for w in WINDOWS])
    c[:, CON["tie"]] = (np.arange(4)[None, :] < np.arange(4)[:, None]).reshape(-1)
    return c


def plan():
    steps = []
    unit = lambda *u: steps.append(("unit",) + u)

    def heads(todo, n=1):
        for _ in range(n):
            h = todo.pop(0)
            for kind, g in (("S", h), ("T", h - 1), ("V", h - 2)):
                if first <= g < last:
                    steps.append((kind, g))

    ada = [c for c in range(2 * N_MOD) for _ in range(2)]
    ada_due = []

    def some_ada(n=2):
        for _ in range(n):
            if ada_due and ada[:1] != ada_due[:1]:
                unit("mod", ada_due.pop(0))
            if ada:
                half = len(ada) % 2
                steps.append(("ada", ada[0], half))
                if half:
                    ada_due.append(ada[0])
                ada.pop(0)

    steps.append(("norm", 0, 0))
    unit("hT", 0, 0, 0)
    unit("hT", 0, 0, 1)
    steps.append(("norm", 0, 1))
    unit("tm", "cv", 0)
    unit("hT", 0, 1, 0)
    unit("hT", 0, 1, 1)
    unit("tm", "cv", 1)
    for name in ("cz", "bz", "az", "ax", "cq", "ck"):
        unit("fm", name, 0)
        unit("fm", name, 1)
        some_ada()
        if name == "ax":
            steps.append(("pool",))
    first, last = 0, 16
    todo = list(range(0, 18))
    seq = [("fm", "bq", 0), ("fm", "bq", 1), ("bkv",), ("mix", 0), ("mix", 1)]
    seq += [("fm", f"g{i}", j) for i in (4, 5, 2, 3, 0, 1) for j in range(2)]
    for n, u in enumerate(seq):
        unit(*u)
        if todo:
            heads(todo)
        some_ada(n % 2)
    while todo:
        heads(todo)
    steps += [("sigmoid", 16), ("sigmoid", 8), ("sigmoid", 0)]
    for br in "cba":
        for j in range(4):
            unit("proj", br, j)
            if j % 2:
                some_ada()
    while ada or ada_due:
        some_ada()
    steps.append(("mods", 0))
    unit("wout", 1, 0, 0)
    unit("wout", 1, 0, 1)
    steps += [("norm", 1, 0), ("norm", 2, 0)]
    unit("wout", 1, 1, 0)
    unit("hT", 1, 0, 0)
    unit("hT", 1, 0, 1)
    unit("wout", 1, 1, 1)
    steps += [("norm", 1, 1), ("norm", 2, 1)]
    unit("tm", "va", 0)
    unit("tm", "vb", 0)
    unit("hT", 1, 1, 0)
    unit("hT", 1, 1, 1)
    unit("tm", "va", 1)
    unit("tm", "vb", 1)
    for name in ("qa", "ka"):
        unit("fm", name, 0)
        unit("fm", name, 1)
    unit("fa",)
    steps.append(("logf",))
    unit("fm", "qb", 0)
    unit("FT",)
    first, last = 16, 32
    todo = list(range(16, 34))
    seq = [(("fm", "qb", 1), 1), (("fm", "kb", 0), 1), (("fm", "kb", 1), 1), (("fm", "h0", 0), 1),
           (("fm", "h0", 1), 1), (("fm", "h1", 0), 1), (("fm", "h1", 1), 2), (("fm", "h2", 0), 1),
           (("fm", "h2", 1), 2), (("fm", "h3", 0), 1), (("fm", "h3", 1), 2), (("proj", "f", 0), 1),
           (("proj", "f", 1), 1), (("proj", "f", 2), 1), (("proj", "f", 3), 1)]
    for u, n in seq:
        unit(*u)
        heads(todo, n)
        if u == ("fm", "h1", 1):
            steps.append(("sigmoid", 0))
    assert not todo
    steps.append(("sigmoid", 8))
    for j in range(4):
        unit("proj", "s", j)
    steps.append(("mods", 1))
    unit("wout", 2, 0, 0)
    unit("wout", 2, 0, 1)
    steps.append(("norm", 3, 0))
    unit("wout", 2, 1, 0)
    unit("hT", 2, 0, 0)
    unit("hT", 2, 0, 1)
    unit("wout", 2, 1, 1)
    steps.append(("norm", 3, 1))
    unit("logit", 0)
    unit("hT", 2, 1, 0)
    unit("hT", 2, 1, 1)
    unit("logit", 1)
    steps.append(("route",))
    unit("rank",)
    steps.append(("slots",))

    chunks = []
    for s in steps:
        for name in chunk_of(s):
            if name not in chunks:
                chunks.append(name)
    return steps, chunks


def chunk_of(step):
    if step[0] == "ada":
        return [("ada", step[1])]
    if step[0] == "unit" and step[1] in ("fm", "tm"):
        return [(step[2],)]
    if step[0] == "unit" and step[1] == "bkv":
        return [("bkv",)]
    if step[0] == "unit" and step[1] == "proj":
        return [("proj", step[2])]
    if step[0] == "unit" and step[1] == "wout":
        return [("wout", step[2], step[4])]
    return []


STEPS, CHUNKS = plan()
UNITS = [s[1:] for s in STEPS if s[0] == "unit"]
SILU = ("cz", "bz", "az")


def evictor(u):
    if u[0] in ("tm", "bkv", "fa", "FT") or (u[0] == "fm" and u[1] not in SILU):
        return "act"
    return "dve"


def evict_count(u):
    n = UNITS.index(u)
    return sum(evictor(v) == evictor(u) for v in UNITS[:n + 1])


def last_reader(chunk):
    if chunk[0] == "ada":
        order = [s[1] for s in STEPS if s[0] == "ada" and s[2]]
        return "dve", order.index(chunk[1]) + 1
    n = [i for i, u in enumerate(UNITS) if chunk in chunk_of(("unit",) + u)][-1]
    return "pe", n + 1


SILU_UNITS = [u for u in UNITS if u[0] == "fm" and u[1] in SILU]
SIGMOIDS = [s for s in STEPS if s[0] == "sigmoid"]
NORMS = [s[1:] for s in STEPS if s[0] == "norm"] + [(4, 0), (4, 1)]
XN_NORMS = [s for s in NORMS if s[0] in (0, 2, 3)]


def two_block_kernel(nc, a, out):
    x_in, w_in1, w_in2 = a["x"][0], a["w_in"][0], a["w_in_2"][0]

    def k_rows(w, cols):
        return w[:, cols].rearrange("(k p) n -> p k n", p=P)

    def chunk_source(c):
        if c[0] == "ada":
            return k_rows(a["ada_w_2"][0], slice(c[1] * W512, (c[1] + 1) * W512))
        if c[0] == "proj":
            w = dict(a="w_proj_a", b="w_proj_b", c="w_proj_c", f="w_branch_fox_2", s="w_branch_sb_2")[c[1]]
            return k_rows(a[w][0], slice(0, D))
        if c[0] == "wout":
            return k_rows(a[("w_out", "w_out_2")[c[1] - 1]][0], slice(c[2] * W512, (c[2] + 1) * W512))
        if c[0] == "bkv":
            return k_rows(w_in1, slice(IN1["bkv"], IN1["bkv"] + 256))
        if c[0] in IN1:
            at, w = IN1[c[0]], w_in1
        elif c[0] in IN2:
            at, w = IN2[c[0]], w_in2
        elif c[0][0] == "g":
            at, w = IN1["gate"] + W512 * int(c[0][1]), w_in1
        else:
            at, w = IN2["gate"] + W512 * int(c[0][1]), w_in2
        return k_rows(w, slice(at, at + W512))

    with ExitStack() as ctx:
        def sb(name, shape, dt=F32):
            return ctx.enter_context(nc.sbuf_tensor(name, shape, dt))

        def sem(name):
            return ctx.enter_context(nc.semaphore(name))

        ring = sb("ring", [P, RING, CHUNK])
        con = sb("con", [P, N_CON])
        vec = sb("vec", [P, N_VEC])
        gate_rows = sb("gate_rows", [P, 2, D])
        fin_g = sb("fin_g", [P, D])
        x_res = sb("x_res", [P, TT, D])
        hT = sb("hT", [P, KD, T])
        work = sb("work", [P, 7680])
        mixed = sb("mixed", [P, 3, 4, T])
        gates = sb("gates", [P, 24, T])
        sig = sb("sig", [P, 2, W512])
        ada_acc = sb("ada_acc", [P, W512])
        score = sb("score", [P, 2, 384])
        probT = sb("probT", [P, 2, 384])
        stat = sb("stat", [P, 10, 8])
        hstat = sb("hstat", [P, 2, 12])
        mod = sb("mod", [P, 2 * N_MOD, 4])
        aff = sb("aff", [P, 2, KD])
        c_act = sb("c_act", [P, KD])
        c_tmp = sb("c_tmp", [P, 2, KD])
        pw = sb("pw", [P, 4, P])
        fa_w = sb("fa_w", [P, KD, 8])
        rt_w = sb("rt_w", [P, KD, 20])
        fox = sb("fox", [8, 5, T])
        fox_neg_ident = sb("fox_neg_ident", [8, 8])
        fox_ones = sb("fox_ones", [8, T])
        foxT = sb("foxT", [P, TT, 8])
        n_rounds = sb("n_rounds", [P, 1], I32)

        xn = gates[:, 8:16, :].rearrange("p k t -> p (k t)").rearrange("p (t d) -> p t d", t=TT)
        junk = gates[:, 16:20, :].rearrange("p k t -> p (k t)")
        pool_x, pool_a, pool_b = (gates[:, n:n + 4, :] for n in (12, 16, 20))
        fm4 = lambda at: work[:, at:at + 1024].rearrange("p (n t) -> p n t", n=4)
        tm2 = lambda at: work[:, at:at + 1024].rearrange("p (t n) -> p t n", t=TT)
        qm, km, vm, qs, kb2, vb2 = fm4(0), fm4(1024), tm2(2048), fm4(3072), fm4(4608), tm2(5632)
        kvs = work[:, 4096:4608]
        soft = mixed[:, 2, 0:3, :].rearrange("p k t -> p (k t)").rearrange("p (b n) -> p b n", b=2)
        xg = work[:, 0:1024].rearrange("p (k s) -> p k s", k=KD)
        onehot = work[:, 1024:1280].rearrange("p (t e s) -> p t e s", t=TT, e=2)
        combine = work[:, 1280:1536].rearrange("p (t e s) -> p t e s", t=TT, e=2)
        act = work[:, 1536:2048]
        sil = work[:, 2048:3072].rearrange("p (e f) -> p e f", e=2)
        actT = work[:, 3072:3584].rearrange("p (k s) -> p k s", k=4)
        y_pair = work[:, 3584:4608]
        combT = work[:, 4608:4864]
        rt = work[:, 4864:5964]

        psum = ctx.enter_context(nc.psum_tensor("psum", [P, 8, W512], F32))
        bank = [psum[:, i, :] for i in range(8)]
        unit_bank, o_bank, score_bank, trans_bank = bank[0:3], bank[3], bank[4:6], bank[6:8]
        out_bank = bank[0:4]
        gu_bank, x_bank = bank[4:6], bank[6:8]

        cs = lambda name: con[:, CON[name]]
        ident, ones = cs("ident"), cs("ones")

        x_loaded = [sem(f"x_loaded{t}") for t in range(TT)]
        ident_loaded = sem("ident_loaded")
        con_loaded = sem("con_loaded")
        gate_rows_loaded = sem("gate_rows_loaded")
        vec_loaded = sem("vec_loaded")
        small_loaded = sem("small_loaded")
        fin1_loaded = sem("fin1_loaded")
        fin2_loaded = sem("fin2_loaded")
        chunk_loaded = [sem(f"chunk_loaded{s}") for s in range(RING)]
        unit_done = sem("unit_done")
        act_evicted = sem("act_evicted")
        dve_evicted = sem("dve_evicted")
        sig_ready = sem("sig_ready")
        ada_done = sem("ada_done")
        c_exp = sem("c_exp")
        sumsq_ready = sem("sumsq_ready")
        ms_ready = sem("ms_ready")
        guess_ready = sem("guess_ready")
        gates_ready = sem("gates_ready")
        x1_ready = sem("x1_ready")
        xn_ready = sem("xn_ready")
        pooled_ready = sem("pooled_ready")
        scores_done = sem("scores_done")
        scores_masked = sem("scores_masked")
        max_ready = sem("max_ready")
        exp_done = sem("exp_done")
        probs_ready = sem("probs_ready")
        pt_done = sem("pt_done")
        stick_ready = sem("stick_ready")
        pt_evicted = sem("pt_evicted")
        o_done = sem("o_done")
        o_evicted = sem("o_evicted")
        fox_abs = sem("fox_abs")
        fox_log = sem("fox_log")
        fox_ready = sem("fox_ready")
        mods_ready = sem("mods_ready")
        group_shifted = sem("group_shifted")
        group_exp = sem("group_exp")
        sel_ready = sem("sel_ready")
        rounds_ready = sem("rounds_ready")
        dve_chain = sem("dve_chain")
        act_chain = sem("act_chain")
        onehot_ready = sem("onehot_ready")
        gather_done = sem("gather_done")
        xg_act = sem("xg_act")
        xg_dve = sem("xg_dve")
        gu_done = sem("gu_done")
        silu_done = sem("silu_done")
        act_ready = sem("act_ready")
        combine_ready = sem("combine_ready")
        actT_done = sem("actT_done")
        combT_done = sem("combT_done")
        actT_evicted = sem("actT_evicted")
        combT_evicted = sem("combT_evicted")
        down_done = sem("down_done")
        y_ready = sem("y_ready")
        scatter_done = sem("scatter_done")
        tile_done = sem("tile_done")
        out_ready = sem("out_ready")
        stored = sem("stored")

        block = ctx.enter_context(nc.Block())

        def evicted(u):
            return (act_evicted if evictor(u) == "act" else dve_evicted), evict_count(u)

        def sigmoids(first_tile, block):
            return [n for n, g in enumerate(SIGMOIDS) if g[1] == first_tile][block - 1 if first_tile < 16 else 0] + 1

        def wait_chunk(eng, c):
            n = CHUNKS.index(c)
            eng.wait_ge(chunk_loaded[n % RING], 16 * (n // RING + 1))
            return ring[:, n % RING, :]

        def dense_uses(s):
            return len(range(s, len(CHUNKS), RING))

        first_expert_slot = len(CHUNKS) % RING
        slot_of = lambda j: (first_expert_slot + j) % RING
        PAIR_LOADS = (("expert_w_gate_2", 0), ("expert_w_up_2", 0), ("expert_w_gate_2", 1),
                      ("expert_w_up_2", 1), ("expert_w_down_2", 0), ("expert_w_down_2", 1))

        def pair_chunk(j):
            c = ring[:, slot_of(j), :]
            return c.rearrange("p (k n) -> p k n", n=W512 if j < 4 else D)

        def pair_loaded(eng, j, it):
            eng.wait_ge(chunk_loaded[slot_of(j)], it * 16 + 16 * (dense_uses(slot_of(j)) + 1))

        @block.sync
        def _(sp):
            def wait_slot_free(n):
                if n >= RING:
                    who, count = last_reader(CHUNKS[n - RING])
                    sp.wait_ge(ada_done if who == "dve" else unit_done, count)

            for t in range(TT):
                sp.dma_start(x_res[:, t, :], x_in[t * P:(t + 1) * P, :]).then_inc(x_loaded[t], 16)
            for n, c in enumerate(CHUNKS):
                wait_slot_free(n)
                src = chunk_source(c)
                dst = ring[:, n % RING, 0:src.shape[1] * src.shape[2]]
                sp.dma_start(dst.rearrange("p (k n) -> p k n", n=src.shape[2]), src)\
                  .then_inc(chunk_loaded[n % RING], 16)

            def load_pair(it, pair, first):
                for j, (name, e) in enumerate(PAIR_LOADS):
                    if first:
                        wait_slot_free(len(CHUNKS) + j)
                    elif j < 4:
                        sp.wait_ge(gu_done, it * 2 - 1 + j // 2)
                    else:
                        sp.wait_ge(down_done, it * 2 - 1 + j - 4)
                    w = a[name][0][bass.ds(pair * 2 + e, 1)]
                    sp.dma_start(pair_chunk(j), w.rearrange("e (k p) n -> p (e k) n", p=P))\
                      .then_inc(chunk_loaded[slot_of(j)], 16)

            load_pair(0, 0, True)
            with sp.Fori(1, PAIRS) as pair:
                load_pair(pair, pair, False)
            sp.wait_ge(rounds_ready, 1)
            rounds = sp.value_load(n_rounds[0:1, 0:1], min_val=1, max_val=T // SLOTS)
            with sp.If(rounds > 1):
                with sp.Fori(1, rounds) as r:
                    with sp.Fori(0, PAIRS) as pair:
                        load_pair(r * PAIRS + pair, pair, False)
            for t in range(TT):
                sp.wait_ge(out_ready, t + 1)
                sp.dma_start(out[0][t * P:(t + 1) * P, :], x_res[:, t, :]).then_inc(stored, 16)
            sp.wait_ge(stored, 16 * TT)

        @block.tensor
        def _(pe):
            def unit(n, u):
                b = unit_bank[n % 3]
                if n >= 3:
                    pe.wait_ge(*evicted(UNITS[n - 3]))
                kind = u[0]
                if kind == "hT":
                    _, norm, t, half = u
                    pe.wait_ge(xn_ready, XN_NORMS.index(((0, 2, 3)[norm], t)) + 1)
                    if n == 0:
                        pe.wait_ge(ident_loaded, 16)
                    for k in range(4):
                        f = (4 * half + k) * P
                        last = nc.tensor.transpose(b[:, k * P:(k + 1) * P], xn[:, t, f:f + P], ident)
                elif kind in ("fm", "tm", "bkv", "fa"):
                    block2 = kind == "fa" or u[1:2] and (u[1] in IN2 or u[1][0] == "h")
                    pe.wait_ge(*evicted(("hT", 1 if block2 else 0, u[2] if kind == "tm" else 1, 1)))
                    if kind == "fa":
                        pe.wait_ge(small_loaded, 16 * 3)
                        for k in range(KD):
                            last = nc.tensor.matmul(b[0:8, 0:T], fa_w[:, k, :], hT[:, k, :],
                                                    start=k == 0, stop=k == KD - 1)
                    elif kind == "bkv":
                        w = wait_chunk(pe, ("bkv",))[:, 0:KD * 256].rearrange("p (k n) -> p k n", n=256)
                        for k in range(KD):
                            nc.tensor.matmul(b[:, 0:T], w[:, k, 0:P], hT[:, k, :], start=k == 0, stop=k == KD - 1)
                        for t in range(TT):
                            for k in range(KD):
                                last = nc.tensor.matmul(b[:, T + t * P:T + (t + 1) * P],
                                                        hT[:, k, t * P:(t + 1) * P], w[:, k, P:2 * P],
                                                        start=k == 0, stop=k == KD - 1)
                    elif kind == "tm":
                        w = wait_chunk(pe, (u[1],)).rearrange("p (k n) -> p k n", n=W512)
                        t = u[2]
                        for k in range(KD):
                            last = nc.tensor.matmul(b[:, :], hT[:, k, t * P:(t + 1) * P], w[:, k, :],
                                                    start=k == 0, stop=k == KD - 1)
                    else:
                        w = wait_chunk(pe, (u[1],)).rearrange("p (k n) -> p k n", n=W512)
                        for j in range(2):
                            n_tile = 2 * u[2] + j
                            for k in range(KD):
                                if u[1] == "bq":
                                    for g in range(2):
                                        f = (4 * g + n_tile) * HD
                                        last = nc.tensor.matmul(b[HD * g:HD * (g + 1), j * T:(j + 1) * T],
                                                                w[:, k, f:f + HD], hT[:, k, :], start=k == 0,
                                                                stop=k == KD - 1, skip_group_check=True)
                                else:
                                    last = nc.tensor.matmul(b[:, j * T:(j + 1) * T], w[:, k, n_tile * P:(n_tile + 1) * P],
                                                            hT[:, k, :], start=k == 0, stop=k == KD - 1)
                elif kind == "mix":
                    pe.wait_ge(pooled_ready, 1)
                    pe.wait_ge(small_loaded, 16 * 3)
                    for j in range(2):
                        g = 2 * u[1] + j
                        last = nc.tensor.matmul(b[:, j * T:(j + 1) * T], pw[:, g, :], pool_a[:, g, :],
                                                start=True, stop=True)
                elif kind == "mod":
                    c = u[1]
                    pe.wait_ge(con_loaded, 16)
                    pe.wait_ge(ada_done, c + 1)
                    if c // 2 in (2, 5):
                        last = nc.tensor.matmul(b[:, :], ones, ada_acc[:, :], start=True, stop=True)
                    else:
                        for j in range(4):
                            last = nc.tensor.matmul(b[:, j:j + 1], ada_acc[:, j * P:(j + 1) * P], ones[:, 0:1],
                                                    start=True, stop=True)
                elif kind == "proj":
                    _, br, j2 = u
                    w = wait_chunk(pe, ("proj", br)).rearrange("p (k n) -> p k n", n=D)
                    if br == "a":
                        pe.wait_ge(*evicted(("mix", 1)))
                    else:
                        pe.wait_ge(o_evicted, dict(c=4, b=8, f=12, s=16)[br])
                    y = mixed[:, dict(c=0, b=1, a=2, f=0, s=1)[br]]
                    for j in range(2):
                        f = (2 * j2 + j) * P
                        for k in range(4):
                            last = nc.tensor.matmul(b[:, j * T:(j + 1) * T], w[:, k, f:f + P], y[:, k, :],
                                                    start=k == 0, stop=k == 3)
                elif kind == "wout":
                    _, blk, t, half = u
                    w = wait_chunk(pe, ("wout", blk, half)).rearrange("p (k n) -> p k n", n=W512)
                    pe.wait_ge(*evicted(("proj", "a" if blk == 1 else "s", 3)))
                    for k in range(KD):
                        last = nc.tensor.matmul(b[:, :], gates[:, k, t * P:(t + 1) * P], w[:, k, :],
                                                start=k == 0, stop=k == KD - 1)
                elif kind == "FT":
                    pe.wait_ge(fox_ready, 1)
                    for t in range(TT):
                        last = nc.tensor.transpose(b[:, t * 8:(t + 1) * 8], fox[:, 4, t * P:(t + 1) * P],
                                                   ident[0:8, 0:8])
                elif kind == "logit":
                    t = u[1]
                    pe.wait_ge(*evicted(("hT", 2, t, 1)))
                    for k in range(KD):
                        last = nc.tensor.matmul(b[:, 0:20], hT[:, k, t * P:(t + 1) * P], rt_w[:, k, :],
                                                start=k == 0, stop=k == KD - 1)
                elif kind == "rank":
                    pe.wait_ge(sel_ready, 1)
                    before = cs("before")
                    sel = rt[:, 0:32]
                    nc.tensor.matmul(b[:, 0:16], before, sel[:, 0:16], start=True, stop=True)
                    nc.tensor.matmul(b[:, 16:32], ones, sel[:, 0:16], start=True, stop=False)
                    nc.tensor.matmul(b[:, 16:32], before, sel[:, 16:32], start=False, stop=True)
                    nc.tensor.matmul(b[:, 32:48], ones, sel[:, 0:16], start=True, stop=False)
                    last = nc.tensor.matmul(b[:, 32:48], ones, sel[:, 16:32], start=False, stop=True)
                last.then_inc(unit_done, 1)

            def operands(h):
                if h < 8:
                    lo = HD * (h % 2)
                    return qm[lo:lo + HD, h // 2], km[lo:lo + HD, h // 2], [vm[:, t, h * HD:(h + 1) * HD] for t in range(TT)]
                if h < 16:
                    g = (h - 8) // 4
                    lo = HD * g
                    return (qs[lo:lo + HD, (h - 8) % 4], kvs[lo:lo + HD, 0:T],
                            [kvs[:, T + t * P + g * HD:T + t * P + (g + 1) * HD] for t in range(TT)])
                i = h % 8
                lo = HD * (i % 2)
                q, k, v = (qm, km, vm) if h < 24 else (qs, kb2, vb2)
                return q[lo:lo + HD, i // 2], k[lo:lo + HD, i // 2], [v[:, t, i * HD:(i + 1) * HD] for t in range(TT)]

            def wait_operands(h):
                if h in (0, 8, 16, 24):
                    for u in ((("fm", "cq", 1), ("fm", "ck", 1)), (("fm", "bq", 1), ("bkv",)),
                              (("fm", "qa", 1), ("fm", "ka", 1), ("FT",)), (("fm", "qb", 1), ("fm", "kb", 1)))[h // 8]:
                        pe.wait_ge(*evicted(u))

            def scores(h):
                wait_operands(h)
                if h >= 2:
                    pe.wait_ge(scores_masked, h - 1)
                b = score_bank[h % 2]
                q, k, _ = operands(h)
                if h < 24:
                    fox_head = 16 <= h
                    for t, (lo, n) in enumerate(((0, P), (P, T))):
                        last = nc.tensor.matmul(b[:, lo:lo + n], q[:, t * P:(t + 1) * P], k[:, 0:n],
                                                start=True, stop=not fox_head)
                        if fox_head:
                            row = fox_neg_ident[:, h - 16:h - 15].to_broadcast([8, P])
                            last = nc.tensor.matmul(b[:, lo:lo + n], row, fox[:, 4, 0:n], start=False, stop=True)
                else:
                    nc.tensor.matmul(b[:, 0:T], k[:, 0:P], q[:, 0:T], start=True, stop=True)
                    last = nc.tensor.matmul(b[:, T:T + P], k[:, P:T], q[:, P:T], start=True, stop=True)
                last.then_inc(scores_done, 1)

            def turn(h):
                b = trans_bank[h % 2]
                if h >= 2:
                    pe.wait_ge(pt_evicted, h - 1)
                pe.wait_ge(probs_ready, h + 1)
                if h < 24:
                    for j in range(3):
                        last = nc.tensor.transpose(b[:, j * P:(j + 1) * P], score[:, h % 2, j * P:(j + 1) * P], ident)
                else:
                    nc.tensor.matmul(b[:, 0:384], cs("suffix"), soft[:, h % 2, :], start=True, stop=False,
                                     skip_group_check=True)
                    last = nc.tensor.matmul(b[:, P:T], ones, soft[:, h % 2, T:T + P], start=False, stop=True,
                                            skip_group_check=True)
                last.then_inc(pt_done, 1)

            def values(h):
                if h in (0, 8, 16, 24):
                    pe.wait_ge(*evicted((("tm", "cv", 1), ("bkv",), ("tm", "va", 1), ("tm", "vb", 1))[h // 8]))
                if h % 2 == 0 and h >= 2:
                    pe.wait_ge(o_evicted, h // 2)
                pe.wait_ge(pt_evicted, h + 1)
                _, _, v = operands(h)
                o = o_bank[HD * (h % 2):HD * (h % 2) + HD, :]
                nc.tensor.matmul(o[:, 0:T], v[0], probT[:, h % 2, 0:T], start=True, stop=False,
                                 skip_group_check=True)
                nc.tensor.matmul(o[:, P:T], v[1], probT[:, h % 2, T:T + P], start=False, stop=True,
                                 skip_group_check=True).then_inc(o_done, 1)

            def residual(n):
                t, half = n // 2, n % 2
                nc.tensor.matmul(out_bank[n], ident, x_res[:, t, half * W512:(half + 1) * W512], start=True, stop=True,
                                 skip_group_check=True)

            rank_bank = (len(UNITS) - 1) % 3
            n = 0
            for s in STEPS:
                if s == ("unit", "rank"):
                    pe.wait_ge(o_evicted, 16)
                    pe.wait_ge(act_evicted, evict_count([u for u in UNITS if evictor(u) == "act"][-1]))
                    pe.wait_ge(*evicted(("logit", 1)))
                    for i in range(4):
                        if i != rank_bank:
                            residual(i)
                if s[0] == "unit":
                    unit(n, s[1:])
                    n += 1
                elif s[0] == "S":
                    scores(s[1])
                elif s[0] == "T":
                    turn(s[1])
                elif s[0] == "V":
                    values(s[1])

            def scatter(t):
                for half in range(2):
                    last = nc.tensor.matmul(out_bank[2 * t + half], combT[:, t * P:(t + 1) * P],
                                            y_pair[:, half * W512:(half + 1) * W512], start=False, stop=True,
                                            skip_group_check=True)
                return last

            def gather(it):
                pe.wait_ge(onehot_ready, it + 1)
                for k in range(KD):
                    for t in range(TT):
                        last = nc.tensor.matmul(x_bank[k // 4][:, (k % 4) * P:(k % 4 + 1) * P],
                                                xn[:, t, k * P:(k + 1) * P],
                                                onehot[:, t].rearrange("p e s -> p (e s)"),
                                                start=t == 0, stop=t == TT - 1)
                last.then_inc(gather_done, 1)

            pe.wait_ge(*evicted(("rank",)))
            residual(rank_bank)
            gather(0)
            pe.wait_ge(rounds_ready, 1)
            rounds = pe.value_load(n_rounds[0:1, 0:1], min_val=1, max_val=T // SLOTS)
            with pe.Fori(0, rounds) as r:
                with pe.Fori(0, PAIRS) as pair:
                    it = r * PAIRS + pair

                    def gate_up(e):
                        pair_loaded(pe, 2 * e, it)
                        pair_loaded(pe, 2 * e + 1, it)
                        for k in range(KD):
                            for half in range(2):
                                last = nc.tensor.matmul(gu_bank[e][HD * half:HD * half + HD, :],
                                                        xg[:, k, e * SLOTS:(e + 1) * SLOTS],
                                                        pair_chunk(2 * e + half)[:, k, :],
                                                        start=k == 0, stop=k == KD - 1, skip_group_check=True)
                        last.then_inc(gu_done, 1)

                    pe.wait_ge(xg_act, it + 1)
                    pe.wait_ge(xg_dve, it + 1)
                    pe.wait_ge(y_ready, it * 2 + 1)
                    gate_up(0)
                    gather(it + 1)
                    pe.wait_ge(y_ready, it * 2 + 2)
                    gate_up(1)
                    pe.wait_ge(combT_evicted, it + 1)
                    scatter(0)
                    scatter(1).then_inc(scatter_done, 1)
                    pe.wait_ge(act_ready, it * 2 + 1)
                    pe.wait_ge(combine_ready, it + 1)
                    for t in range(TT):
                        last = nc.tensor.transpose(gu_bank[0][:, t * P:(t + 1) * P],
                                                   combine[:, t].rearrange("p e s -> p (e s)"), ident)
                    last.then_inc(combT_done, 1)
                    pe.wait_ge(act_ready, it * 2 + 2)
                    for k in range(4):
                        last = nc.tensor.transpose(gu_bank[1][:, k * P:(k + 1) * P], act[:, k * P:(k + 1) * P], ident)
                    last.then_inc(actT_done, 1)
                    pe.wait_ge(combT_evicted, it + 2)
                    pe.wait_ge(actT_evicted, it + 1)
                    for e in range(2):
                        pair_loaded(pe, 4 + e, it)
                        for k in range(4):
                            for half in range(2):
                                last = nc.tensor.matmul(gu_bank[e][HD * half:HD * half + HD, :],
                                                        actT[:, k, e * SLOTS:(e + 1) * SLOTS],
                                                        pair_chunk(4 + e)[:, k, half * W512:(half + 1) * W512],
                                                        start=k == 0, stop=k == 3, skip_group_check=True)
                        last.then_inc(down_done, 1)
            pe.wait_ge(y_ready, rounds * (2 * PAIRS) + 2)
            for t in range(TT):
                scatter(t).then_inc(tile_done, 1)

        @block.scalar
        def _(act_e):
            links = [0]

            def link(ins):
                links[0] += 1
                ins.then_inc(act_chain, 1)
                act_e.wait_ge(act_chain, links[0])

            def load_rest():
                act_e.dma_start(con[:, P:N_CON], a["con"][:, P:N_CON]).then_inc(con_loaded, 16)
                with nc.allow_non_contiguous_dma(reason="few bytes"):
                    act_e.dma_start(pw[:, :, :], a["pool_w"][0].rearrange("g c d -> c g d")).then_inc(small_loaded, 16)
                    act_e.dma_start(fa_w[:, :, :], k_rows(w_in2, slice(IN2["fa"], IN2["fa"] + 8))).then_inc(small_loaded, 16)
                    act_e.dma_start(rt_w[:, :, :], a["router_w"].rearrange("(k p) n -> p k n", p=P)).then_inc(small_loaded, 16)
                act_e.dma_start(gate_rows[:, :, :], a["gate_b"]).then_inc(gate_rows_loaded, 16)
                act_e.dma_start(fin_g[:, :], a["fin1"]).then_inc(fin1_loaded, 16)

            act_e.dma_start(vec[:, :], a["vec"]).then_inc(vec_loaded, 16)
            act_e.dma_start(con[:, 0:P], a["con"][:, 0:P]).then_inc(ident_loaded, 16)
            nc.scalar.preload_act_table_set(LN_EXP)
            act_e.wait_ge(vec_loaded, 16)
            nc.scalar.activation(c_tmp[:, 0, :], vec[:, VEC["c"]], ACT.Exp, scale=-1.0).then_inc(c_exp, 1)

            def norm(n, t):
                i = NORMS.index((n, t))
                if t == 0 and n in (1, 3, 4):
                    nc.scalar.preload_act_table_set(LN_EXP)
                if n == 0:
                    act_e.wait_ge(x_loaded[t], 16)
                elif n in (1, 3):
                    act_e.wait_ge(*evicted(("wout", 1 if n == 1 else 2, t, 1)))
                elif n == 2:
                    act_e.wait_ge(x1_ready, t + 1)
                else:
                    act_e.wait_ge(tile_done, t + 1)
                s = stat[:, i, :]
                x = x_res[:, t, :] if n < 4 else psum[:, 2 * t:2 * t + 2, :].rearrange("p h n -> p (h n)")
                nc.scalar.activation(junk, x, ACT.Square, accum_out=s[:, 0:1]).then_inc(sumsq_ready, 1)
                act_e.wait_ge(sumsq_ready, i + 1)
                link(nc.scalar.activation(s[:, 2:3], s[:, 0:1], ACT.Ln, scale=1.0 / D, bias=vec[:, VEC["eps"]]))
                nc.scalar.activation(s[:, 3:4], s[:, 2:3], ACT.Exp, scale=-0.5).then_inc(guess_ready, 1)

            def unit(n, u):
                b = unit_bank[n % 3]
                kind = u[0]
                if evictor(u) == "dve":
                    if kind == "fm":
                        i = SILU_UNITS.index(u)
                        if i >= 2:
                            act_e.wait_ge(*evicted(SILU_UNITS[i - 2]))
                        act_e.wait_ge(unit_done, n + 1)
                        nc.scalar.activation(sig[:, i % 2, :], b, ACT.Sigmoid).then_inc(sig_ready, 1)
                    return
                act_e.wait_ge(unit_done, n + 1)
                if kind == "fm":
                    if u[1][0] in "gh":
                        dst = gates[:, 4 * int(u[1][1]):4 * int(u[1][1]) + 4]
                    else:
                        dst = dict(cq=qm, ck=km, bq=qs, ax=pool_x, qa=qm, ka=km, qb=qs, kb=kb2)[u[1]]
                    scale = HD ** -0.5 if u[1] in ("cq", "bq", "qa", "qb") else 1.0
                    last = nc.scalar.activation(dst[:, 2 * u[2]:2 * u[2] + 2, :].rearrange("p n t -> p (n t)"), b,
                                                ACT.Copy, scale=scale)
                elif kind == "tm":
                    dst = dict(cv=vm, va=vm, vb=vb2)[u[1]]
                    last = nc.scalar.activation(dst[:, u[2], :], b[:, :], ACT.Copy)
                elif kind == "bkv":
                    last = nc.scalar.activation(kvs, b[:, :], ACT.Copy)
                elif kind == "fa":
                    last = nc.scalar.activation(fox[:, 0, :], b[0:8, 0:T], ACT.Identity,
                                                bias=vec[0:8, VEC["b_forget"]])
                elif kind == "FT":
                    last = nc.scalar.activation(foxT[:, :, :].rearrange("p t h -> p (t h)"), b[:, 0:16], ACT.Copy)
                last.then_inc(act_evicted, 1)

            def probs(h):
                s = score[:, h % 2, :]
                if h < 24:
                    st = hstat[:, h % 2, :]
                    act_e.wait_ge(max_ready, h + 1)
                    if 8 <= h < 16:
                        nc.scalar.activation(st[:, 4:6], st[:, 0:2], ACT.Exp, bias=vec[:, VEC["sink"]][:, h - 8:h - 7])
                    nc.scalar.activation(s[:, 0:P], s[:, 0:P], ACT.Exp, bias=st[:, 0:1], accum_out=st[:, 2:3])
                    nc.scalar.activation(s[:, P:384], s[:, P:384], ACT.Exp, bias=st[:, 1:2], accum_out=st[:, 3:4])\
                      .then_inc(exp_done, 1)
                else:
                    z = soft[:, h % 2, :]
                    act_e.wait_ge(scores_masked, h + 1)
                    if h >= 26:
                        act_e.wait_ge(pt_done, h - 1)
                    else:
                        act_e.wait_ge(unit_done, UNITS.index(("proj", "a", 3)) + 1)
                    link(nc.scalar.activation(z, s, ACT.Abs))
                    link(nc.scalar.activation(z, z, ACT.Exp, scale=-1.0))
                    nc.scalar.activation(z, z, ACT.Ln, bias=1.0).then_inc(exp_done, 1)

            def turned(h):
                act_e.wait_ge(pt_done, h + 1)
                if h >= 2:
                    act_e.wait_ge(o_done, h - 1)
                if h < 24:
                    nc.scalar.activation(probT[:, h % 2, :], trans_bank[h % 2][:, 0:384], ACT.Copy)\
                      .then_inc(pt_evicted, 1)
                else:
                    act_e.wait_ge(stick_ready, h - 23)
                    nc.scalar.activation(probT[:, h % 2, :], score[:, h % 2, :], ACT.Exp).then_inc(pt_evicted, 1)

            def sigmoid(first_tile):
                block = 2 if first_tile < 16 and gates_made[0] >= 3 else 1
                units = [u for u in UNITS if u[0] == "fm" and u[1] in [f"{'gh'[block - 1]}{first_tile // 4 + i}" for i in range(2)]]
                act_e.wait_ge(act_evicted, max(map(evict_count, units)))
                g = gates[:, first_tile:first_tile + 8, :].rearrange("p n t -> p (n t)")
                nc.scalar.activation(g, g, ACT.Sigmoid).then_inc(gates_ready, 1)
                gates_made[0] += 1

            gates_made = [0]

            def logf():
                act_e.wait_ge(act_evicted, evict_count(("fa",)))
                link(nc.scalar.activation(fox[:, 1, :], fox[:, 0, :], ACT.Abs))
                link(nc.scalar.activation(fox[:, 2, :], fox[:, 1, :], ACT.Exp, scale=-1.0))
                nc.scalar.preload_act_table_set(LN)
                nc.scalar.activation(fox[:, 1, :], fox[:, 2, :], ACT.Ln, bias=1.0).then_inc(fox_log, 1)

            n = 0
            for s in STEPS:
                if s[0] == "unit":
                    unit(n, s[1:])
                    n += 1
                elif s[0] == "norm":
                    norm(s[1], s[2])
                    if s[1:] == (0, 1):
                        load_rest()
                elif s[0] == "sigmoid":
                    sigmoid(s[1])
                elif s[0] == "S":
                    probs(s[1])
                elif s[0] == "T":
                    turned(s[1])
                elif s[0] == "logf":
                    logf()
                elif s[0] == "route":
                    act_e.wait_ge(group_shifted, 1)
                    nc.scalar.activation(rt[:, 100:108], rt[:, 100:108], ACT.Exp)
                    nc.scalar.activation(rt[:, 110:142], rt[:, 110:142], ACT.Exp).then_inc(group_exp, 1)
            act_e.wait_ge(x1_ready, TT)
            act_e.dma_start(fin_g[:, :], a["fin2"]).then_inc(fin2_loaded, 16)

            def xg_half(it):
                act_e.wait_ge(gather_done, it + 1)
                for k in range(4):
                    last = nc.scalar.activation(xg[:, k, :], x_bank[0][:, k * P:(k + 1) * P], ACT.Identity,
                                                scale=aff[:, 1, k:k + 1],
                                                bias=mod[:, 6:8, :].rearrange("p c j -> p (c j)")[:, k:k + 1])
                last.then_inc(xg_act, 1)

            xg_half(0)
            nc.scalar.preload_act_table_set(SILU_SET)
            act_e.wait_ge(rounds_ready, 1)
            rounds = act_e.value_load(n_rounds[0:1, 0:1], min_val=1, max_val=T // SLOTS)
            with act_e.Fori(0, rounds) as r:
                with act_e.Fori(0, PAIRS) as pair:
                    it = r * PAIRS + pair
                    for e in range(2):
                        act_e.wait_ge(gu_done, it * 2 + e + 1)
                        nc.scalar.activation(sil[HD:P, e, :], gu_bank[e][0:HD, :], ACT.Silu).then_inc(silu_done, 1)
                    act_e.wait_ge(actT_done, it + 1)
                    nc.scalar.activation(actT.rearrange("p k s -> p (k s)"), gu_bank[1], ACT.Copy)\
                      .then_inc(actT_evicted, 1)
                    xg_half(it + 1)
            for t in range(TT):
                norm(4, t)

        @block.vector
        def _(dve):
            v = nc.vector
            links = [0]

            def link(ins):
                links[0] += 1
                ins.then_inc(dve_chain, 1)
                dve.wait_ge(dve_chain, links[0])

            dve.wait_ge(c_exp, 1)
            link(v.tensor_scalar(c_tmp[:, 1, :], c_tmp[:, 0, :], 1.0, None, ALU.add))
            link(v.reciprocal(c_tmp[:, 0, :], c_tmp[:, 1, :]))
            link(v.tensor_tensor(c_act[:, :], c_tmp[:, 0, :], vec[:, VEC["c"]], ALU.mult))
            dve.wait_ge(ident_loaded, 16)
            v.tensor_scalar(fox_neg_ident[:, :], ident[0:8, 0:8], -1.0, None, ALU.mult)
            link(v.memset(fox_ones[:, :], 1.0))
            norms_on_xn = [0]

            def norm(n, t):
                i = NORMS.index((n, t))
                s = stat[:, i, :]
                dve.wait_ge(sumsq_ready, i + 1)
                v.tensor_scalar(s[:, 1:2], s[:, 0:1], 1.0 / D, EPS, ALU.mult, ALU.add).then_inc(ms_ready, 1)
                dve.wait_ge(guess_ready, i + 1)
                y = s[:, 3:4]
                dve.wait_ge(ms_ready, i + 1)
                link(v.tensor_scalar(s[:, 4:5], y, y, s[:, 1:2], ALU.mult, ALU.mult))
                link(v.tensor_scalar(s[:, 5:6], s[:, 4:5], -0.5, 1.5, ALU.mult, ALU.add))
                link(v.tensor_tensor(s[:, 7:8], y, s[:, 5:6], ALU.mult))
                rstd = s[:, 7:8]
                if n in (1, 4):
                    dve.wait_ge(fin1_loaded if n == 1 else fin2_loaded, 16)
                    x = x_res[:, t, :] if n == 1 else psum[:, 2 * t:2 * t + 2, :].rearrange("p h n -> p (h n)")
                    v.scalar_tensor_tensor(x_res[:, t, :], x, rstd, fin_g[:, :], ALU.mult, ALU.mult)\
                     .then_inc(x1_ready if n == 1 else out_ready, 1)
                else:
                    if n == 2:
                        dve.wait_ge(x1_ready, t + 1)
                    v.tensor_scalar(xn[:, t, :], x_res[:, t, :], rstd, None, ALU.mult).then_inc(xn_ready, 1)

            def unit(n, u):
                if evictor(u) != "dve":
                    return
                b = unit_bank[n % 3]
                kind = u[0]
                flat = lambda ap: ap.rearrange("p n t -> p (n t)")
                if kind == "fm":
                    i = SILU_UNITS.index(u)
                    dve.wait_ge(sig_ready, i + 1)
                    z = mixed[:, "cba".index(u[1][0]), 2 * u[2]:2 * u[2] + 2, :]
                    v.tensor_tensor(flat(z), b, sig[:, i % 2, :], ALU.mult).then_inc(dve_evicted, 1)
                    return
                dve.wait_ge(unit_done, n + 1)
                if kind == "hT":
                    _, norm_i, t, half = u
                    if norm_i == 1 and (t, half) == (0, 0):
                        dve.wait_ge(mods_ready, 1)
                    if norm_i == 2 and (t, half) == (0, 0):
                        dve.wait_ge(mods_ready, 2)
                    for k in range(4):
                        f = 4 * half + k
                        dst, src = hT[:, f, t * P:(t + 1) * P], b[:, k * P:(k + 1) * P]
                        if norm_i == 0:
                            last = v.tensor_scalar(dst, src, vec[:, VEC["norm_g"]][:, f:f + 1], None, ALU.mult)
                        else:
                            shift = mod[:, (0 if norm_i == 1 else 6) + f // 4, f % 4:f % 4 + 1]
                            last = v.tensor_scalar(dst, src, aff[:, norm_i - 1, f:f + 1], shift, ALU.mult, ALU.add)
                elif kind == "mix":
                    dve.wait_ge(*evicted(("fm", "az", 1)))
                    for j in range(2):
                        g = 2 * u[1] + j
                        y = mixed[:, 2, g, :]
                        last = v.scalar_tensor_tensor(y, b[:, j * T:(j + 1) * T], vec[:, VEC["pool_scale"]][:, g:g + 1],
                                                      y, ALU.mult, ALU.mult)
                elif kind == "mod":
                    c = u[1]
                    if c // 2 in (2, 5):
                        dve.wait_ge(gate_rows_loaded, 16)
                        row = gate_rows[:, c // 2 == 5, (c % 2) * W512:(c % 2 + 1) * W512]
                        last = v.tensor_tensor(row, b[:, :], row, ALU.add)
                    else:
                        bias = vec[:, VEC["ada_b"]][:, 4 * c:4 * c + 4]
                        last = v.tensor_tensor(mod[:, c, :], b[:, 0:4], bias, ALU.add)
                elif kind == "proj":
                    _, br, j = u
                    first = "c" if br in "abc" else "f"
                    at = dict(c=16, b=8, a=0, f=0, s=8)[br] + 2 * j
                    g = flat(gates[:, at:at + 2, :])
                    dve.wait_ge(gates_ready, sigmoids(at - 2 * j, 1 if br in "abc" else 2))
                    last = v.tensor_tensor(g, b[:, :], g, ALU.mult)
                    if br != first:
                        link(last)
                        if br == "b":
                            m, other = g, flat(gates[:, 16 + 2 * j:18 + 2 * j, :])
                        elif br == "a":
                            m, other = g, flat(gates[:, 8 + 2 * j:10 + 2 * j, :])
                        else:
                            m, other = flat(gates[:, 2 * j:2 * j + 2, :]), g
                        last = v.tensor_tensor(m, m, other, ALU.add)
                elif kind == "wout":
                    _, blk, t, half = u
                    x = x_res[:, t, half * W512:(half + 1) * W512]
                    if blk == 1:
                        last = v.tensor_tensor(x, b[:, :], x, ALU.add)
                    else:
                        tmp = sig[:, half, :]
                        link(v.tensor_tensor(tmp, b[:, :], gate_rows[:, 0, half * W512:(half + 1) * W512], ALU.mult))
                        last = v.tensor_tensor(x, x, tmp, ALU.add)
                elif kind == "logit":
                    t = u[1]
                    rb = vec[:, VEC["router_b"]]
                    if t == 0:
                        dve.wait_ge(o_done, 32)
                    v.tensor_tensor(rt[:, 32 + 4 * t:36 + 4 * t], b[:, 0:4], rb[:, 0:4], ALU.add)
                    last = v.tensor_tensor(rt[:, 40 + 16 * t:56 + 16 * t], b[:, 4:20], rb[:, 4:20], ALU.add)
                elif kind == "rank":
                    pos = rt[:, 300:336].rearrange("p (t e) -> p t e", t=TT)
                    sel = rt[:, 0:32].rearrange("p (t e) -> p t e", t=TT)
                    link(v.scalar_tensor_tensor(pos[:, :, 0:16], b[:, 0:32].rearrange("p (t e) -> p t e", t=TT), 1.0,
                                                sel, ALU.add, ALU.mult))
                    link(v.tensor_scalar(pos[:, :, 0:16], pos[:, :, 0:16], -1.0, None, ALU.add))
                    v.tensor_scalar(pos[:, :, 16:18], pos[:, :, 0:2], -float(SLOTS), None, ALU.add)
                    last = v.tensor_reduce(rt[:, 340:341], b[:, 32:48], X, ALU.max)
                last.then_inc(dve_evicted, 1)

            def pool():
                dve.wait_ge(*evicted(("fm", "ax", 1)))
                src = pool_x
                for i, w in enumerate(WINDOWS):
                    dst, h = (pool_a, pool_b)[i % 2], w // 2
                    v.tensor_copy(dst[:, i:4, 0:h], src[:, i:4, 0:h])
                    link(v.tensor_tensor(dst[:, i:4, h:T], src[:, i:4, h:T], src[:, i:4, 0:T - h], ALU.add))
                    src = dst
                inv = cs("inv_count").rearrange("p (g t) -> p g t", g=4)
                for g, w in enumerate(WINDOWS):
                    s = (pool_a, pool_b)[g % 2][:, g, :]
                    link(v.tensor_tensor(s[:, 0:16], s[:, 0:16], inv[:, g, :], ALU.mult))
                    v.tensor_tensor(pool_a[:, g, 0:16], s[:, 0:16], pool_x[:, g, 0:16], ALU.subtract)
                    last = v.scalar_tensor_tensor(pool_a[:, g, 16:T], s[:, 16:T], 1.0 / w, pool_x[:, g, 16:T],
                                                  ALU.mult, ALU.subtract)
                last.then_inc(pooled_ready, 1)

            def ada(c, half):
                w = wait_chunk(dve, ("ada", c)).rearrange("p (k n) -> p k n", n=W512)
                if c and not half:
                    dve.wait_ge(unit_done, UNITS.index(("mod", c - 1)) + 1)
                for k in range(4 * half, 4 * half + 4):
                    if k == 0:
                        ins = v.tensor_scalar(ada_acc[:, :], w[:, 0, :], c_act[:, 0:1], None, ALU.mult)
                    else:
                        ins = v.scalar_tensor_tensor(ada_acc[:, :], w[:, k, :], c_act[:, k:k + 1], ada_acc[:, :],
                                                     ALU.mult, ALU.add)
                    if k < KD - 1:
                        link(ins)
                    else:
                        ins.then_inc(ada_done, 1)

            def mods(i):
                c = (2, 8)[i]
                dve.wait_ge(*evicted(("mod", c + 1)))
                g = vec[:, VEC["norm1_g" if i == 0 else "norm2_g"]]
                v.scalar_tensor_tensor(aff[:, i, :], mod[:, c:c + 2, :].rearrange("p c j -> p (c j)"), 1.0, g,
                                       ALU.add, ALU.mult).then_inc(mods_ready, 1)

            def probs(h):
                s = score[:, h % 2, :]
                st = hstat[:, h % 2, :]
                b = score_bank[h % 2]
                dve.wait_ge(scores_done, h + 1)
                if h == 0:
                    dve.wait_ge(con_loaded, 16)
                if h >= 2:
                    if h - 2 < 24:
                        dve.wait_ge(pt_done, h - 1)
                    else:
                        dve.wait_ge(pt_evicted, h - 1)
                mask = cs("mask_causal" if h < 8 or 16 <= h < 24 else "mask_swa" if h < 16 else "mask_strict")
                if 16 <= h < 24:
                    v.scalar_tensor_tensor(s[:, 0:P], b[:, 0:P], foxT[:, 0, h - 16:h - 15], mask[:, 0:P], ALU.add, ALU.add)
                    v.scalar_tensor_tensor(s[:, P:384], b[:, P:384], foxT[:, 1, h - 16:h - 15], mask[:, P:384], ALU.add, ALU.add)\
                     .then_inc(scores_masked, 1)
                else:
                    v.tensor_tensor(s, b[:, 0:384], mask, ALU.add).then_inc(scores_masked, 1)
                dve.wait_ge(scores_masked, h + 1)
                if h < 24:
                    ins = v.tensor_reduce(st[:, 0:1], s[:, 0:P], X, ALU.max, negate=True)
                    ins = v.tensor_reduce(st[:, 1:2], s[:, P:384], X, ALU.max, negate=True)
                    if 8 <= h < 16:
                        link(ins)
                        link(v.tensor_scalar(st[:, 8:9], vec[:, VEC["sink"]][:, h - 8:h - 7], -1.0, None, ALU.mult))
                        ins = v.tensor_scalar(st[:, 0:2], st[:, 0:2], st[:, 8:9], None, ALU.min)
                    ins.then_inc(max_ready, 1)
                    dve.wait_ge(exp_done, h + 1)
                    if 8 <= h < 16:
                        link(v.tensor_tensor(st[:, 2:4], st[:, 2:4], st[:, 4:6], ALU.add))
                    link(v.reciprocal(st[:, 6:8], st[:, 2:4]))
                    v.tensor_scalar(s[:, 0:P], s[:, 0:P], st[:, 6:7], None, ALU.mult)
                    v.tensor_scalar(s[:, P:384], s[:, P:384], st[:, 7:8], None, ALU.mult).then_inc(probs_ready, 1)
                else:
                    dve.wait_ge(exp_done, h + 1)
                    z = soft[:, h % 2, :]
                    v.scalar_tensor_tensor(z, s, 0.0, z, ALU.max, ALU.add).then_inc(probs_ready, 1)

            def turned(h):
                if h >= 24:
                    dve.wait_ge(pt_done, h + 1)
                    s = score[:, h % 2, :]
                    v.tensor_tensor(s, s, trans_bank[h % 2][:, 0:384], ALU.subtract).then_inc(stick_ready, 1)

            def outputs(h):
                if h % 2 == 0:
                    return
                dve.wait_ge(o_done, h + 1)
                mixer = (0, 1, 0, 1)[h // 8]
                y = mixed[:, mixer, (h % 8) // 2, :]
                if h < 16:
                    if h in (1, 9):
                        dve.wait_ge(*evicted(("fm", "cz" if h == 1 else "bz", 1)))
                    v.tensor_tensor(y, o_bank[:, 0:T], y, ALU.mult).then_inc(o_evicted, 1)
                else:
                    v.tensor_copy(y, o_bank[:, 0:T]).then_inc(o_evicted, 1)

            def logf():
                dve.wait_ge(fox_log, 1)
                link(v.scalar_tensor_tensor(fox[:, 3, :], fox[:, 0, :], 0.0, fox[:, 1, :], ALU.min, ALU.subtract))
                v.tensor_tensor_scan(fox[:, 4, :], fox_ones[:, :], fox[:, 3, :], 0.0, ALU.mult, ALU.add)\
                 .then_inc(fox_ready, 1)

            def ranks(dst, logits, n, scratch):
                other = logits.unsqueeze(2).to_broadcast([P, n, 4, 4])
                own = logits.unsqueeze(3).to_broadcast([P, n, 4, 4])
                more = rt[:, scratch:scratch + 16 * n].rearrange("p (n i j) -> p n i j", n=n, i=4)
                same = rt[:, scratch + 128:scratch + 128 + 16 * n].rearrange("p (n i j) -> p n i j", n=n, i=4)
                tie = cs("tie").rearrange("p (i j) -> p i j", i=4).unsqueeze(1).to_broadcast([P, n, 4, 4])
                v.tensor_tensor(more, other, own, ALU.is_gt)
                link(v.tensor_tensor(same, other, own, ALU.is_equal))
                link(v.tensor_tensor(same, same, tie, ALU.mult))
                link(v.tensor_tensor(more, more, same, ALU.add))
                link(v.tensor_reduce(dst, more, X, ALU.add))

            def route():
                v.memset(y_pair, 0.0).then_inc(y_ready, 2)
                v.memset(combT, 0.0).then_inc(combT_evicted, 1)
                dve.wait_ge(*evicted(("logit", 1)))
                gl = rt[:, 32:40].rearrange("p (t g) -> p t g", t=TT)
                el = rt[:, 40:72].rearrange("p (n e) -> p n e", e=4)
                gd, ed = rt[:, 100:108].rearrange("p (t g) -> p t g", t=TT), rt[:, 110:142].rearrange("p (n e) -> p n e", e=4)
                gmax, emax = rt[:, 80:82], rt[:, 84:92]
                v.tensor_reduce(gmax, gl, X, ALU.max)
                link(v.tensor_reduce(emax, el, X, ALU.max))
                v.tensor_tensor(gd, gl, gmax.unsqueeze(2).to_broadcast([P, TT, 4]), ALU.subtract)
                v.tensor_tensor(ed, el, emax.unsqueeze(2).to_broadcast([P, 8, 4]), ALU.subtract).then_inc(group_shifted, 1)
                grank = rt[:, 150:158].rearrange("p (t g) -> p t g", t=TT)
                erank = rt[:, 160:192].rearrange("p (n e) -> p n e", e=4)
                ranks(grank, gl, TT, 400)
                ranks(erank, el, 8, 700)
                top = rt[:, 200:208]
                two = rt[:, 210:242].rearrange("p (n e) -> p n e", e=4)
                v.tensor_scalar(top, rt[:, 150:158], 0.5, None, ALU.is_lt)
                link(v.tensor_scalar(two, erank, 1.5, None, ALU.is_lt))
                sel = rt[:, 0:32].rearrange("p (n e) -> p n e", e=4)
                v.tensor_tensor(sel, two, top.unsqueeze(2).to_broadcast([P, 8, 4]), ALU.mult).then_inc(sel_ready, 1)
                dve.wait_ge(group_exp, 1)
                gsum, esum, f = rt[:, 250:252], rt[:, 254:262], rt[:, 264:272]
                v.tensor_reduce(gsum, gd, X, ALU.add)
                link(v.tensor_tensor(ed, ed, two, ALU.mult))
                link(v.tensor_reduce(esum, ed, X, ALU.add))
                v.reciprocal(gsum, gsum)
                link(v.reciprocal(f, esum))
                link(v.tensor_tensor(f, f, top, ALU.mult))
                link(v.tensor_tensor(f.rearrange("p (t g) -> p t g", t=TT), f.rearrange("p (t g) -> p t g", t=TT),
                                     gsum.unsqueeze(2).to_broadcast([P, TT, 4]), ALU.mult))
                comb = rt[:, 1000:1036].rearrange("p (t e) -> p t e", t=TT)
                for t in range(TT):
                    last = v.tensor_tensor(comb[:, t, 0:16].rearrange("p (g e) -> p g e", e=4), ed[:, 4 * t:4 * t + 4, :],
                                           f[:, 4 * t:4 * t + 4].unsqueeze(2).to_broadcast([P, 4, 4]), ALU.mult)
                link(last)
                link(v.tensor_copy(comb[:, :, 16:18], comb[:, :, 0:2]))

            def slots():
                dve.wait_ge(*evicted(("rank",)))
                v.tensor_tensor(onehot, iota, columns(pos, 0), ALU.is_equal).then_inc(onehot_ready, 1)
                r = rt[:, 344:348]
                for i in range(3):
                    last = v.tensor_scalar(r[:, i:i + 1], rt[:, 340:341], SLOTS * (i + 1) + 0.5, None, ALU.is_gt)
                link(last)
                link(v.tensor_reduce(r[:, 3:4], r[:, 0:3], X, ALU.add))
                v.tensor_scalar(n_rounds[:, :], r[:, 3:4], 1.0, None, ALU.add).then_inc(rounds_ready, 1)

            pos = rt[:, 300:336].rearrange("p (t e) -> p t e", t=TT)
            comb = rt[:, 1000:1036].rearrange("p (t e) -> p t e", t=TT)
            iota = cs("iota").unsqueeze(1).unsqueeze(1).to_broadcast([P, TT, 2, SLOTS])

            def columns(ap, pair):
                return ap[:, :, bass.ds(pair * 2, 2)].unsqueeze(3).to_broadcast([P, TT, 2, SLOTS])

            n = 0
            for s in STEPS:
                if s[0] == "unit":
                    unit(n, s[1:])
                    n += 1
                elif s[0] != "sigmoid":
                    dict(norm=norm, ada=ada, S=probs, T=turned, V=outputs, pool=pool, mods=mods, logf=logf,
                         route=route, slots=slots)[s[0]](*s[1:])

            def xg_half(it):
                dve.wait_ge(gather_done, it + 1)
                for k in range(4, KD):
                    last = v.tensor_scalar(xg[:, k, :], x_bank[1][:, (k - 4) * P:(k - 3) * P], aff[:, 1, k:k + 1],
                                           mod[:, 7, k - 4:k - 3], ALU.mult, ALU.add)
                last.then_inc(xg_dve, 1)

            xg_half(0)
            dve.wait_ge(rounds_ready, 1)
            rounds = dve.value_load(n_rounds[0:1, 0:1], min_val=1, max_val=T // SLOTS)
            with dve.Fori(0, rounds) as r:
                with dve.Fori(0, PAIRS) as pair:
                    it = r * PAIRS + pair
                    dve.wait_ge(onehot_ready, it + 1)
                    v.tensor_tensor(combine, onehot, columns(comb, pair), ALU.mult).then_inc(combine_ready, 1)
                    dve.wait_ge(gather_done, it + 1)
                    dve.wait_ge(combine_ready, it + 1)
                    v.tensor_tensor(onehot, iota, columns(pos, pair + 1), ALU.is_equal).then_inc(onehot_ready, 1)
                    for e in range(2):
                        dve.wait_ge(silu_done, it * 2 + e + 1)
                        v.tensor_tensor(act[e * SLOTS:(e + 1) * SLOTS, :], sil[HD:P, e, :], gu_bank[e][HD:P, :], ALU.mult)\
                         .then_inc(act_ready, 1)
                    dve.wait_ge(combT_done, it + 1)
                    dve.wait_ge(scatter_done, it + 1)
                    v.tensor_copy(combT, gu_bank[0][:, 0:T]).then_inc(combT_evicted, 1)
                    xg_half(it + 1)
                    for e in range(2):
                        dve.wait_ge(down_done, it * 2 + e + 1)
                        rows = slice(e * SLOTS, (e + 1) * SLOTS)
                        v.tensor_tensor(y_pair[rows, 0:W512], gu_bank[e][0:HD, :], gate_rows[0:HD, 1, 0:W512], ALU.mult)
                        v.tensor_tensor(y_pair[rows, W512:D], gu_bank[e][HD:P, :], gate_rows[HD:P, 1, W512:D], ALU.mult)\
                         .then_inc(y_ready, 1)
                dve.wait_ge(onehot_ready, r * PAIRS + PAIRS + 1)
                v.tensor_scalar(pos, pos, -float(SLOTS), None, ALU.add)
            for t in range(TT):
                norm(4, t)


_MATRICES = ["x", "w_in", "pool_w", "w_proj_a", "w_proj_b", "w_proj_c", "w_out", "ada_w_2", "w_in_2",
             "w_branch_fox_2", "w_branch_sb_2", "w_out_2", "expert_w_gate_2", "expert_w_up_2", "expert_w_down_2"]


def kernel(**inputs):
    import concourse.bacc as bacc
    from concourse.bass_utils import run_bass_kernel_spmd

    inp = {k: np.asarray(v) for k, v in inputs.items()}
    columns = lambda v: v.reshape(-1, P).T
    rows = lambda v: np.broadcast_to(v.reshape(1, -1), (P, v.size))
    forget = np.zeros((P, 1), np.float32)
    forget[0:8, 0] = inp["b_forget_2"][0]
    router_b = np.concatenate([inp["router_group_b_2"][0], inp["router_expert_b_2"][0]])
    vec = np.concatenate([np.full((P, 1), EPS, np.float32), columns(inp["norm_g"]), columns(inp["norm1_g_2"]), columns(inp["norm2_g_2"]),
                          columns(inp["c_2"]), columns(inp["pool_scale"]), columns(inp["ada_b_2"]), forget,
                          rows(inp["sink_logits"]), rows(router_b)], 1)
    ada_b = inp["ada_b_2"].reshape(N_MOD, D)
    arrays = {n: np.ascontiguousarray(inp[n]) for n in _MATRICES}
    arrays["con"] = constants()
    arrays["vec"] = np.ascontiguousarray(vec)
    arrays["fin1"] = np.ascontiguousarray(rows(inp["final_norm_g"]))
    arrays["fin2"] = np.ascontiguousarray(rows(inp["final_g_2"]))
    arrays["gate_b"] = np.ascontiguousarray(np.stack([rows(ada_b[2]), rows(ada_b[5])], 1))
    arrays["router_w"] = np.ascontiguousarray(np.concatenate([inp["router_group_w_2"][0], inp["router_expert_w_2"][0]], 1))

    nc = bacc.Bacc("TRN2", target_bir_lowering=False, num_devices=1, dynamic_dma_scratch_size=1024)
    aps = {n: nc.dram_tensor("in_" + n, v.shape, mybir.dt.from_np(v.dtype), kind="ExternalInput").ap()
           for n, v in arrays.items()}
    out = nc.dram_tensor("out", (1, T, D), F32, kind="ExternalOutput").ap()
    two_block_kernel(nc, aps, out)
    result = run_bass_kernel_spmd(nc, [{"in_" + n: v for n, v in arrays.items()}], core_ids=[0])
    return result.results[0]["out"]
```

```python
from contextlib import ExitStack

import numpy as np
import concourse.bass as bass
from concourse import mybir

F32 = mybir.dt.float32
F32R = mybir.dt.float32r
I32 = mybir.dt.int32
ALU = mybir.AluOpType
ACT = mybir.ActivationFunctionType
X = mybir.AxisListType.X

LN_EXP, SILU_SET = "natural_log_exp_and_others", "silu_and_others"
P = 128
T = 256
TT = T // P
D = 1024
KD = D // P
HD = 64
W512 = 512
EPS = 1e-6
NEG = -1e30
N_MOD = 6
N_EXPERTS = 16
EXPERTS_PER_GROUP = 4
N_GROUPS = 4
FF = 512
SLOTS = 64
PAIRS = N_EXPERTS // 2
WINDOWS = (2, 4, 8, 16)
CHUNK = KD * W512
RING = 5
SPLIT = 4
POOL_FROM = 1
PIECES = (1, 0, 2, 3)

IN1 = dict(ax=0, az=512, bq=1024, bkv=1536, bz=1792, cq=2304, ck=2816, cv=3328, cz=3840, gate=4352)
IN2 = dict(qa=0, ka=512, va=1024, fa=1536, qb=1544, kb=2056, vb=2568, gate=3080)

VEC = {}
_at = 0
for _name, _n in (("eps", 1), ("norm_g", 8), ("norm1_g", 8), ("norm2_g", 8), ("c", 8), ("pool_scale", 4),
                  ("ada_b", 48), ("b_forget", 1), ("sink", 8), ("router_b", 20)):
    VEC[_name] = slice(_at, _at + _n)
    _at += _n
N_VEC = _at

CON = {}
_at = 0
for _name, _n in (("ident", 128), ("mask_causal", 384), ("mask_swa", 384), ("mask_strict", 384),
                  ("suffix", 128), ("before", 128), ("ones", 256), ("iota", 64), ("inv_count", 64),
                  ("tie", 16)):
    CON[_name] = slice(_at, _at + _n)
    _at += _n
N_CON = _at


def constants():
    c = np.zeros((P, N_CON), np.float32)
    i, j = np.arange(P)[:, None], np.arange(P)[None, :]
    causal = np.where(j <= i, 0.0, NEG)
    c[:, CON["ident"]] = i == j
    c[:, CON["mask_causal"]] = np.concatenate([causal, np.zeros((P, P)), causal], 1)
    c[:, CON["mask_swa"]] = np.concatenate([causal, np.where(j > i, 0.0, NEG), causal], 1)
    strict = np.where(i < j, 0.0, NEG)
    c[:, CON["mask_strict"]] = np.concatenate([strict, np.zeros((P, P)), strict], 1)
    c[:, CON["suffix"]] = i >= j
    c[:, CON["before"]] = i < j
    c[:, CON["ones"]] = 1.0
    c[:, CON["iota"]] = np.arange(SLOTS)
    c[:, CON["inv_count"]] = np.concatenate([1.0 / np.minimum(np.arange(16) + 1, w) for w in WINDOWS])
    c[:, CON["tie"]] = (np.arange(4)[None, :] < np.arange(4)[:, None]).reshape(-1)
    return c


def plan():
    steps = []
    unit = lambda *u: steps.append(("unit",) + u)

    def heads(todo, n=1):
        for _ in range(n):
            h = todo.pop(0)
            for kind, g in (("S", h), ("T", h - 1), ("V", h - 2)):
                if first <= g < last:
                    steps.append((kind, g))

    ada = [c for c in range(2 * N_MOD) for _ in range(2)]
    ada_due = []

    def some_ada(n=2):
        for _ in range(n):
            if ada_due and ada[:1] != ada_due[:1]:
                unit("mod", ada_due.pop(0))
            if ada:
                half = len(ada) % 2
                steps.append(("ada", ada[0], half))
                if half:
                    ada_due.append(ada[0])
                ada.pop(0)

    steps += [("norm", 0, 0), ("norm", 0, 1)]
    unit("hT", 0, 0, 0)
    unit("hT", 0, 0, 1)
    unit("hT", 0, 1, 0)
    unit("hT", 0, 1, 1)
    unit("tm", "cv", 0)
    unit("tm", "cv", 1)
    for name in ("cz", "bz", "az", "ax", "cq", "ck"):
        unit("fm", name, 0)
        unit("fm", name, 1)
        some_ada()
        if name == "ax":
            steps.append(("pool",))
    steps.append(("load_final_g", 0))
    first, last = 0, 16
    todo = list(range(0, 18))
    seq = [("fm", "bq", 0), ("fm", "bq", 1), ("bkv",), ("mix", 0), ("mix", 1)]
    seq += [("tm", f"g{i}", t) for i in (4, 5, 2, 3, 0, 1) for t in range(TT)]
    for n, u in enumerate(seq):
        unit(*u)
        if todo:
            heads(todo)
        if n == 10:
            steps.append(("y_split", "c"))
        if n == 11:
            steps.append(("y_split", "a"))
        some_ada(n % 2)
    while todo:
        heads(todo)
    steps.append(("fa_split",))
    steps += [("y_split", "b"), ("sigmoid", 16)]
    for br in "cb":
        for t in range(TT):
            for half in range(2):
                unit("proj", br, t, half)
                some_ada(1)
                if (t, half) == (0, 1):
                    steps.append(("sigmoid", 8 if br == "c" else 0))
    while ada or ada_due:
        some_ada()
    steps.append(("mods", 0))

    def merge_and_out(br, blk):
        unit("proj", br, 0, 0)
        unit("proj", br, 0, 1)
        unit("proj", br, 1, 0)
        unit("mT", blk, 0, 0)
        unit("mT", blk, 0, 1)
        unit("proj", br, 1, 1)
        unit("wout", blk, 0, 0)
        unit("mT", blk, 1, 0)
        unit("mT", blk, 1, 1)
        unit("wout", blk, 0, 1)

    merge_and_out("a", 1)
    steps += [("norm", 1, 0), ("norm", 2, 0)]
    unit("wout", 1, 1, 0)
    unit("hT", 1, 0, 0)
    unit("hT", 1, 0, 1)
    unit("wout", 1, 1, 1)
    steps += [("norm", 1, 1), ("norm", 2, 1)]
    unit("tm", "va", 0)
    unit("hT", 1, 1, 0)
    unit("hT", 1, 1, 1)
    unit("tm", "vb", 0)
    unit("tm", "va", 1)
    unit("tm", "vb", 1)
    for name in ("qa", "ka"):
        unit("fm", name, 0)
        unit("fm", name, 1)
    unit("fa",)
    steps.append(("logf",))
    unit("fm", "qb", 0)
    unit("FT",)
    first, last = 16, 32
    todo = list(range(16, 34))
    seq = [(("fm", "qb", 1), 1), (("fm", "kb", 0), 1), (("fm", "kb", 1), 1), (("tm", "h0", 0), 1),
           (("tm", "h0", 1), 1), (("tm", "h1", 0), 1), (("tm", "h1", 1), 2), (("tm", "h2", 0), 1),
           (("tm", "h2", 1), 2), (("tm", "h3", 0), 1), (("tm", "h3", 1), 2), (("proj", "f", 0, 0), 1),
           (("proj", "f", 0, 1), 1), (("proj", "f", 1, 0), 1), (("proj", "f", 1, 1), 1)]
    for u, n in seq:
        unit(*u)
        heads(todo, n)
        if u == ("tm", "h1", 1):
            steps.append(("sigmoid", 0))
        if u == ("tm", "h3", 0):
            steps.append(("y_split", "f"))
    assert not todo
    steps += [("y_split", "s"), ("sigmoid", 8), ("mods", 1), ("load_final_g", 1)]
    merge_and_out("s", 2)
    steps.append(("norm", 3, 0))
    unit("wout", 2, 1, 0)
    unit("hT", 2, 0, 0)
    unit("hT", 2, 0, 1)
    unit("wout", 2, 1, 1)
    steps.append(("norm", 3, 1))
    unit("logit", 0)
    unit("hT", 2, 1, 0)
    unit("hT", 2, 1, 1)
    unit("logit", 1)
    steps.append(("route",))
    unit("rank",)
    steps.append(("slots",))

    split = []
    for s in steps:
        split += [c for c in chunk_of(s) if c[0] != "ada" and c not in split]
    before = {}
    for m, c in enumerate(split):
        first_use = next(i for i, s in enumerate(steps) if c in chunk_of(s))
        if m:
            free = max(i for i, s in enumerate(steps) if m > 1 and split[m - 2] in chunk_of(s) or
                       m == 1 and s == ("unit", "tm", "cv", 0))
            place = next(i for i in range(free + 1, first_use + 1) if steps[i][0] == "unit")
        else:
            place = first_use
        before.setdefault(place, []).extend(("split", c, q) for q in PIECES)
    steps = [x for i, s in enumerate(steps) for x in before.get(i, []) + [s]]

    chunks = []
    for s in steps:
        for name in chunk_of(s):
            if name not in chunks:
                chunks.append(name)
    return steps, chunks


def chunk_of(step):
    if step[0] == "ada":
        return [("ada", step[1])]
    if step[0] == "split":
        return [step[1]]
    if step[0] == "unit" and step[1] in ("fm", "tm"):
        return [(step[2],)]
    if step[0] == "unit" and step[1] == "bkv":
        return [("bkv",)]
    if step[0] == "unit" and step[1] == "proj":
        return [("proj", step[2])]
    if step[0] == "unit" and step[1] == "wout":
        return [("wout", step[2], step[4])]
    return []


STEPS, CHUNKS = plan()
UNITS = [s[1:] for s in STEPS if s[0] == "unit"]
SILU = ("cz", "bz", "az")


def evictor(u):
    if u[0] in ("tm", "bkv", "fa", "FT") or (u[0] == "fm" and u[1] not in SILU):
        return "act"
    return "dve"


def evict_count(u):
    n = UNITS.index(u)
    return sum(evictor(v) == evictor(u) for v in UNITS[:n + 1])


def last_reader(chunk, first=False):
    if chunk[0] == "ada":
        order = [s[1] for s in STEPS if s[0] == "ada" and s[2]]
        return "dve", order.index(chunk[1]) + 1
    n = [i for i, u in enumerate(UNITS) if chunk in chunk_of(("unit",) + u)][0 if first else -1]
    return "pe", n + 1


SPLITS = [s[1] for s in STEPS if s[0] == "split" and s[2] == PIECES[0]]
Y_SPLITS = [s[1] for s in STEPS if s[0] == "y_split"]
HI_UNITS = [u for u in UNITS if u[0] == "mT" or u[0] == "hT" and u[1] < 2]
SILU_UNITS = [u for u in UNITS if u[0] == "fm" and u[1] in SILU]
SIGMOIDS = [s for s in STEPS if s[0] == "sigmoid"]
NORMS = [s[1:] for s in STEPS if s[0] == "norm"] + [(4, 0), (4, 1)]
XN_NORMS = [s for s in NORMS if s[0] in (0, 2, 3)]


def two_block_kernel(nc, a, out):
    x_in, w_in1, w_in2 = a["x"][0], a["w_in"][0], a["w_in_2"][0]

    def k_rows(w, cols):
        return w[:, cols].rearrange("(k p) n -> p k n", p=P)

    def chunk_source(c):
        if c[0] == "ada":
            return k_rows(a["ada_w_2"][0], slice(c[1] * W512, (c[1] + 1) * W512))
        if c[0] == "proj":
            w = dict(a="w_proj_a", b="w_proj_b", c="w_proj_c", f="w_branch_fox_2", s="w_branch_sb_2")[c[1]]
            return k_rows(a[w][0], slice(0, D))
        if c[0] == "wout":
            return k_rows(a[("w_out", "w_out_2")[c[1] - 1]][0], slice(c[2] * W512, (c[2] + 1) * W512))
        if c[0] == "bq":
            return k_rows(a["w_bq"], slice(0, W512))
        if c[0] == "bkv":
            return k_rows(w_in1, slice(IN1["bkv"], IN1["bkv"] + 256))
        if c[0] in IN1:
            at, w = IN1[c[0]], w_in1
        elif c[0] in IN2:
            at, w = IN2[c[0]], w_in2
        elif c[0][0] == "g":
            at, w = IN1["gate"] + W512 * int(c[0][1]), w_in1
        else:
            at, w = IN2["gate"] + W512 * int(c[0][1]), w_in2
        return k_rows(w, slice(at, at + W512))

    with ExitStack() as ctx:
        def sb(name, shape, dt=F32):
            return ctx.enter_context(nc.sbuf_tensor(name, shape, dt))

        def sem(name):
            return ctx.enter_context(nc.semaphore(name))

        rounded = {}

        def two_names(name, shape):
            at = -(-nc.sbuf_base // 32) * 32
            t = sb(name, shape)
            rounded[name] = nc.alloc_sbuf_tensor_at(name + "_rounded", shape, F32R, offset=at)
            return t

        shared = dict(hT=[P, KD, T], work=[P, 6656], mixed=[P, 3, 4, T],
                      gates=[P, 24, T], fa_w=[P, KD, 8], fa_hi=[P, KD, 8])
        ring = [two_names(f"ring{i}", [P, CHUNK]) for i in range(RING + 2)]
        hT, work, mixed, gates, fa_w, fa_hi = (two_names(n, shape) for n, shape in shared.items())
        as_rounded = lambda ap: bass.AP(rounded[ap.tensor.name], ap.offset, ap.ap)
        was_rounded = lambda ap: as_rounded(ap).bitcast(F32)
        con = sb("con", [P, N_CON])
        vec = sb("vec", [P, N_VEC])
        gate_rows = sb("gate_rows", [P, 2, D])
        x_res = sb("x_res", [P, TT, D])
        sig = sb("sig", [P, 2, W512])
        ada_acc = sb("ada_acc", [P, W512])
        attn = sb("attn", [P, 4, 384])
        score = attn[:, 0:2, :]
        probT = attn[:, 2:4, :]
        stat = sb("stat", [P, 10, 8])
        hstat = sb("hstat", [P, 2, 12])
        mod = sb("mod", [P, 2 * N_MOD, 4])
        aff = sb("aff", [P, 2, KD])
        c_act = sb("c_act", [P, KD])
        c_tmp = sb("c_tmp", [P, 2, KD])
        pw = sb("pw", [P, 4, P])
        rt_w = sb("rt_w", [P, KD, 20])
        fox_neg_ident = sb("fox_neg_ident", [8, 8])
        foxT = sb("foxT", [P, TT, 8])
        n_rounds = sb("n_rounds", [P, 1], I32)

        gate_tm = gates[:, :, :].rearrange("p k t -> p (k t)").rearrange("p (b t f) -> p b t f", b=3, t=TT)
        xn = gate_tm[:, 0]
        fin_g = sig[:, :, :].rearrange("p h n -> p (h n)")
        fox = sig[0:8, :, :].rearrange("p h n -> p (h n)").rearrange("p (r t) -> p r t", r=4)
        tmp = attn[:, :, :].rearrange("p b n -> p (b n)")[:, D:D + W512]
        junk = attn[:, :, :].rearrange("p b n -> p (b n)")[:, 0:D]
        hT_lo = work[:, 4608:6656].rearrange("p (k t) -> p k t", k=KD)
        fm4 = lambda at: work[:, at:at + 1024].rearrange("p (n t) -> p n t", n=4)
        y_high = dict(c=fm4(0), b=fm4(1024), a=fm4(2048), f=fm4(0), s=fm4(1024))
        y_low = {br: mixed[:, i] for br, i in dict(c=0, b=1, a=2, f=0, s=1).items()}
        merged_hi = gates[:, 16:24, :]
        merged_lo = lambda blk, half: mixed[:, (0, blk)[half]]
        pool_x, pool_a, pool_b = (gates[:, n:n + 4, :] for n in (12, 16, 20))
        tm2 = lambda at: work[:, at:at + 1024].rearrange("p (t n) -> p t n", t=TT)
        qm, km, vm, qs = fm4(0), fm4(1024), tm2(2048), fm4(3072)
        kb2, vb2 = gates[:, 16:20, :], gates[:, 20:24, :].rearrange("p k t -> p (k t)").rearrange("p (t n) -> p t n", t=TT)
        kvs = work[:, 4096:4608]
        soft = mixed[:, 2, 0:3, :].rearrange("p k t -> p (k t)").rearrange("p (b n) -> p b n", b=2)
        xg = work[:, 0:1024].rearrange("p (k s) -> p k s", k=KD)
        onehot = work[:, 1024:1280].rearrange("p (t e s) -> p t e s", t=TT, e=2)
        combine = work[:, 1280:1536].rearrange("p (t e s) -> p t e s", t=TT, e=2)
        act = work[:, 1536:2048]
        sil = work[:, 2048:3072].rearrange("p (e f) -> p e f", e=2)
        actT = work[:, 3072:3584].rearrange("p (k s) -> p k s", k=4)
        y_pair = work[:, 3584:4608]
        combT = work[:, 4608:4864]
        rt = work[:, 4864:5964]

        psum = ctx.enter_context(nc.psum_tensor("psum", [P, 8, W512], F32))
        bank = [psum[:, i, :] for i in range(8)]
        unit_bank, o_bank, score_bank, trans_bank = bank[0:3], bank[3], bank[4:6], bank[6:8]
        out_bank = bank[0:4]
        gu_bank, x_bank = bank[4:6], bank[6:8]

        cs = lambda name: con[:, CON[name]]
        ident, ones = cs("ident"), cs("ones")

        x_loaded = [sem(f"x_loaded{t}") for t in range(TT)]
        ident_loaded = sem("ident_loaded")
        con_loaded = sem("con_loaded")
        gate_rows_loaded = sem("gate_rows_loaded")
        vec_loaded = sem("vec_loaded")
        small_loaded = sem("small_loaded")
        fin1_loaded = sem("fin1_loaded")
        fin2_loaded = sem("fin2_loaded")
        chunk_loaded = [sem(f"chunk_loaded{s}") for s in range(RING + 2)]
        unit_done = sem("unit_done")
        act_evicted = sem("act_evicted")
        dve_evicted = sem("dve_evicted")
        sig_ready = sem("sig_ready")
        ada_done = sem("ada_done")
        c_exp = sem("c_exp")
        sumsq_ready = sem("sumsq_ready")
        ms_ready = sem("ms_ready")
        guess_ready = sem("guess_ready")
        gates_ready = sem("gates_ready")
        chunk_hi = sem("chunk_hi")
        chunk_split = sem("chunk_split")
        chunk_split_pool = sem("chunk_split_pool")
        y_hi = sem("y_hi")
        y_split_done = sem("y_split_done")
        hi_ready = sem("hi_ready")
        fa_hi_ready = sem("fa_hi_ready")
        fa_split_done = sem("fa_split_done")
        x1_ready = sem("x1_ready")
        xn_ready = sem("xn_ready")
        pooled_ready = sem("pooled_ready")
        scores_done = sem("scores_done")
        scores_masked = sem("scores_masked")
        max_ready = sem("max_ready")
        exp_done = sem("exp_done")
        probs_ready = sem("probs_ready")
        pt_done = sem("pt_done")
        stick_ready = sem("stick_ready")
        pt_evicted = sem("pt_evicted")
        o_done = sem("o_done")
        o_evicted = sem("o_evicted")
        fox_abs = sem("fox_abs")
        fox_log = sem("fox_log")
        fox_ready = sem("fox_ready")
        mods_ready = sem("mods_ready")
        group_shifted = sem("group_shifted")
        group_exp = sem("group_exp")
        sel_ready = sem("sel_ready")
        rounds_ready = sem("rounds_ready")
        dve_chain = sem("dve_chain")
        act_chain = sem("act_chain")
        onehot_ready = sem("onehot_ready")
        gather_done = sem("gather_done")
        xg_act = sem("xg_act")
        xg_dve = sem("xg_dve")
        gu_done = sem("gu_done")
        silu_done = sem("silu_done")
        act_ready = sem("act_ready")
        combine_ready = sem("combine_ready")
        actT_done = sem("actT_done")
        combT_done = sem("combT_done")
        actT_evicted = sem("actT_evicted")
        combT_evicted = sem("combT_evicted")
        down_done = sem("down_done")
        y_ready = sem("y_ready")
        scatter_done = sem("scatter_done")
        tile_done = sem("tile_done")
        out_ready = sem("out_ready")
        stored = sem("stored")

        block = ctx.enter_context(nc.Block())

        def evicted(u):
            return (act_evicted if evictor(u) == "act" else dve_evicted), evict_count(u)

        def sigmoids(first_tile, block):
            return [n for n, g in enumerate(SIGMOIDS) if g[1] == first_tile][block - 1 if first_tile < 16 else 0] + 1

        def wait_chunk(eng, c):
            n = CHUNKS.index(c)
            eng.wait_ge(chunk_loaded[n % RING], 16 * (n // RING + 1))
            return ring[n % RING][:, :]

        def piece_of(c, q):
            n = CHUNK // (2 if c == ("bkv",) else 1) // SPLIT
            return slice(q * n, (q + 1) * n)

        def dense_uses(s):
            return len(range(s, len(CHUNKS), RING)) if s < RING else 0

        first_expert_slot = len(CHUNKS) % RING
        slot_of = lambda j: (first_expert_slot + j) % RING if j < RING else j

        def high(c):
            return ring[RING + SPLITS.index(c) % 2][:, :]
        PAIR_LOADS = (("expert_w_gate_2", 0), ("expert_w_up_2", 0), ("expert_w_gate_2", 1),
                      ("expert_w_up_2", 1), ("expert_w_down_2", 0), ("expert_w_down_2", 1))

        def pair_chunk(j):
            c = ring[slot_of(j)][:, :]
            return c.rearrange("p (k n) -> p k n", n=W512 if j < 4 else D)

        def pair_loaded(eng, j, it):
            eng.wait_ge(chunk_loaded[slot_of(j)], it * 16 + 16 * (dense_uses(slot_of(j)) + 1))

        @block.sync
        def _(sp):
            def wait_slot_free(n):
                if n >= RING:
                    who, count = last_reader(CHUNKS[n - RING])
                    sp.wait_ge(ada_done if who == "dve" else unit_done, count)

            for t in range(TT):
                sp.dma_start(x_res[:, t, :], x_in[t * P:(t + 1) * P, :]).then_inc(x_loaded[t], 16)
            for n, c in enumerate(CHUNKS):
                wait_slot_free(n)
                src = chunk_source(c)
                dst = ring[n % RING][:, 0:src.shape[1] * src.shape[2]]
                sp.dma_start(dst.rearrange("p (k n) -> p k n", n=src.shape[2]), src)\
                  .then_inc(chunk_loaded[n % RING], 16)

            def load_pair(it, pair, first):
                for j, (name, e) in enumerate(PAIR_LOADS):
                    if first and j < RING:
                        wait_slot_free(len(CHUNKS) + j)
                    elif first:
                        sp.wait_ge(unit_done, UNITS.index(("wout", 2, 1, 1)) + 1)
                    elif j < 4:
                        sp.wait_ge(gu_done, it * 2 - 1 + j // 2)
                    else:
                        sp.wait_ge(down_done, it * 2 - 1 + j - 4)
                    w = a[name][0][bass.ds(pair * 2 + e, 1)]
                    sp.dma_start(pair_chunk(j), w.rearrange("e (k p) n -> p (e k) n", p=P))\
                      .then_inc(chunk_loaded[slot_of(j)], 16)

            load_pair(0, 0, True)
            with sp.Fori(1, PAIRS) as pair:
                load_pair(pair, pair, False)
            sp.wait_ge(rounds_ready, 1)
            rounds = sp.value_load(n_rounds[0:1, 0:1], min_val=1, max_val=T // SLOTS)
            with sp.If(rounds > 1):
                with sp.Fori(1, rounds) as r:
                    with sp.Fori(0, PAIRS) as pair:
                        load_pair(r * PAIRS + pair, pair, False)
            for t in range(TT):
                sp.wait_ge(out_ready, t + 1)
                sp.dma_start(out[0][t * P:(t + 1) * P, :], x_res[:, t, :]).then_inc(stored, 16)
            sp.wait_ge(stored, 16 * TT)

        @block.tensor
        def _(pe):
            def product(out, a, b, start, stop):
                nc.tensor.matmul(out, a[0], b[0], start=start, stop=False, skip_group_check=True)
                nc.tensor.matmul(out, a[0], b[1], start=False, stop=False, skip_group_check=True)
                return nc.tensor.matmul(out, a[1], b[0], start=False, stop=stop, skip_group_check=True)

            def x_parts(k, at, n):
                return as_rounded(hT[:, k, at:at + n]), as_rounded(hT_lo[:, k, at:at + n])

            def parts(c, width):
                hi, lo = (x.rearrange("p (k n) -> p k n", n=width)
                          for x in (high(c), ring[CHUNKS.index(c) % RING][:, :]))
                return lambda k, at, n: (as_rounded(hi[:, k, at:at + n]), as_rounded(lo[:, k, at:at + n]))

            def wait_piece(n, c, q):
                if last_reader(c, first=True)[1] == n + 1:
                    m = SPLITS.index(c)
                    if q < POOL_FROM:
                        pe.wait_ge(chunk_split, POOL_FROM * m + q + 1)
                    else:
                        pe.wait_ge(chunk_split_pool, (SPLIT - POOL_FROM) * m + q - POOL_FROM + 1)

            def unit(n, u):
                b = unit_bank[n % 3]
                if n >= 3:
                    pe.wait_ge(*evicted(UNITS[n - 3]))
                kind = u[0]
                if kind == "hT":
                    _, norm, t, half = u
                    pe.wait_ge(xn_ready, XN_NORMS.index(((0, 2, 3)[norm], t)) + 1)
                    if n == 0:
                        pe.wait_ge(ident_loaded, 16)
                    for k in range(4):
                        f = (4 * half + k) * P
                        last = nc.tensor.transpose(b[:, k * P:(k + 1) * P], xn[:, t, f:f + P], ident)
                elif kind in ("fm", "tm", "bkv", "fa"):
                    block2 = kind == "fa" or u[1:2] and (u[1] in IN2 or u[1][0] == "h")
                    pe.wait_ge(*evicted(("hT", 1 if block2 else 0, u[2] if kind == "tm" else 1, 1)))
                    if kind == "fa":
                        pe.wait_ge(fa_split_done, 1)
                        for k in range(KD):
                            last = product(b[0:8, 0:T], (as_rounded(fa_hi[:, k, :]), as_rounded(fa_w[:, k, :])), x_parts(k, 0, T),
                                           k == 0, k == KD - 1)
                    elif kind == "bkv":
                        w = parts(("bkv",), 256)
                        for k in range(KD):
                            wait_piece(n, ("bkv",), k // 2)
                            product(b[:, 0:T], w(k, 0, P), x_parts(k, 0, T), k == 0, k == KD - 1)
                        for t in range(TT):
                            for k in range(KD):
                                last = product(b[:, T + t * P:T + (t + 1) * P], x_parts(k, t * P, P), w(k, P, P),
                                               k == 0, k == KD - 1)
                    elif kind == "tm":
                        w = parts((u[1],), W512)
                        for k in range(KD):
                            wait_piece(n, (u[1],), k // 2)
                            last = product(b, x_parts(k, u[2] * P, P), w(k, 0, W512), k == 0, k == KD - 1)
                    else:
                        w = parts((u[1],), W512)
                        for j in range(2):
                            n_tile = 2 * u[2] + j
                            for k in range(KD):
                                if j == 0:
                                    wait_piece(n, (u[1],), k // 2)
                                last = product(b[:, j * T:(j + 1) * T], w(k, n_tile * P, P), x_parts(k, 0, T),
                                               k == 0, k == KD - 1)
                elif kind == "mix":
                    pe.wait_ge(pooled_ready, 1)
                    pe.wait_ge(small_loaded, 16 * 3)
                    for j in range(2):
                        g = 2 * u[1] + j
                        last = nc.tensor.matmul(b[:, j * T:(j + 1) * T], pw[:, g, :], pool_a[:, g, :],
                                                start=True, stop=True)
                elif kind == "mod":
                    c = u[1]
                    pe.wait_ge(con_loaded, 16)
                    pe.wait_ge(ada_done, c + 1)
                    if c // 2 in (2, 5):
                        last = nc.tensor.matmul(b[:, :], ones[:, 0:P], ada_acc[:, :], start=True, stop=True)
                    else:
                        for j in range(4):
                            last = nc.tensor.matmul(b[:, j:j + 1], ada_acc[:, j * P:(j + 1) * P], ones[:, 0:1],
                                                    start=True, stop=True)
                elif kind == "proj":
                    _, br, t, half = u
                    w = parts(("proj", br), D)
                    pe.wait_ge(y_split_done, Y_SPLITS.index(br) + 1)
                    for k in range(4):
                        wait_piece(n, ("proj", br), k)
                        y = [as_rounded(x[:, k, t * P:(t + 1) * P]) for x in (y_high[br], y_low[br])]
                        last = product(b, y, w(k, half * W512, W512), k == 0, k == 3)
                elif kind == "mT":
                    _, blk, t, half = u
                    pe.wait_ge(*evicted(("proj", "a" if blk == 1 else "s", t, half)))
                    for k in range(4):
                        f = (4 * half + k) * P
                        last = nc.tensor.transpose(b[:, k * P:(k + 1) * P], gate_tm[:, 0, t, f:f + P], ident)
                elif kind == "wout":
                    _, blk, t, half = u
                    w = parts(("wout", blk, half), W512)
                    pe.wait_ge(*evicted(("mT", blk, t, 1)))
                    for k in range(KD):
                        wait_piece(n, ("wout", blk, half), k // 2)
                        m = [as_rounded(x[:, i, t * P:(t + 1) * P]) for x, i in ((merged_hi, k), (merged_lo(blk, k // 4), k % 4))]
                        last = product(b, m, w(k, 0, W512), k == 0, k == KD - 1)
                elif kind == "FT":
                    pe.wait_ge(fox_ready, 1)
                    for t in range(TT):
                        last = nc.tensor.transpose(b[:, t * 8:(t + 1) * 8], fox[:, 2, t * P:(t + 1) * P],
                                                   ident[0:8, 0:8])
                elif kind == "logit":
                    t = u[1]
                    pe.wait_ge(*evicted(("hT", 2, t, 1)))
                    for k in range(KD):
                        last = nc.tensor.matmul(b[:, 0:20], hT[:, k, t * P:(t + 1) * P], rt_w[:, k, :],
                                                start=k == 0, stop=k == KD - 1)
                elif kind == "rank":
                    pe.wait_ge(sel_ready, 1)
                    before = cs("before")
                    sel = rt[:, 0:32]
                    nc.tensor.matmul(b[:, 0:16], before, sel[:, 0:16], start=True, stop=True)
                    nc.tensor.matmul(b[:, 16:32], ones[:, 0:P], sel[:, 0:16], start=True, stop=False)
                    nc.tensor.matmul(b[:, 16:32], before, sel[:, 16:32], start=False, stop=True)
                    nc.tensor.matmul(b[:, 32:48], ones[:, 0:P], sel[:, 0:16], start=True, stop=False)
                    last = nc.tensor.matmul(b[:, 32:48], ones[:, 0:P], sel[:, 16:32], start=False, stop=True)
                last.then_inc(unit_done, 1)

            def operands(h):
                if h < 8:
                    lo = HD * (h % 2)
                    return qm[lo:lo + HD, h // 2], km[lo:lo + HD, h // 2], [vm[:, t, h * HD:(h + 1) * HD] for t in range(TT)]
                if h < 16:
                    g = (h - 8) // 4
                    lo = HD * g
                    return (qs[lo:lo + HD, (h - 8) % 4], kvs[lo:lo + HD, 0:T],
                            [kvs[:, T + t * P + g * HD:T + t * P + (g + 1) * HD] for t in range(TT)])
                i = h % 8
                lo = HD * (i % 2)
                q, k, v = (qm, km, vm) if h < 24 else (qs, kb2, vb2)
                return q[lo:lo + HD, i // 2], k[lo:lo + HD, i // 2], [v[:, t, i * HD:(i + 1) * HD] for t in range(TT)]

            def wait_operands(h):
                if h in (0, 8, 16, 24):
                    for u in ((("fm", "cq", 1), ("fm", "ck", 1)), (("fm", "bq", 1), ("bkv",)),
                              (("fm", "qa", 1), ("fm", "ka", 1), ("FT",)), (("fm", "qb", 1), ("fm", "kb", 1)))[h // 8]:
                        pe.wait_ge(*evicted(u))

            def scores(h):
                wait_operands(h)
                if h >= 2:
                    pe.wait_ge(scores_masked, h - 1)
                b = score_bank[h % 2]
                q, k, _ = operands(h)
                if h < 24:
                    fox_head = 16 <= h
                    for t, (lo, n) in enumerate(((0, P), (P, T))):
                        last = nc.tensor.matmul(b[:, lo:lo + n], q[:, t * P:(t + 1) * P], k[:, 0:n],
                                                start=True, stop=not fox_head)
                        if fox_head:
                            row = fox_neg_ident[:, h - 16:h - 15].to_broadcast([8, P])
                            last = nc.tensor.matmul(b[:, lo:lo + n], row, fox[:, 2, 0:n], start=False, stop=True)
                else:
                    nc.tensor.matmul(b[:, 0:T], k[:, 0:P], q[:, 0:T], start=True, stop=True)
                    last = nc.tensor.matmul(b[:, T:T + P], k[:, P:T], q[:, P:T], start=True, stop=True)
                last.then_inc(scores_done, 1)

            def turn(h):
                b = trans_bank[h % 2]
                if h >= 2:
                    pe.wait_ge(pt_evicted, h - 1)
                pe.wait_ge(probs_ready, h + 1)
                if h < 24:
                    for j in range(3):
                        last = nc.tensor.transpose(b[:, j * P:(j + 1) * P], score[:, h % 2, j * P:(j + 1) * P], ident)
                else:
                    nc.tensor.matmul(b[:, 0:384], cs("suffix"), soft[:, h % 2, :], start=True, stop=False,
                                     skip_group_check=True)
                    last = nc.tensor.matmul(b[:, P:T], ones[:, 0:P], soft[:, h % 2, T:T + P], start=False, stop=True,
                                            skip_group_check=True)
                last.then_inc(pt_done, 1)

            def values(h):
                if h in (0, 8, 16, 24):
                    pe.wait_ge(*evicted((("tm", "cv", 1), ("bkv",), ("tm", "va", 1), ("tm", "vb", 1))[h // 8]))
                if h % 2 == 0 and h >= 2:
                    pe.wait_ge(o_evicted, h // 2)
                pe.wait_ge(pt_evicted, h + 1)
                _, _, v = operands(h)
                o = o_bank[HD * (h % 2):HD * (h % 2) + HD, :]
                nc.tensor.matmul(o[:, 0:T], v[0], probT[:, h % 2, 0:T], start=True, stop=False,
                                 skip_group_check=True)
                nc.tensor.matmul(o[:, P:T], v[1], probT[:, h % 2, T:T + P], start=False, stop=True,
                                 skip_group_check=True).then_inc(o_done, 1)

            def residual(n):
                t, half = n // 2, n % 2
                nc.tensor.matmul(out_bank[n], ident, x_res[:, t, half * W512:(half + 1) * W512], start=True, stop=True,
                                 skip_group_check=True)

            rank_bank = (len(UNITS) - 1) % 3
            n = 0
            for s in STEPS:
                if s == ("unit", "rank"):
                    pe.wait_ge(o_evicted, 16)
                    pe.wait_ge(act_evicted, evict_count([u for u in UNITS if evictor(u) == "act"][-1]))
                    pe.wait_ge(*evicted(("logit", 1)))
                    for i in range(4):
                        if i != rank_bank:
                            residual(i)
                if s[0] == "unit":
                    unit(n, s[1:])
                    n += 1
                elif s[0] == "S":
                    scores(s[1])
                elif s[0] == "T":
                    turn(s[1])
                elif s[0] == "V":
                    values(s[1])

            def scatter(t):
                for half in range(2):
                    last = nc.tensor.matmul(out_bank[2 * t + half], combT[:, t * P:(t + 1) * P],
                                            y_pair[:, half * W512:(half + 1) * W512], start=False, stop=True,
                                            skip_group_check=True)
                return last

            def gather(it):
                pe.wait_ge(onehot_ready, it + 1)
                for k in range(KD):
                    for t in range(TT):
                        last = nc.tensor.matmul(x_bank[k // 4][:, (k % 4) * P:(k % 4 + 1) * P],
                                                xn[:, t, k * P:(k + 1) * P],
                                                onehot[:, t].rearrange("p e s -> p (e s)"),
                                                start=t == 0, stop=t == TT - 1)
                last.then_inc(gather_done, 1)

            pe.wait_ge(*evicted(("rank",)))
            residual(rank_bank)
            gather(0)
            pe.wait_ge(rounds_ready, 1)
            rounds = pe.value_load(n_rounds[0:1, 0:1], min_val=1, max_val=T // SLOTS)
            with pe.Fori(0, rounds) as r:
                with pe.Fori(0, PAIRS) as pair:
                    it = r * PAIRS + pair

                    def gate_up(e):
                        pair_loaded(pe, 2 * e, it)
                        pair_loaded(pe, 2 * e + 1, it)
                        for k in range(KD):
                            for half in range(2):
                                last = nc.tensor.matmul(gu_bank[e][HD * half:HD * half + HD, :],
                                                        xg[:, k, e * SLOTS:(e + 1) * SLOTS],
                                                        pair_chunk(2 * e + half)[:, k, :],
                                                        start=k == 0, stop=k == KD - 1, skip_group_check=True)
                        last.then_inc(gu_done, 1)

                    pe.wait_ge(xg_act, it + 1)
                    pe.wait_ge(xg_dve, it + 1)
                    pe.wait_ge(y_ready, it * 2 + 1)
                    gate_up(0)
                    gather(it + 1)
                    pe.wait_ge(y_ready, it * 2 + 2)
                    gate_up(1)
                    pe.wait_ge(combT_evicted, it + 1)
                    scatter(0)
                    scatter(1).then_inc(scatter_done, 1)
                    pe.wait_ge(act_ready, it * 2 + 1)
                    pe.wait_ge(combine_ready, it + 1)
                    for t in range(TT):
                        last = nc.tensor.transpose(gu_bank[0][:, t * P:(t + 1) * P],
                                                   combine[:, t].rearrange("p e s -> p (e s)"), ident)
                    last.then_inc(combT_done, 1)
                    pe.wait_ge(act_ready, it * 2 + 2)
                    for k in range(4):
                        last = nc.tensor.transpose(gu_bank[1][:, k * P:(k + 1) * P], act[:, k * P:(k + 1) * P], ident)
                    last.then_inc(actT_done, 1)
                    pe.wait_ge(combT_evicted, it + 2)
                    pe.wait_ge(actT_evicted, it + 1)
                    for e in range(2):
                        pair_loaded(pe, 4 + e, it)
                        for k in range(4):
                            for half in range(2):
                                last = nc.tensor.matmul(gu_bank[e][HD * half:HD * half + HD, :],
                                                        actT[:, k, e * SLOTS:(e + 1) * SLOTS],
                                                        pair_chunk(4 + e)[:, k, half * W512:(half + 1) * W512],
                                                        start=k == 0, stop=k == 3, skip_group_check=True)
                        last.then_inc(down_done, 1)
            pe.wait_ge(y_ready, rounds * (2 * PAIRS) + 2)
            for t in range(TT):
                scatter(t).then_inc(tile_done, 1)

        @block.scalar
        def _(act_e):
            links = [0]

            def link(ins):
                links[0] += 1
                ins.then_inc(act_chain, 1)
                act_e.wait_ge(act_chain, links[0])

            def load_rest():
                act_e.dma_start(con[:, P:N_CON], a["con"][:, P:N_CON]).then_inc(con_loaded, 16)
                with nc.allow_non_contiguous_dma(reason="few bytes"):
                    act_e.dma_start(pw[:, :, :], a["pool_w"][0].rearrange("g c d -> c g d")).then_inc(small_loaded, 16)
                    act_e.dma_start(fa_w[:, :, :], k_rows(w_in2, slice(IN2["fa"], IN2["fa"] + 8))).then_inc(small_loaded, 16)
                    act_e.dma_start(rt_w[:, :, :], a["router_w"].rearrange("(k p) n -> p k n", p=P)).then_inc(small_loaded, 16)
                act_e.dma_start(gate_rows[:, :, :], a["gate_b"]).then_inc(gate_rows_loaded, 16)

            act_e.dma_start(vec[:, :], a["vec"]).then_inc(vec_loaded, 16)
            act_e.dma_start(con[:, 0:P], a["con"][:, 0:P]).then_inc(ident_loaded, 16)
            nc.scalar.preload_act_table_set(LN_EXP)
            act_e.wait_ge(vec_loaded, 16)
            nc.scalar.activation(c_tmp[:, 0, :], vec[:, VEC["c"]], ACT.Exp, scale=-1.0).then_inc(c_exp, 1)

            def norm(n, t):
                i = NORMS.index((n, t))
                if t == 0 and n in (1, 3, 4):
                    nc.scalar.preload_act_table_set(LN_EXP)
                if n == 0:
                    act_e.wait_ge(x_loaded[t], 16)
                elif n in (1, 3):
                    act_e.wait_ge(*evicted(("wout", 1 if n == 1 else 2, t, 1)))
                elif n == 2:
                    act_e.wait_ge(x1_ready, t + 1)
                else:
                    act_e.wait_ge(tile_done, t + 1)
                s = stat[:, i, :]
                x = x_res[:, t, :] if n < 4 else psum[:, 2 * t:2 * t + 2, :].rearrange("p h n -> p (h n)")
                nc.scalar.activation(junk, x, ACT.Square, accum_out=s[:, 0:1]).then_inc(sumsq_ready, 1)
                act_e.wait_ge(sumsq_ready, i + 1)
                link(nc.scalar.activation(s[:, 2:3], s[:, 0:1], ACT.Ln, scale=1.0 / D, bias=vec[:, VEC["eps"]]))
                nc.scalar.activation(s[:, 3:4], s[:, 2:3], ACT.Exp, scale=-0.5).then_inc(guess_ready, 1)

            def unit(n, u):
                b = unit_bank[n % 3]
                kind = u[0]
                if evictor(u) == "dve":
                    if kind == "fm":
                        i = SILU_UNITS.index(u)
                        if i >= 2:
                            act_e.wait_ge(*evicted(SILU_UNITS[i - 2]))
                        act_e.wait_ge(unit_done, n + 1)
                        nc.scalar.activation(sig[:, i % 2, :], b, ACT.Sigmoid).then_inc(sig_ready, 1)
                    if u in HI_UNITS:
                        t, half = u[2:]
                        act_e.wait_ge(unit_done, n + 1)
                        if kind == "hT" and u[1] == 1:
                            act_e.wait_ge(mods_ready, 1)
                        for k in range(4):
                            f, src = 4 * half + k, b[:, k * P:(k + 1) * P]
                            if kind == "mT":
                                if k == 0:
                                    last = nc.scalar.activation(as_rounded(merged_hi[:, f:f + 4, t * P:(t + 1) * P]),
                                                                b.rearrange("p (k t) -> p k t", k=4), ACT.Copy)
                            elif u[1] == 0:
                                last = nc.scalar.activation(as_rounded(hT[:, f, t * P:(t + 1) * P]), src, ACT.Identity,
                                                            scale=vec[:, VEC["norm_g"]][:, f:f + 1])
                            else:
                                last = nc.scalar.activation(as_rounded(hT[:, f, t * P:(t + 1) * P]), src, ACT.Identity,
                                                            scale=aff[:, 0, f:f + 1], bias=mod[:, f // 4, f % 4:f % 4 + 1])
                        last.then_inc(hi_ready, 1)
                    return
                act_e.wait_ge(unit_done, n + 1)
                if kind == "fm":
                    dst = dict(cq=qm, ck=km, bq=qs, ax=pool_x, qa=qm, ka=km, qb=qs, kb=kb2)[u[1]]
                    scale = HD ** -0.5 if u[1] in ("cq", "bq", "qa", "qb") else 1.0
                    last = nc.scalar.activation(dst[:, 2 * u[2]:2 * u[2] + 2, :].rearrange("p n t -> p (n t)"), b,
                                                ACT.Copy, scale=scale)
                elif kind == "tm":
                    if u[1][0] in "gh":
                        i = int(u[1][1])
                        dst = gate_tm[:, i // 2, u[2], (i % 2) * W512:(i % 2 + 1) * W512]
                    else:
                        dst = dict(cv=vm, va=vm, vb=vb2)[u[1]][:, u[2], :]
                    last = nc.scalar.activation(dst, b, ACT.Copy)
                elif kind == "bkv":
                    last = nc.scalar.activation(kvs, b[:, :], ACT.Copy)
                elif kind == "fa":
                    last = nc.scalar.activation(fox[:, 0, :], b[0:8, 0:T], ACT.Identity,
                                                bias=vec[0:8, VEC["b_forget"]])
                elif kind == "FT":
                    last = nc.scalar.activation(foxT[:, :, :].rearrange("p t h -> p (t h)"), b[:, 0:16], ACT.Copy)
                last.then_inc(act_evicted, 1)

            def probs(h):
                s = score[:, h % 2, :]
                if h < 24:
                    st = hstat[:, h % 2, :]
                    act_e.wait_ge(max_ready, h + 1)
                    if 8 <= h < 16:
                        nc.scalar.activation(st[:, 4:6], st[:, 0:2], ACT.Exp, bias=vec[:, VEC["sink"]][:, h - 8:h - 7])
                    nc.scalar.activation(s[:, 0:P], s[:, 0:P], ACT.Exp, bias=st[:, 0:1], accum_out=st[:, 2:3])
                    nc.scalar.activation(s[:, P:384], s[:, P:384], ACT.Exp, bias=st[:, 1:2], accum_out=st[:, 3:4])\
                      .then_inc(exp_done, 1)
                else:
                    z = soft[:, h % 2, :]
                    act_e.wait_ge(scores_masked, h + 1)
                    if h >= 26:
                        act_e.wait_ge(pt_done, h - 1)
                    else:
                        act_e.wait_ge(unit_done, UNITS.index(("proj", "a", 1, 1)) + 1)
                    link(nc.scalar.activation(z, s, ACT.Abs))
                    link(nc.scalar.activation(z, z, ACT.Exp, scale=-1.0))
                    nc.scalar.activation(z, z, ACT.Ln, bias=1.0).then_inc(exp_done, 1)

            def turned(h):
                act_e.wait_ge(pt_done, h + 1)
                if h >= 2:
                    act_e.wait_ge(o_done, h - 1)
                if h < 24:
                    nc.scalar.activation(probT[:, h % 2, :], trans_bank[h % 2][:, 0:384], ACT.Copy)\
                      .then_inc(pt_evicted, 1)
                else:
                    act_e.wait_ge(stick_ready, h - 23)
                    nc.scalar.activation(probT[:, h % 2, :], score[:, h % 2, :], ACT.Exp).then_inc(pt_evicted, 1)

            def sigmoid(first_tile):
                block = 2 if first_tile < 16 and gates_made[0] >= 3 else 1
                units = [u for u in UNITS if u[0] == "tm" and u[1] in [f"{'gh'[block - 1]}{first_tile // 4 + i}" for i in range(2)]]
                act_e.wait_ge(act_evicted, max(map(evict_count, units)))
                g = gates[:, first_tile:first_tile + 8, :].rearrange("p n t -> p (n t)")
                nc.scalar.activation(g, g, ACT.Sigmoid).then_inc(gates_ready, 1)
                gates_made[0] += 1
                if block == 2:
                    nc.scalar.preload_act_table_set(LN_EXP)

            gates_made = [0]

            def split(c, q):
                m, src = SPLITS.index(c), wait_chunk(act_e, c)
                if m >= 2 and q == PIECES[0]:
                    act_e.wait_ge(unit_done, last_reader(SPLITS[m - 2])[1])
                piece = piece_of(c, q)
                nc.scalar.activation(as_rounded(high(c)[:, piece]), src[:, piece], ACT.Copy).then_inc(chunk_hi, 1)

            def y_split(br):
                if br == "a":
                    act_e.wait_ge(*evicted(("mix", 1)))
                act_e.wait_ge(o_evicted, dict(a=4, c=4, b=8, f=12, s=16)[br])
                nc.scalar.activation(as_rounded(y_high[br]), y_low[br], ACT.Copy).then_inc(y_hi, 1)

            def load_final_g(i):
                if i == 0:
                    act_e.wait_ge(*evicted(SILU_UNITS[-1]))
                    act_e.dma_start(fin_g, a["fin1"]).then_inc(fin1_loaded, 16)
                else:
                    act_e.wait_ge(scores_done, 24)
                    act_e.wait_ge(scores_masked, 24)
                    act_e.dma_start(fin_g, a["fin2"]).then_inc(fin2_loaded, 16)

            def fa_split():
                act_e.wait_ge(small_loaded, 16 * 3)
                nc.scalar.activation(as_rounded(fa_hi[:, :, :]), fa_w[:, :, :], ACT.Copy).then_inc(fa_hi_ready, 1)

            def logf():
                act_e.wait_ge(act_evicted, evict_count(("fa",)))
                link(nc.scalar.activation(fox[:, 1, :], fox[:, 0, :], ACT.Abs))
                link(nc.scalar.activation(fox[:, 2, :], fox[:, 1, :], ACT.Exp, scale=-1.0))
                nc.scalar.activation(fox[:, 1, :], fox[:, 2, :], ACT.Ln, bias=1.0).then_inc(fox_log, 1)

            n = 0
            for s in STEPS:
                if s[0] == "unit":
                    unit(n, s[1:])
                    n += 1
                elif s[0] == "norm":
                    norm(s[1], s[2])
                    if s[1:] == (0, 1):
                        load_rest()
                elif s[0] in ("sigmoid", "split", "y_split", "fa_split", "load_final_g"):
                    dict(load_final_g=load_final_g, sigmoid=sigmoid, split=split, y_split=y_split, fa_split=fa_split)[s[0]](*s[1:])
                elif s[0] == "S":
                    probs(s[1])
                elif s[0] == "T":
                    turned(s[1])
                elif s[0] == "logf":
                    logf()
                elif s[0] == "route":
                    act_e.wait_ge(group_shifted, 1)
                    nc.scalar.activation(rt[:, 100:108], rt[:, 100:108], ACT.Exp)
                    nc.scalar.activation(rt[:, 110:142], rt[:, 110:142], ACT.Exp).then_inc(group_exp, 1)
            def xg_half(it):
                act_e.wait_ge(gather_done, it + 1)
                for k in range(4):
                    last = nc.scalar.activation(xg[:, k, :], x_bank[0][:, k * P:(k + 1) * P], ACT.Identity,
                                                scale=aff[:, 1, k:k + 1],
                                                bias=mod[:, 6:8, :].rearrange("p c j -> p (c j)")[:, k:k + 1])
                last.then_inc(xg_act, 1)

            xg_half(0)
            nc.scalar.preload_act_table_set(SILU_SET)
            act_e.wait_ge(rounds_ready, 1)
            rounds = act_e.value_load(n_rounds[0:1, 0:1], min_val=1, max_val=T // SLOTS)
            with act_e.Fori(0, rounds) as r:
                with act_e.Fori(0, PAIRS) as pair:
                    it = r * PAIRS + pair
                    for e in range(2):
                        act_e.wait_ge(gu_done, it * 2 + e + 1)
                        nc.scalar.activation(sil[HD:P, e, :], gu_bank[e][0:HD, :], ACT.Silu).then_inc(silu_done, 1)
                    act_e.wait_ge(actT_done, it + 1)
                    nc.scalar.activation(actT.rearrange("p k s -> p (k s)"), gu_bank[1], ACT.Copy)\
                      .then_inc(actT_evicted, 1)
                    xg_half(it + 1)
            for t in range(TT):
                norm(4, t)

        @block.gpsimd
        def _(pool_e):
            for s in STEPS:
                if s[0] == "split" and s[2] >= POOL_FROM:
                    _, c, q = s
                    pool_e.wait_ge(chunk_hi, SPLIT * SPLITS.index(c) + PIECES.index(q) + 1)
                    w, piece = ring[CHUNKS.index(c) % RING][:, :], piece_of(c, q)
                    nc.gpsimd.tensor_tensor(as_rounded(w[:, piece]), w[:, piece], was_rounded(high(c)[:, piece]), ALU.subtract)\
                      .then_inc(chunk_split_pool, 1)

        @block.vector
        def _(dve):
            v = nc.vector
            links = [0]

            def link(ins):
                links[0] += 1
                ins.then_inc(dve_chain, 1)
                dve.wait_ge(dve_chain, links[0])

            dve.wait_ge(c_exp, 1)
            link(v.tensor_scalar(c_tmp[:, 1, :], c_tmp[:, 0, :], 1.0, None, ALU.add))
            link(v.reciprocal(c_tmp[:, 0, :], c_tmp[:, 1, :]))
            link(v.tensor_tensor(c_act[:, :], c_tmp[:, 0, :], vec[:, VEC["c"]], ALU.mult))
            dve.wait_ge(ident_loaded, 16)
            v.tensor_scalar(fox_neg_ident[:, :], ident[0:8, 0:8], -1.0, None, ALU.mult)
            norms_on_xn = [0]

            def norm(n, t):
                i = NORMS.index((n, t))
                s = stat[:, i, :]
                dve.wait_ge(sumsq_ready, i + 1)
                v.tensor_scalar(s[:, 1:2], s[:, 0:1], 1.0 / D, EPS, ALU.mult, ALU.add).then_inc(ms_ready, 1)
                dve.wait_ge(guess_ready, i + 1)
                y = s[:, 3:4]
                dve.wait_ge(ms_ready, i + 1)
                link(v.tensor_scalar(s[:, 4:5], y, y, s[:, 1:2], ALU.mult, ALU.mult))
                link(v.tensor_scalar(s[:, 5:6], s[:, 4:5], -0.5, 1.5, ALU.mult, ALU.add))
                link(v.tensor_tensor(s[:, 7:8], y, s[:, 5:6], ALU.mult))
                rstd = s[:, 7:8]
                if n in (1, 4):
                    dve.wait_ge(fin1_loaded if n == 1 else fin2_loaded, 16)
                    x = x_res[:, t, :] if n == 1 else psum[:, 2 * t:2 * t + 2, :].rearrange("p h n -> p (h n)")
                    v.scalar_tensor_tensor(x_res[:, t, :], x, rstd, fin_g, ALU.mult, ALU.mult)\
                     .then_inc(x1_ready if n == 1 else out_ready, 1)
                else:
                    if n == 2:
                        dve.wait_ge(x1_ready, t + 1)
                    v.tensor_scalar(xn[:, t, :], x_res[:, t, :], rstd, None, ALU.mult).then_inc(xn_ready, 1)

            def unit(n, u):
                if evictor(u) != "dve":
                    return
                b = unit_bank[n % 3]
                kind = u[0]
                flat = lambda ap: ap.rearrange("p n t -> p (n t)")
                if kind == "fm":
                    i = SILU_UNITS.index(u)
                    dve.wait_ge(sig_ready, i + 1)
                    z = mixed[:, "cba".index(u[1][0]), 2 * u[2]:2 * u[2] + 2, :]
                    v.tensor_tensor(flat(z), b, sig[:, i % 2, :], ALU.mult).then_inc(dve_evicted, 1)
                    return
                dve.wait_ge(unit_done, n + 1)
                if u in HI_UNITS:
                    dve.wait_ge(hi_ready, HI_UNITS.index(u) + 1)
                if kind == "hT":
                    _, norm_i, t, half = u
                    if norm_i == 1 and (t, half) == (0, 0):
                        dve.wait_ge(mods_ready, 1)
                    if norm_i == 2 and (t, half) == (0, 0):
                        dve.wait_ge(mods_ready, 2)
                    for k in range(4):
                        f = 4 * half + k
                        dst, src = hT[:, f, t * P:(t + 1) * P], b[:, k * P:(k + 1) * P]
                        if norm_i < 2:
                            dst = hT_lo[:, f, t * P:(t + 1) * P]
                        if norm_i == 0:
                            last = v.scalar_tensor_tensor(as_rounded(dst), src, vec[:, VEC["norm_g"]][:, f:f + 1],
                                                          was_rounded(hT[:, f, t * P:(t + 1) * P]), ALU.mult, ALU.subtract)
                        else:
                            shift = mod[:, (0 if norm_i == 1 else 6) + f // 4, f % 4:f % 4 + 1]
                            last = v.tensor_scalar(dst, src, aff[:, norm_i - 1, f:f + 1], shift, ALU.mult, ALU.add)
                    if norm_i == 1:
                        link(last)
                        rows = slice(4 * half, 4 * half + 4), slice(t * P, (t + 1) * P)
                        last = v.tensor_tensor(as_rounded(hT_lo[:, rows[0], rows[1]]), hT_lo[:, rows[0], rows[1]],
                                               was_rounded(hT[:, rows[0], rows[1]]), ALU.subtract)
                elif kind == "mT":
                    _, blk, t, half = u
                    last = v.tensor_tensor(as_rounded(merged_lo(blk, half)[:, :, t * P:(t + 1) * P]),
                                           b.rearrange("p (k t) -> p k t", k=4),
                                           was_rounded(merged_hi[:, 4 * half:4 * half + 4, t * P:(t + 1) * P]),
                                           ALU.subtract)
                elif kind == "mix":
                    dve.wait_ge(*evicted(("fm", "az", 1)))
                    for j in range(2):
                        g = 2 * u[1] + j
                        y = mixed[:, 2, g, :]
                        last = v.scalar_tensor_tensor(y, b[:, j * T:(j + 1) * T], vec[:, VEC["pool_scale"]][:, g:g + 1],
                                                      y, ALU.mult, ALU.mult)
                elif kind == "mod":
                    c = u[1]
                    if c // 2 in (2, 5):
                        dve.wait_ge(gate_rows_loaded, 16)
                        row = gate_rows[:, c // 2 == 5, (c % 2) * W512:(c % 2 + 1) * W512]
                        last = v.tensor_tensor(row, b[:, :], row, ALU.add)
                    else:
                        bias = vec[:, VEC["ada_b"]][:, 4 * c:4 * c + 4]
                        last = v.tensor_tensor(mod[:, c, :], b[:, 0:4], bias, ALU.add)
                elif kind == "proj":
                    _, br, t, half = u
                    place = dict(c=2, b=1, a=0, f=0, s=1)
                    at = lambda br: gate_tm[:, place[br], t, half * W512:(half + 1) * W512]
                    dve.wait_ge(gates_ready, sigmoids(8 * place[br], 1 if br in "abc" else 2))
                    last = v.tensor_tensor(at(br), b, at(br), ALU.mult)
                    if br not in "cf":
                        link(last)
                        dst, one, two = dict(b="bbc", a="aab", s="ffs")[br]
                        last = v.tensor_tensor(at(dst), at(one), at(two), ALU.add)
                elif kind == "wout":
                    _, blk, t, half = u
                    x = x_res[:, t, half * W512:(half + 1) * W512]
                    if blk == 1:
                        last = v.tensor_tensor(x, b[:, :], x, ALU.add)
                    else:
                        dve.wait_ge(dve_evicted, evict_count(u) - 1)
                        link(v.tensor_tensor(tmp, b[:, :], gate_rows[:, 0, half * W512:(half + 1) * W512], ALU.mult))
                        last = v.tensor_tensor(x, x, tmp, ALU.add)
                elif kind == "logit":
                    t = u[1]
                    rb = vec[:, VEC["router_b"]]
                    if t == 0:
                        dve.wait_ge(o_done, 32)
                    v.tensor_tensor(rt[:, 32 + 4 * t:36 + 4 * t], b[:, 0:4], rb[:, 0:4], ALU.add)
                    last = v.tensor_tensor(rt[:, 40 + 16 * t:56 + 16 * t], b[:, 4:20], rb[:, 4:20], ALU.add)
                elif kind == "rank":
                    pos = rt[:, 300:336].rearrange("p (t e) -> p t e", t=TT)
                    sel = rt[:, 0:32].rearrange("p (t e) -> p t e", t=TT)
                    link(v.scalar_tensor_tensor(pos[:, :, 0:16], b[:, 0:32].rearrange("p (t e) -> p t e", t=TT), 1.0,
                                                sel, ALU.add, ALU.mult))
                    link(v.tensor_scalar(pos[:, :, 0:16], pos[:, :, 0:16], -1.0, None, ALU.add))
                    v.tensor_scalar(pos[:, :, 16:18], pos[:, :, 0:2], -float(SLOTS), None, ALU.add)
                    last = v.tensor_reduce(rt[:, 340:341], b[:, 32:48], X, ALU.max)
                last.then_inc(dve_evicted, 1)

            def pool():
                dve.wait_ge(*evicted(("fm", "ax", 1)))
                src = pool_x
                for i, w in enumerate(WINDOWS):
                    dst, h = (pool_a, pool_b)[i % 2], w // 2
                    v.tensor_copy(dst[:, i:4, 0:h], src[:, i:4, 0:h])
                    link(v.tensor_tensor(dst[:, i:4, h:T], src[:, i:4, h:T], src[:, i:4, 0:T - h], ALU.add))
                    src = dst
                inv = cs("inv_count").rearrange("p (g t) -> p g t", g=4)
                for g, w in enumerate(WINDOWS):
                    s = (pool_a, pool_b)[g % 2][:, g, :]
                    link(v.tensor_tensor(s[:, 0:16], s[:, 0:16], inv[:, g, :], ALU.mult))
                    v.tensor_tensor(pool_a[:, g, 0:16], s[:, 0:16], pool_x[:, g, 0:16], ALU.subtract)
                    last = v.scalar_tensor_tensor(pool_a[:, g, 16:T], s[:, 16:T], 1.0 / w, pool_x[:, g, 16:T],
                                                  ALU.mult, ALU.subtract)
                last.then_inc(pooled_ready, 1)

            def ada(c, half):
                w = wait_chunk(dve, ("ada", c)).rearrange("p (k n) -> p k n", n=W512)
                if c and not half:
                    dve.wait_ge(unit_done, UNITS.index(("mod", c - 1)) + 1)
                for k in range(4 * half, 4 * half + 4):
                    if k == 0:
                        ins = v.tensor_scalar(ada_acc[:, :], w[:, 0, :], c_act[:, 0:1], None, ALU.mult)
                    else:
                        ins = v.scalar_tensor_tensor(ada_acc[:, :], w[:, k, :], c_act[:, k:k + 1], ada_acc[:, :],
                                                     ALU.mult, ALU.add)
                    if k < KD - 1:
                        link(ins)
                    else:
                        ins.then_inc(ada_done, 1)

            def split(c, q):
                if q < POOL_FROM:
                    dve.wait_ge(chunk_hi, SPLIT * SPLITS.index(c) + PIECES.index(q) + 1)
                    w, piece = ring[CHUNKS.index(c) % RING][:, :], piece_of(c, q)
                    v.tensor_tensor(as_rounded(w[:, piece]), w[:, piece], was_rounded(high(c)[:, piece]), ALU.subtract)\
                     .then_inc(chunk_split, 1)

            def y_split(br):
                dve.wait_ge(y_hi, Y_SPLITS.index(br) + 1)
                v.tensor_tensor(as_rounded(y_low[br]), y_low[br], was_rounded(y_high[br]), ALU.subtract).then_inc(y_split_done, 1)

            def fa_split():
                dve.wait_ge(fa_hi_ready, 1)
                v.tensor_tensor(as_rounded(fa_w[:, :, :]), fa_w[:, :, :], was_rounded(fa_hi[:, :, :]), ALU.subtract).then_inc(fa_split_done, 1)

            def mods(i):
                c = (2, 8)[i]
                dve.wait_ge(*evicted(("mod", c + 1)))
                g = vec[:, VEC["norm1_g" if i == 0 else "norm2_g"]]
                v.scalar_tensor_tensor(aff[:, i, :], mod[:, c:c + 2, :].rearrange("p c j -> p (c j)"), 1.0, g,
                                       ALU.add, ALU.mult).then_inc(mods_ready, 1)

            def probs(h):
                s = score[:, h % 2, :]
                st = hstat[:, h % 2, :]
                b = score_bank[h % 2]
                dve.wait_ge(scores_done, h + 1)
                if h == 0:
                    dve.wait_ge(con_loaded, 16)
                if h >= 2:
                    if h - 2 < 24:
                        dve.wait_ge(pt_done, h - 1)
                    else:
                        dve.wait_ge(pt_evicted, h - 1)
                mask = cs("mask_causal" if h < 8 or 16 <= h < 24 else "mask_swa" if h < 16 else "mask_strict")
                if 16 <= h < 24:
                    v.scalar_tensor_tensor(s[:, 0:P], b[:, 0:P], foxT[:, 0, h - 16:h - 15], mask[:, 0:P], ALU.add, ALU.add)
                    v.scalar_tensor_tensor(s[:, P:384], b[:, P:384], foxT[:, 1, h - 16:h - 15], mask[:, P:384], ALU.add, ALU.add)\
                     .then_inc(scores_masked, 1)
                else:
                    v.tensor_tensor(s, b[:, 0:384], mask, ALU.add).then_inc(scores_masked, 1)
                dve.wait_ge(scores_masked, h + 1)
                if h < 24:
                    ins = v.tensor_reduce(st[:, 0:1], s[:, 0:P], X, ALU.max, negate=True)
                    ins = v.tensor_reduce(st[:, 1:2], s[:, P:384], X, ALU.max, negate=True)
                    if 8 <= h < 16:
                        link(ins)
                        link(v.tensor_scalar(st[:, 8:9], vec[:, VEC["sink"]][:, h - 8:h - 7], -1.0, None, ALU.mult))
                        ins = v.tensor_scalar(st[:, 0:2], st[:, 0:2], st[:, 8:9], None, ALU.min)
                    ins.then_inc(max_ready, 1)
                    dve.wait_ge(exp_done, h + 1)
                    if 8 <= h < 16:
                        link(v.tensor_tensor(st[:, 2:4], st[:, 2:4], st[:, 4:6], ALU.add))
                    link(v.reciprocal(st[:, 6:8], st[:, 2:4]))
                    v.tensor_scalar(s[:, 0:P], s[:, 0:P], st[:, 6:7], None, ALU.mult)
                    v.tensor_scalar(s[:, P:384], s[:, P:384], st[:, 7:8], None, ALU.mult).then_inc(probs_ready, 1)
                else:
                    dve.wait_ge(exp_done, h + 1)
                    z = soft[:, h % 2, :]
                    v.scalar_tensor_tensor(z, s, 0.0, z, ALU.max, ALU.add).then_inc(probs_ready, 1)

            def turned(h):
                if h >= 24:
                    dve.wait_ge(pt_done, h + 1)
                    s = score[:, h % 2, :]
                    v.tensor_tensor(s, s, trans_bank[h % 2][:, 0:384], ALU.subtract).then_inc(stick_ready, 1)

            def outputs(h):
                if h % 2 == 0:
                    return
                dve.wait_ge(o_done, h + 1)
                mixer = (0, 1, 0, 1)[h // 8]
                y = mixed[:, mixer, (h % 8) // 2, :]
                if h < 16:
                    if h in (1, 9):
                        dve.wait_ge(*evicted(("fm", "cz" if h == 1 else "bz", 1)))
                    v.tensor_tensor(y, o_bank[:, 0:T], y, ALU.mult).then_inc(o_evicted, 1)
                else:
                    v.tensor_copy(y, o_bank[:, 0:T]).then_inc(o_evicted, 1)

            def logf():
                dve.wait_ge(fox_log, 1)
                link(v.scalar_tensor_tensor(fox[:, 3, :], fox[:, 0, :], 0.0, fox[:, 1, :], ALU.min, ALU.subtract))
                v.tensor_tensor_scan(fox[:, 2, :], ones[0:8, 0:T], fox[:, 3, :], 0.0, ALU.mult, ALU.add)\
                 .then_inc(fox_ready, 1)

            def ranks(dst, logits, n, scratch):
                other = logits.unsqueeze(2).to_broadcast([P, n, 4, 4])
                own = logits.unsqueeze(3).to_broadcast([P, n, 4, 4])
                more = rt[:, scratch:scratch + 16 * n].rearrange("p (n i j) -> p n i j", n=n, i=4)
                same = rt[:, scratch + 128:scratch + 128 + 16 * n].rearrange("p (n i j) -> p n i j", n=n, i=4)
                tie = cs("tie").rearrange("p (i j) -> p i j", i=4).unsqueeze(1).to_broadcast([P, n, 4, 4])
                v.tensor_tensor(more, other, own, ALU.is_gt)
                link(v.tensor_tensor(same, other, own, ALU.is_equal))
                link(v.tensor_tensor(same, same, tie, ALU.mult))
                link(v.tensor_tensor(more, more, same, ALU.add))
                link(v.tensor_reduce(dst, more, X, ALU.add))

            def route():
                v.memset(y_pair, 0.0).then_inc(y_ready, 2)
                v.memset(combT, 0.0).then_inc(combT_evicted, 1)
                dve.wait_ge(*evicted(("logit", 1)))
                gl = rt[:, 32:40].rearrange("p (t g) -> p t g", t=TT)
                el = rt[:, 40:72].rearrange("p (n e) -> p n e", e=4)
                gd, ed = rt[:, 100:108].rearrange("p (t g) -> p t g", t=TT), rt[:, 110:142].rearrange("p (n e) -> p n e", e=4)
                gmax, emax = rt[:, 80:82], rt[:, 84:92]
                v.tensor_reduce(gmax, gl, X, ALU.max)
                link(v.tensor_reduce(emax, el, X, ALU.max))
                v.tensor_tensor(gd, gl, gmax.unsqueeze(2).to_broadcast([P, TT, 4]), ALU.subtract)
                v.tensor_tensor(ed, el, emax.unsqueeze(2).to_broadcast([P, 8, 4]), ALU.subtract).then_inc(group_shifted, 1)
                grank = rt[:, 150:158].rearrange("p (t g) -> p t g", t=TT)
                erank = rt[:, 160:192].rearrange("p (n e) -> p n e", e=4)
                ranks(grank, gl, TT, 400)
                ranks(erank, el, 8, 700)
                top = rt[:, 200:208]
                two = rt[:, 210:242].rearrange("p (n e) -> p n e", e=4)
                v.tensor_scalar(top, rt[:, 150:158], 0.5, None, ALU.is_lt)
                link(v.tensor_scalar(two, erank, 1.5, None, ALU.is_lt))
                sel = rt[:, 0:32].rearrange("p (n e) -> p n e", e=4)
                v.tensor_tensor(sel, two, top.unsqueeze(2).to_broadcast([P, 8, 4]), ALU.mult).then_inc(sel_ready, 1)
                dve.wait_ge(group_exp, 1)
                gsum, esum, f = rt[:, 250:252], rt[:, 254:262], rt[:, 264:272]
                v.tensor_reduce(gsum, gd, X, ALU.add)
                link(v.tensor_tensor(ed, ed, two, ALU.mult))
                link(v.tensor_reduce(esum, ed, X, ALU.add))
                v.reciprocal(gsum, gsum)
                link(v.reciprocal(f, esum))
                link(v.tensor_tensor(f, f, top, ALU.mult))
                link(v.tensor_tensor(f.rearrange("p (t g) -> p t g", t=TT), f.rearrange("p (t g) -> p t g", t=TT),
                                     gsum.unsqueeze(2).to_broadcast([P, TT, 4]), ALU.mult))
                comb = rt[:, 1000:1036].rearrange("p (t e) -> p t e", t=TT)
                for t in range(TT):
                    last = v.tensor_tensor(comb[:, t, 0:16].rearrange("p (g e) -> p g e", e=4), ed[:, 4 * t:4 * t + 4, :],
                                           f[:, 4 * t:4 * t + 4].unsqueeze(2).to_broadcast([P, 4, 4]), ALU.mult)
                link(last)
                link(v.tensor_copy(comb[:, :, 16:18], comb[:, :, 0:2]))

            def slots():
                dve.wait_ge(*evicted(("rank",)))
                v.tensor_tensor(onehot, iota, columns(pos, 0), ALU.is_equal).then_inc(onehot_ready, 1)
                r = rt[:, 344:348]
                for i in range(3):
                    last = v.tensor_scalar(r[:, i:i + 1], rt[:, 340:341], SLOTS * (i + 1) + 0.5, None, ALU.is_gt)
                link(last)
                link(v.tensor_reduce(r[:, 3:4], r[:, 0:3], X, ALU.add))
                v.tensor_scalar(n_rounds[:, :], r[:, 3:4], 1.0, None, ALU.add).then_inc(rounds_ready, 1)

            pos = rt[:, 300:336].rearrange("p (t e) -> p t e", t=TT)
            comb = rt[:, 1000:1036].rearrange("p (t e) -> p t e", t=TT)
            iota = cs("iota").unsqueeze(1).unsqueeze(1).to_broadcast([P, TT, 2, SLOTS])

            def columns(ap, pair):
                return ap[:, :, bass.ds(pair * 2, 2)].unsqueeze(3).to_broadcast([P, TT, 2, SLOTS])

            n = 0
            for s in STEPS:
                if s[0] == "unit":
                    unit(n, s[1:])
                    n += 1
                elif s[0] not in ("sigmoid", "load_final_g"):
                    dict(split=split, y_split=y_split, fa_split=fa_split, norm=norm, ada=ada, S=probs, T=turned, V=outputs, pool=pool, mods=mods, logf=logf,
                         route=route, slots=slots)[s[0]](*s[1:])

            def xg_half(it):
                dve.wait_ge(gather_done, it + 1)
                for k in range(4, KD):
                    last = v.tensor_scalar(xg[:, k, :], x_bank[1][:, (k - 4) * P:(k - 3) * P], aff[:, 1, k:k + 1],
                                           mod[:, 7, k - 4:k - 3], ALU.mult, ALU.add)
                last.then_inc(xg_dve, 1)

            xg_half(0)
            dve.wait_ge(rounds_ready, 1)
            rounds = dve.value_load(n_rounds[0:1, 0:1], min_val=1, max_val=T // SLOTS)
            with dve.Fori(0, rounds) as r:
                with dve.Fori(0, PAIRS) as pair:
                    it = r * PAIRS + pair
                    dve.wait_ge(onehot_ready, it + 1)
                    v.tensor_tensor(combine, onehot, columns(comb, pair), ALU.mult).then_inc(combine_ready, 1)
                    dve.wait_ge(gather_done, it + 1)
                    dve.wait_ge(combine_ready, it + 1)
                    v.tensor_tensor(onehot, iota, columns(pos, pair + 1), ALU.is_equal).then_inc(onehot_ready, 1)
                    for e in range(2):
                        dve.wait_ge(silu_done, it * 2 + e + 1)
                        v.tensor_tensor(act[e * SLOTS:(e + 1) * SLOTS, :], sil[HD:P, e, :], gu_bank[e][HD:P, :], ALU.mult)\
                         .then_inc(act_ready, 1)
                    dve.wait_ge(combT_done, it + 1)
                    dve.wait_ge(scatter_done, it + 1)
                    v.tensor_copy(combT, gu_bank[0][:, 0:T]).then_inc(combT_evicted, 1)
                    xg_half(it + 1)
                    for e in range(2):
                        dve.wait_ge(down_done, it * 2 + e + 1)
                        rows = slice(e * SLOTS, (e + 1) * SLOTS)
                        v.tensor_tensor(y_pair[rows, 0:W512], gu_bank[e][0:HD, :], gate_rows[0:HD, 1, 0:W512], ALU.mult)
                        v.tensor_tensor(y_pair[rows, W512:D], gu_bank[e][HD:P, :], gate_rows[HD:P, 1, W512:D], ALU.mult)\
                         .then_inc(y_ready, 1)
                dve.wait_ge(onehot_ready, r * PAIRS + PAIRS + 1)
                v.tensor_scalar(pos, pos, -float(SLOTS), None, ALU.add)
            for t in range(TT):
                norm(4, t)


_MATRICES = ["x", "w_in", "pool_w", "w_proj_a", "w_proj_b", "w_proj_c", "w_out", "ada_w_2", "w_in_2",
             "w_branch_fox_2", "w_branch_sb_2", "w_out_2", "expert_w_gate_2", "expert_w_up_2", "expert_w_down_2"]


def kernel(**inputs):
    import concourse.bacc as bacc
    from concourse.bass_utils import run_bass_kernel_spmd

    inp = {k: np.asarray(v) for k, v in inputs.items()}
    columns = lambda v: v.reshape(-1, P).T
    rows = lambda v: np.broadcast_to(v.reshape(1, -1), (P, v.size))
    forget = np.zeros((P, 1), np.float32)
    forget[0:8, 0] = inp["b_forget_2"][0]
    router_b = np.concatenate([inp["router_group_b_2"][0], inp["router_expert_b_2"][0]])
    vec = np.concatenate([np.full((P, 1), EPS, np.float32), columns(inp["norm_g"]), columns(inp["norm1_g_2"]), columns(inp["norm2_g_2"]),
                          columns(inp["c_2"]), columns(inp["pool_scale"]), columns(inp["ada_b_2"]), forget,
                          rows(inp["sink_logits"]), rows(router_b)], 1)
    ada_b = inp["ada_b_2"].reshape(N_MOD, D)
    arrays = {n: np.ascontiguousarray(inp[n]) for n in _MATRICES}
    arrays["con"] = constants()
    w_bq = inp["w_in"][0][:, IN1["bq"]:IN1["bq"] + W512]
    arrays["w_bq"] = np.ascontiguousarray(w_bq.reshape(D, 2, 4, HD).transpose(0, 2, 1, 3).reshape(D, W512))
    arrays["vec"] = np.ascontiguousarray(vec)
    arrays["fin1"] = np.ascontiguousarray(rows(inp["final_norm_g"]))
    arrays["fin2"] = np.ascontiguousarray(rows(inp["final_g_2"]))
    arrays["gate_b"] = np.ascontiguousarray(np.stack([rows(ada_b[2]), rows(ada_b[5])], 1))
    arrays["router_w"] = np.ascontiguousarray(np.concatenate([inp["router_group_w_2"][0], inp["router_expert_w_2"][0]], 1))

    nc = bacc.Bacc("TRN2", target_bir_lowering=False, num_devices=1, dynamic_dma_scratch_size=1024)
    aps = {n: nc.dram_tensor("in_" + n, v.shape, mybir.dt.from_np(v.dtype), kind="ExternalInput").ap()
           for n, v in arrays.items()}
    out = nc.dram_tensor("out", (1, T, D), F32, kind="ExternalOutput").ap()
    two_block_kernel(nc, aps, out)
    result = run_bass_kernel_spmd(nc, [{"in_" + n: v for n, v in arrays.items()}], core_ids=[0])
    return result.results[0]["out"]
```

```python
from contextlib import ExitStack

import numpy as np
import concourse.bass as bass
from concourse import mybir

F32 = mybir.dt.float32
F32R = mybir.dt.float32r
I32 = mybir.dt.int32
ALU = mybir.AluOpType
ACT = mybir.ActivationFunctionType
X = mybir.AxisListType.X

LN_EXP, SILU_SET = "natural_log_exp_and_others", "silu_and_others"
P = 128
T = 256
TT = T // P
D = 1024
KD = D // P
HD = 64
W512 = 512
EPS = 1e-6
NEG = -1e30
N_MOD = 6
N_EXPERTS = 16
EXPERTS_PER_GROUP = 4
N_GROUPS = 4
FF = 512
SLOTS = 64
PAIRS = N_EXPERTS // 2
WINDOWS = (2, 4, 8, 16)
CHUNK = KD * W512
RING = 5
DOUBLED = 4
SPLIT = 4
ADA_PARTS = 4
POOL_FROM = 1
PIECES = (1, 0, 2, 3)

IN1 = dict(ax=0, az=512, bq=1024, bkv=1536, bz=1792, cq=2304, ck=2816, cv=3328, cz=3840, gate=4352)
IN2 = dict(qa=0, ka=512, va=1024, fa=1536, qb=1544, kb=2056, vb=2568, gate=3080)

VEC = {}
_at = 0
for _name, _n in (("eps", 1), ("norm_g", 8), ("norm1_g", 8), ("norm2_g", 8), ("c", 8), ("pool_scale", 4),
                  ("ada_b", 48), ("b_forget", 1), ("sink", 8), ("router_b", 20)):
    VEC[_name] = slice(_at, _at + _n)
    _at += _n
N_VEC = _at

CON = {}
_at = 0
for _name, _n in (("ident", 128), ("mask_causal", 384), ("mask_swa", 384), ("mask_strict", 384),
                  ("suffix", 128), ("before", 128), ("ones", 256), ("iota", 64), ("inv_count", 64),
                  ("tie", 16)):
    CON[_name] = slice(_at, _at + _n)
    _at += _n
N_CON = _at


def constants():
    c = np.zeros((P, N_CON), np.float32)
    i, j = np.arange(P)[:, None], np.arange(P)[None, :]
    causal = np.where(j <= i, 0.0, NEG)
    c[:, CON["ident"]] = i == j
    c[:, CON["mask_causal"]] = np.concatenate([causal, np.zeros((P, P)), causal], 1)
    c[:, CON["mask_swa"]] = np.concatenate([causal, np.where(j > i, 0.0, NEG), causal], 1)
    strict = np.where(i < j, 0.0, NEG)
    c[:, CON["mask_strict"]] = np.concatenate([strict, np.zeros((P, P)), strict], 1)
    c[:, CON["suffix"]] = i >= j
    c[:, CON["before"]] = i < j
    c[:, CON["ones"]] = 1.0
    c[:, CON["iota"]] = np.arange(SLOTS)
    c[:, CON["inv_count"]] = np.concatenate([1.0 / np.minimum(np.arange(16) + 1, w) for w in WINDOWS])
    c[:, CON["tie"]] = (np.arange(4)[None, :] < np.arange(4)[:, None]).reshape(-1)
    return c


def plan():
    steps = []
    unit = lambda *u: steps.append(("unit",) + u)

    def unit_and_heads(u, n):
        if n == 2:
            steps.append(("begin",) + u)
            heads(todo)
        unit(*u)
        heads(todo, min(n, 1))

    def heads(todo, n=1):
        for _ in range(n):
            h = todo.pop(0)
            for kind, g in (("S", h), ("T", h - 1), ("V", h - 2)):
                if first <= g < last:
                    steps.append((kind, g))

    ada = [(c, part) for c in range(2 * N_MOD) for part in range(ADA_PARTS)]
    ada_due = []

    def some_ada(n):
        for _ in range(n):
            if ada:
                c, part = ada.pop(0)
                if ada_due and part == ADA_PARTS // 2:
                    unit("mod", ada_due.pop(0))
                steps.append(("ada", c, part))
                if part == ADA_PARTS - 1:
                    ada_due.append(c)
            elif ada_due:
                unit("mod", ada_due.pop(0))

    steps += [("norm", 0, 0), ("norm", 0, 1)]
    unit("hT", 0, 0, 0)
    unit("hT", 0, 0, 1)
    unit("hT", 0, 1, 0)
    unit("hT", 0, 1, 1)
    unit("tm", "cv", 0)
    unit("tm", "cv", 1)
    for name in ("cz", "bz", "az", "ax", "cq", "ck"):
        unit("fm", name, 0)
        some_ada(2 * (name != "cz"))
        unit("fm", name, 1)
        some_ada(2 * (name != "cz"))
        if name == "ax":
            steps.append(("pool",))
    steps.append(("load_final_g", 0))
    first, last = 0, 16
    todo = list(range(0, 18))
    seq = [(("fm", "bq", 0), 1), (("fm", "bq", 1), 1), (("bkv",), 1), (("mix", 0), 0), (("mix", 1), 0)]
    seq += [(("tm", f"g{i}", t), 2 if (i, t) in ((2, 0), (3, 0), (0, 0)) else 1) for i in (4, 5, 2, 3, 0, 1) for t in range(TT)]
    low_due = None
    for n, (u, entering) in enumerate(seq):
        unit_and_heads(u, entering)
        if low_due:
            steps.append(("y_split_low", low_due))
            low_due = None
        if n == 10:
            steps.append(("y_split", "c"))
            low_due = "c"
        if n == 11:
            steps.append(("y_split", "a"))
            low_due = "a"
        if n < 5 and n != 2 or entering == 1 and u[0] == "tm" and u != ("tm", "g2", 1):
            some_ada(1)
    assert not todo
    steps += [("sigmoid", 16), ("y_split", "b"), ("fa_split",), ("y_split_low", "b")]
    for br in "cb":
        for t in range(TT):
            for half in range(2):
                unit("proj", br, t, half)
                if half:
                    some_ada(1)
                if (t, half) == (0, 1):
                    steps.append(("sigmoid", 8 if br == "c" else 0))

    def merge_and_out(br, blk):
        unit("proj", br, 0, 0)
        unit("proj", br, 0, 1)
        unit("proj", br, 1, 0)
        unit("mT", blk, 0, 0)
        unit("mT", blk, 0, 1)
        unit("proj", br, 1, 1)
        unit("wout", blk, 0, 0)
        unit("mT", blk, 1, 0)
        unit("mT", blk, 1, 1)
        steps.append(("norm_half", 2 * blk - 1, 0))
        unit("wout", blk, 0, 1)

    steps.append(("mods", 0))
    merge_and_out("a", 1)
    steps += [("norm", 1, 0), ("norm", 2, 0)]
    unit("wout", 1, 1, 0)
    unit("hT", 1, 0, 0)
    unit("hT", 1, 0, 1)
    steps.append(("norm_half", 1, 1))
    unit("wout", 1, 1, 1)
    steps += [("norm", 1, 1), ("norm", 2, 1)]
    unit("tm", "va", 0)
    unit("hT", 1, 1, 0)
    unit("hT", 1, 1, 1)
    for u in (("tm", "vb", 0), ("tm", "va", 1), ("tm", "vb", 1), ("fm", "qa", 0), ("fm", "qa", 1),
              ("fm", "ka", 0), ("fm", "ka", 1)):
        unit(*u)
        some_ada(2)
    while ada or ada_due:
        some_ada(1)
    steps.append(("load_late",))
    unit("fa",)
    steps.append(("logf",))
    unit("fm", "qb", 0)
    unit("FT",)
    first, last = 16, 32
    todo = list(range(16, 34))
    seq = [(("fm", "qb", 1), 1), (("fm", "kb", 0), 1), (("fm", "kb", 1), 2), (("tm", "h0", 0), 1),
           (("tm", "h0", 1), 2), (("tm", "h1", 0), 1), (("tm", "h1", 1), 2), (("tm", "h2", 0), 1),
           (("tm", "h2", 1), 2), (("tm", "h3", 0), 1), (("tm", "h3", 1), 2), (("proj", "f", 0, 0), 1),
           (("proj", "f", 0, 1), 1), (("proj", "f", 1, 0), 0), (("proj", "f", 1, 1), 0)]
    for u, n in seq:
        unit_and_heads(u, n)
        if u == ("tm", "h1", 1):
            steps.append(("sigmoid", 0))
        if u == ("tm", "h2", 1):
            steps.append(("y_split", "f"))
        if u == ("tm", "h3", 0):
            steps.append(("y_split_low", "f"))
        if u == ("proj", "f", 0, 1):
            steps.append(("y_split", "s"))
        if u == ("proj", "f", 1, 0):
            steps.append(("y_split_low", "s"))
    assert not todo
    steps += [("sigmoid", 8), ("mods", 1), ("load_final_g", 1)]
    merge_and_out("s", 2)
    steps.append(("norm", 3, 0))
    unit("wout", 2, 1, 0)
    unit("hT", 2, 0, 0)
    unit("hT", 2, 0, 1)
    steps.append(("norm_half", 3, 1))
    unit("wout", 2, 1, 1)
    steps.append(("norm", 3, 1))
    unit("logit", 0)
    unit("hT", 2, 1, 0)
    unit("hT", 2, 1, 1)
    unit("logit", 1)
    steps.append(("route",))
    unit("rank",)
    steps.append(("slots",))

    split = []
    for s in steps:
        split += [c for c in chunk_of(s) if c[0] != "ada" and c not in split]
    places, before = [], {}
    for m, c in enumerate(split):
        first_use = next(i for i, s in enumerate(steps) if c in chunk_of(s))
        if m:
            free = max(i for i, s in enumerate(steps) if m > 1 and split[m - 2] in chunk_of(s) or
                       m == 1 and s == ("unit", "tm", "cv", 0))
            place = next(i for i in range(free + 1, first_use + 1) if steps[i][0] == "unit")
        else:
            place = first_use = steps.index(("unit", "hT", 0, 1, 0))
        places.append((place, first_use))
    for m, (place, first_use) in enumerate(places):
        for i, q in enumerate(PIECES):
            at = min([place + i * (first_use - place) // (2 * SPLIT)] + [p for p, _ in places[m + 1:m + 2]])
            before.setdefault(at, []).append(("split", split[m], q))
            if q < POOL_FROM:
                later = (first_use - at) // 4 if first_use - at > 5 else 0
                before.setdefault(at + later, []).append(("split_low", split[m], q))
    steps = [x for i, s in enumerate(steps) for x in before.get(i, []) + [s]]
    assert [s[1:] for s in steps if s[0] == "split"] == [(c, q) for c in split for q in PIECES]
    assert [s[1:] for s in steps if s[0] == "split_low"] == [(c, q) for c in split for q in PIECES if q < POOL_FROM]

    chunks = []
    for s in steps:
        for name in chunk_of(s):
            if name not in chunks:
                chunks.append(name)
    return steps, chunks


def chunk_of(step):
    if step[0] == "ada":
        return [("ada", step[1])]
    if step[0] == "split":
        return [step[1]]
    if step[0] in ("unit", "begin") and step[1] in ("fm", "tm"):
        return [(step[2],)]
    if step[0] == "unit" and step[1] == "bkv":
        return [("bkv",)]
    if step[0] == "unit" and step[1] == "proj":
        return [("proj", step[2])]
    if step[0] == "unit" and step[1] == "wout":
        return [("wout", step[2], step[4])]
    return []


STEPS, CHUNKS = plan()
UNITS = [s[1:] for s in STEPS if s[0] == "unit"]
SILU = ("cz", "bz", "az")


def evictor(u):
    if u[0] in ("tm", "bkv", "fa", "FT") or (u[0] == "fm" and u[1] not in SILU) or (u[0:2] == ("hT", 2) and u[3] == 0):
        return "act"
    return "dve"


def evict_count(u):
    n = UNITS.index(u)
    return sum(evictor(v) == evictor(u) for v in UNITS[:n + 1])


def last_reader(chunk, first=False):
    if chunk[0] == "ada":
        order = [s[1] for s in STEPS if s[0] == "ada" and s[2] == ADA_PARTS - 1]
        return "dve", order.index(chunk[1]) + 1
    n = [i for i, u in enumerate(UNITS) if chunk in chunk_of(("unit",) + u)][0 if first else -1]
    return "pe", n + 1


SPLITS = [s[1] for s in STEPS if s[0] == "split" and s[2] == PIECES[0]]
Y_SPLITS = [s[1] for s in STEPS if s[0] == "y_split"]
HI_UNITS = [u for u in UNITS if u[0] == "mT" or u[0] == "hT" and u[1] < 2]
SILU_UNITS = [u for u in UNITS if u[0] == "fm" and u[1] in SILU]
SIGMOIDS = [s for s in STEPS if s[0] == "sigmoid"]
NORMS = [s[1:] for s in STEPS if s[0] == "norm"] + [(4, 0), (4, 1)]
HALF_NORMS = [s[1:] for s in STEPS if s[0] == "norm_half"]
XN_NORMS = [s for s in NORMS if s[0] in (0, 2, 3)]


def two_block_kernel(nc, a, out):
    x_in, w_in1, w_in2 = a["x"][0], a["w_in"][0], a["w_in_2"][0]

    def k_rows(w, cols):
        return w[:, cols].rearrange("(k p) n -> p k n", p=P)

    def chunk_source(c):
        if c[0] == "ada":
            return k_rows(a["ada_w_2"][0], slice(c[1] * W512, (c[1] + 1) * W512))
        if c[0] == "proj":
            w = dict(a="w_proj_a", b="w_proj_b", c="w_proj_c", f="w_branch_fox_2", s="w_branch_sb_2")[c[1]]
            return k_rows(a[w][0], slice(0, D))
        if c[0] == "wout":
            return k_rows(a[("w_out", "w_out_2")[c[1] - 1]][0], slice(c[2] * W512, (c[2] + 1) * W512))
        if c[0] == "bq":
            return k_rows(a["w_bq"], slice(0, W512))
        if c[0] == "bkv":
            return k_rows(w_in1, slice(IN1["bkv"], IN1["bkv"] + 256))
        if c[0] in IN1:
            at, w = IN1[c[0]], w_in1
        elif c[0] in IN2:
            at, w = IN2[c[0]], w_in2
        elif c[0][0] == "g":
            at, w = IN1["gate"] + W512 * int(c[0][1]), w_in1
        else:
            at, w = IN2["gate"] + W512 * int(c[0][1]), w_in2
        return k_rows(w, slice(at, at + W512))

    with ExitStack() as ctx:
        def sb(name, shape, dt=F32):
            return ctx.enter_context(nc.sbuf_tensor(name, shape, dt))

        def sem(name):
            return ctx.enter_context(nc.semaphore(name))

        rounded = {}

        def two_names(name, shape):
            at = -(-nc.sbuf_base // 32) * 32
            t = sb(name, shape)
            rounded[name] = nc.alloc_sbuf_tensor_at(name + "_rounded", shape, F32R, offset=at)
            return t

        shared = dict(hT=[P, KD, T], work=[P, 6656], mixed=[P, 3, 4, T],
                      gates=[P, 24, T], fa_w=[P, KD, 8], fa_hi=[P, KD, 8])
        ring = [two_names(f"ring{i}", [P, CHUNK]) for i in range(RING + 2)]
        hT, work, mixed, gates, fa_w, fa_hi = (two_names(n, shape) for n, shape in shared.items())
        as_rounded = lambda ap: bass.AP(rounded[ap.tensor.name], ap.offset, ap.ap)
        was_rounded = lambda ap: as_rounded(ap).bitcast(F32)
        con = sb("con", [P, N_CON])
        late = slice(CON["mask_strict"].start, CON["suffix"].stop)
        vec = sb("vec", [P, N_VEC])
        gate_rows = sb("gate_rows", [P, 2, D])
        x_res = sb("x_res", [P, TT, D])
        sig = sb("sig", [P, 2, W512])
        ada_acc = sb("ada_acc", [P, W512])
        ada_accs = ada_acc[:, :], con[:, late]
        attn = sb("attn", [P, 4, 384])
        score = attn[:, 0:2, :]
        probT = attn[:, 2:4, :]
        stat = sb("stat", [P, 10, 9])
        hstat = sb("hstat", [P, 2, 12])
        mod = sb("mod", [P, 2 * N_MOD, 4])
        aff = sb("aff", [P, 2, KD])
        c_act = sb("c_act", [P, KD])
        c_tmp = sb("c_tmp", [P, 2, KD])
        pw = sb("pw", [P, 4, P])
        rt_w = sb("rt_w", [P, KD, 20])
        fox_neg_ident = sb("fox_neg_ident", [8, 8])
        foxT = sb("foxT", [P, TT, 8])
        n_rounds = sb("n_rounds", [P, 1], I32)

        gate_tm = gates[:, :, :].rearrange("p k t -> p (k t)").rearrange("p (b t f) -> p b t f", b=3, t=TT)
        xn = gate_tm[:, 0]
        fin_g = sig[:, :, :].rearrange("p h n -> p (h n)")
        fox = sig[0:8, :, :].rearrange("p h n -> p (h n)").rearrange("p (r t) -> p r t", r=4)
        tmp = attn[:, :, :].rearrange("p b n -> p (b n)")[:, D:D + W512]
        junk = attn[:, :, :].rearrange("p b n -> p (b n)")[:, 0:D]
        hT_lo = work[:, 4608:6656].rearrange("p (k t) -> p k t", k=KD)
        fm4 = lambda at: work[:, at:at + 1024].rearrange("p (n t) -> p n t", n=4)
        y_high = dict(c=fm4(0), b=fm4(1024), a=fm4(2048), f=fm4(0), s=fm4(1024))
        y_low = {br: mixed[:, i] for br, i in dict(c=0, b=1, a=2, f=0, s=1).items()}
        merged_hi = gates[:, 16:24, :]
        merged_lo = lambda blk, half: mixed[:, (0, blk)[half]]
        pool_x, pool_a, pool_b = (gates[:, n:n + 4, :] for n in (12, 16, 20))
        tm2 = lambda at: work[:, at:at + 1024].rearrange("p (t n) -> p t n", t=TT)
        qm, km, vm, qs = fm4(0), fm4(1024), tm2(2048), fm4(3072)
        kb2, vb2 = gates[:, 16:20, :], gates[:, 20:24, :].rearrange("p k t -> p (k t)").rearrange("p (t n) -> p t n", t=TT)
        kvs = work[:, 4096:4608]
        soft = mixed[:, 2, 0:3, :].rearrange("p k t -> p (k t)").rearrange("p (b n) -> p b n", b=2)
        xg = work[:, 0:1024].rearrange("p (k s) -> p k s", k=KD)
        onehot = work[:, 1024:1280].rearrange("p (t e s) -> p t e s", t=TT, e=2)
        combine = work[:, 1280:1536].rearrange("p (t e s) -> p t e s", t=TT, e=2)
        act = work[:, 1536:2048]
        sil = work[:, 2048:3072].rearrange("p (e f) -> p e f", e=2)
        actT = work[:, 3072:3584].rearrange("p (k s) -> p k s", k=4)
        y_pair = work[:, 3584:4608]
        combT = work[:, 4608:4864]
        rt = work[:, 4864:5964]

        psum = ctx.enter_context(nc.psum_tensor("psum", [P, 8, W512], F32))
        bank = [psum[:, i, :] for i in range(8)]
        unit_bank, o_bank, score_bank, trans_bank = bank[0:3], bank[3], bank[4:6], bank[6:8]
        out_bank = bank[0:4]
        gu_bank, x_bank = bank[4:6], bank[6:8]

        cs = lambda name: con[:, CON[name]]
        ident, ones = cs("ident"), cs("ones")

        x_loaded = [sem(f"x_loaded{t}") for t in range(TT)]
        ident_loaded = sem("ident_loaded")
        con_loaded = sem("con_loaded")
        late_loaded = sem("late_loaded")
        gate_rows_loaded = sem("gate_rows_loaded")
        vec_loaded = sem("vec_loaded")
        small_loaded = sem("small_loaded")
        fin1_loaded = sem("fin1_loaded")
        fin2_loaded = sem("fin2_loaded")
        chunk_loaded = [sem(f"chunk_loaded{s}") for s in range(RING + 2)]
        odd_loaded = [sem(f"odd_loaded{j}") for j in range(DOUBLED)]
        unit_done = sem("unit_done")
        act_evicted = sem("act_evicted")
        dve_evicted = sem("dve_evicted")
        sig_ready = sem("sig_ready")
        ada_done = sem("ada_done")
        c_exp = sem("c_exp")
        sumsq_ready = sem("sumsq_ready")
        half_sumsq_ready = sem("half_sumsq_ready")
        half_mean_ready = sem("half_mean_ready")
        ms_ready = sem("ms_ready")
        guess_ready = sem("guess_ready")
        gates_ready = sem("gates_ready")
        chunk_hi = sem("chunk_hi")
        chunk_split = sem("chunk_split")
        chunk_split_pool = sem("chunk_split_pool")
        y_hi = sem("y_hi")
        y_split_done = sem("y_split_done")
        hi_ready = sem("hi_ready")
        fa_hi_ready = sem("fa_hi_ready")
        fa_split_done = sem("fa_split_done")
        x1_ready = sem("x1_ready")
        xn_ready = sem("xn_ready")
        pooled_ready = sem("pooled_ready")
        scores_done = sem("scores_done")
        scores_masked = sem("scores_masked")
        max_ready = sem("max_ready")
        exp_done = sem("exp_done")
        probs_ready = sem("probs_ready")
        pt_done = sem("pt_done")
        stick_ready = sem("stick_ready")
        pt_evicted = sem("pt_evicted")
        o_done = sem("o_done")
        o_evicted = sem("o_evicted")
        fox_abs = sem("fox_abs")
        fox_log = sem("fox_log")
        fox_ready = sem("fox_ready")
        mods_ready = sem("mods_ready")
        group_shifted = sem("group_shifted")
        group_exp = sem("group_exp")
        sel_ready = sem("sel_ready")
        rounds_ready = sem("rounds_ready")
        dve_chain = sem("dve_chain")
        act_chain = sem("act_chain")
        onehot_ready = sem("onehot_ready")
        gather_done = sem("gather_done")
        xg_act = sem("xg_act")
        xg_dve = sem("xg_dve")
        gu_done = sem("gu_done")
        silu_done = sem("silu_done")
        act_ready = sem("act_ready")
        combine_ready = sem("combine_ready")
        actT_done = sem("actT_done")
        combT_done = sem("combT_done")
        actT_evicted = sem("actT_evicted")
        combT_evicted = sem("combT_evicted")
        down_done = sem("down_done")
        y_ready = sem("y_ready")
        scatter_done = sem("scatter_done")
        tile_done = sem("tile_done")
        out_ready = sem("out_ready")
        stored = sem("stored")

        block = ctx.enter_context(nc.Block())

        def evicted(u):
            return (act_evicted if evictor(u) == "act" else dve_evicted), evict_count(u)

        def sigmoids(first_tile, block):
            return [n for n, g in enumerate(SIGMOIDS) if g[1] == first_tile][block - 1 if first_tile < 16 else 0] + 1

        def wait_chunk(eng, c):
            n = CHUNKS.index(c)
            eng.wait_ge(chunk_loaded[n % RING], 16 * (n // RING + 1))
            return ring[n % RING][:, :]

        def piece_of(c, q):
            n = CHUNK // (2 if c == ("bkv",) else 1) // SPLIT
            return slice(q * n, (q + 1) * n)

        def dense_uses(s):
            return len(range(s, len(CHUNKS), RING)) if s < RING else 0

        first_expert_slot = len(CHUNKS) % RING
        slot_of = lambda j: (first_expert_slot + j) % RING if j < RING else j

        def high(c):
            return ring[RING + SPLITS.index(c) % 2][:, :]

        PAIR_LOADS = (("expert_w_gate_2", 0), ("expert_w_up_2", 0), ("expert_w_gate_2", 1),
                      ("expert_w_up_2", 1), ("expert_w_down_2", 0), ("expert_w_down_2", 1))

        def flat(ap):
            return ap.rearrange("p k t -> p (k t)")

        odd_places = ([ring[RING + 1][:, :]], [flat(gates[:, 8:24, :])],
                      [flat(hT[:, :, :]), mixed[:, 0:2].rearrange("p b k t -> p (b k t)")],
                      [flat(mixed[:, 2]), con[:, CON["mask_causal"].start:CON["mask_causal"].start + 2 * W512],
                       junk, ada_acc[:, :], pw[:, :, :].rearrange("p g n -> p (g n)")])

        def pair_parts(j, odd):
            places = odd_places[j] if odd and j < DOUBLED else [ring[slot_of(j)][:, :]]
            return [c.rearrange("p (k n) -> p k n", n=W512 if j < 4 else D) for c in places]

        def pair_rows(j, odd, k):
            for part in pair_parts(j, odd):
                if k < part.shape[1]:
                    return part[:, k, :]
                k -= part.shape[1]

        def pair_sem(j, odd):
            return odd_loaded[j] if odd and j < DOUBLED else chunk_loaded[slot_of(j)]

        def pair_loaded(eng, j, it, half, odd):
            if j >= DOUBLED:
                eng.wait_ge(pair_sem(j, odd), it * 16 + 16 * (dense_uses(slot_of(j)) + 1))
            elif odd:
                n = 16 * len(odd_places[j])
                eng.wait_ge(pair_sem(j, odd), half * n + n)
            else:
                eng.wait_ge(pair_sem(j, odd), half * 16 + 16 * (dense_uses(slot_of(j)) + 1))

        @block.sync
        def _(sp):
            def wait_slot_free(n):
                if n >= RING:
                    who, count = last_reader(CHUNKS[n - RING])
                    sp.wait_ge(ada_done if who == "dve" else unit_done, count)

            for t in range(TT):
                sp.dma_start(x_res[:, t, :], x_in[t * P:(t + 1) * P, :]).then_inc(x_loaded[t], 16)
            for n, c in enumerate(CHUNKS):
                wait_slot_free(n)
                src = chunk_source(c)
                dst = ring[n % RING][:, 0:src.shape[1] * src.shape[2]]
                sp.dma_start(dst.rearrange("p (k n) -> p k n", n=src.shape[2]), src)\
                  .then_inc(chunk_loaded[n % RING], 16)

            def load(it, pair, odd, j, first=False):
                name, e = PAIR_LOADS[j]
                if first and not odd and j < RING:
                    wait_slot_free(len(CHUNKS) + j)
                elif first and not odd:
                    assert slot_of(j) == RING + SPLITS.index(("wout", 2, 0)) % 2
                    sp.wait_ge(unit_done, UNITS.index(("wout", 2, 1, 0)) + 1)
                elif first and j == 3:
                    sp.wait_ge(xn_ready, len(XN_NORMS))
                elif first:
                    sp.wait_ge(unit_done, UNITS.index(("wout", 2, 1, 1)) + 1)
                elif j < DOUBLED:
                    sp.wait_ge(gu_done, it * 2 - 3 + j // 2)
                else:
                    sp.wait_ge(down_done, it * 2 - 1 + j - DOUBLED)
                w = a[name][0][bass.ds(pair * 2 + e, 1)].rearrange("e (k p) n -> p (e k) n", p=P)
                at = 0
                for i, part in enumerate(pair_parts(j, odd)):
                    n = part.shape[1]
                    if first and odd and j == 2 and i == 0:
                        sp.wait_ge(unit_done, UNITS.index(("logit", 1)) + 1)
                    if not (first and odd and j == 3 and i in EARLY_PARTS):
                        sp.dma_start(part, w[:, at:at + n]).then_inc(pair_sem(j, odd), 16)
                    at += n

            EARLY_PARTS = (1, 3, 4)

            def load_early(parts):
                name, e = PAIR_LOADS[3]
                w = a[name][0][2 + e].rearrange("(k p) n -> p k n", p=P)
                places = pair_parts(3, 1)
                for i in parts:
                    at = sum(place.shape[1] for place in places[:i])
                    sp.dma_start(places[i], w[:, at:at + places[i].shape[1]]).then_inc(pair_sem(3, 1), 16)

            gates_0, gates_1, downs = (0, 1), (2, 3), (4, 5)

            def load_some(it, pair, odd, which, first=False):
                for j in which:
                    load(it, pair, odd, j, first)

            def load_rest_of_round(r):
                def step(pair, odd, order):
                    for which in order:
                        ahead = 1 if which == downs else 2
                        load_some(r * PAIRS + pair + ahead, pair + ahead, (odd + ahead) % 2, which)

                for pair in range(2):
                    step(pair, pair, (gates_0, gates_1, downs))
                with sp.Fori(1, PAIRS // 2 - 1) as two_pairs:
                    for odd in range(2):
                        step(two_pairs * 2 + odd, odd, (gates_0, downs, gates_1))
                load_some(r * PAIRS + PAIRS - 1, PAIRS - 1, 1, downs)

            load(0, 0, 0, 0, True)
            sp.wait_ge(unit_done, UNITS.index(("mod", 2 * N_MOD - 1)) + 1)
            load_early(EARLY_PARTS[1:])
            load(0, 0, 0, 1, True)
            sp.wait_ge(scores_masked, 32)
            load_early(EARLY_PARTS[:1])
            load_some(0, 0, 0, gates_1 + downs[::-1], True)
            load_some(1, 1, 1, gates_0 + gates_1, True)
            load_rest_of_round(0)
            sp.wait_ge(rounds_ready, 1)
            rounds = sp.value_load(n_rounds[0:1, 0:1], min_val=1, max_val=T // SLOTS)
            with sp.If(rounds > 1):
                with sp.Fori(1, rounds) as r:
                    load_some(r * PAIRS, 0, 0, gates_0 + gates_1 + downs)
                    load_some(r * PAIRS + 1, 1, 1, gates_0 + gates_1)
                    load_rest_of_round(r)
            for t in range(TT):
                for half in range(2):
                    cols = slice(half * W512, (half + 1) * W512)
                    sp.wait_ge(out_ready, 2 * t + half + 1)
                    sp.dma_start(out[0][t * P:(t + 1) * P, cols], x_res[:, t, cols]).then_inc(stored, 16)
            sp.wait_ge(stored, 16 * 2 * TT)

        @block.tensor
        def _(pe):
            def product(out, a, b, start, stop):
                nc.tensor.matmul(out, a[0], b[0], start=start, stop=False, skip_group_check=True)
                nc.tensor.matmul(out, a[0], b[1], start=False, stop=False, skip_group_check=True)
                return nc.tensor.matmul(out, a[1], b[0], start=False, stop=stop, skip_group_check=True)

            def x_parts(k, at, n):
                return as_rounded(hT[:, k, at:at + n]), as_rounded(hT_lo[:, k, at:at + n])

            def parts(c, width):
                hi, lo = (x.rearrange("p (k n) -> p k n", n=width)
                          for x in (high(c), ring[CHUNKS.index(c) % RING][:, :]))
                return lambda k, at, n: (as_rounded(hi[:, k, at:at + n]), as_rounded(lo[:, k, at:at + n]))

            def wait_piece(n, c, q):
                if last_reader(c, first=True)[1] == n + 1:
                    m = SPLITS.index(c)
                    if q < POOL_FROM:
                        pe.wait_ge(chunk_split, POOL_FROM * m + q + 1)
                    else:
                        pe.wait_ge(chunk_split_pool, (SPLIT - POOL_FROM) * m + q - POOL_FROM + 1)

            def unit(n, u, halves):
                b = unit_bank[n % 3]
                if n >= 3 and 0 in halves:
                    pe.wait_ge(*evicted(UNITS[n - 3]))
                kind = u[0]
                if kind == "hT":
                    _, norm, t, half = u
                    pe.wait_ge(xn_ready, XN_NORMS.index(((0, 2, 3)[norm], t)) + 1)
                    if n == 0:
                        pe.wait_ge(ident_loaded, 16)
                    for k in range(4):
                        f = (4 * half + k) * P
                        last = nc.tensor.transpose(b[:, k * P:(k + 1) * P], xn[:, t, f:f + P], ident)
                elif kind in ("fm", "tm", "bkv", "fa"):
                    block2 = kind == "fa" or u[1:2] and (u[1] in IN2 or u[1][0] == "h")
                    pe.wait_ge(*evicted(("hT", 1 if block2 else 0, u[2] if kind == "tm" else 1, 1)))
                    if kind == "fa":
                        pe.wait_ge(fa_split_done, 1)
                        for k in range(KD):
                            last = product(b[0:8, 0:T], (as_rounded(fa_hi[:, k, :]), as_rounded(fa_w[:, k, :])), x_parts(k, 0, T),
                                           k == 0, k == KD - 1)
                    elif kind == "bkv":
                        w = parts(("bkv",), 256)
                        for k in range(KD):
                            wait_piece(n, ("bkv",), k // 2)
                            product(b[:, 0:T], w(k, 0, P), x_parts(k, 0, T), k == 0, k == KD - 1)
                        for t in range(TT):
                            for k in range(KD):
                                last = product(b[:, T + t * P:T + (t + 1) * P], x_parts(k, t * P, P), w(k, P, P),
                                               k == 0, k == KD - 1)
                    elif kind == "tm":
                        w = parts((u[1],), W512)
                        for k in [k for h in halves for k in range(KD // 2 * h, KD // 2 * (h + 1))]:
                            wait_piece(n, (u[1],), k // 2)
                            last = product(b, x_parts(k, u[2] * P, P), w(k, 0, W512), k == 0, k == KD - 1)
                    else:
                        w = parts((u[1],), W512)
                        for j in halves:
                            n_tile = 2 * u[2] + j
                            for k in range(KD):
                                if j == 0:
                                    wait_piece(n, (u[1],), k // 2)
                                last = product(b[:, j * T:(j + 1) * T], w(k, n_tile * P, P), x_parts(k, 0, T),
                                               k == 0, k == KD - 1)
                elif kind == "mix":
                    pe.wait_ge(pooled_ready, 1)
                    pe.wait_ge(small_loaded, 16 * 3)
                    for j in range(2):
                        g = 2 * u[1] + j
                        last = nc.tensor.matmul(b[:, j * T:(j + 1) * T], pw[:, g, :], pool_a[:, g, :],
                                                start=True, stop=True)
                elif kind == "mod":
                    c = u[1]
                    pe.wait_ge(con_loaded, 16 * 2)
                    pe.wait_ge(ada_done, c + 1)
                    if c // 2 in (2, 5):
                        last = nc.tensor.matmul(b[:, :], ones[:, 0:P], ada_accs[c % 2], start=True, stop=True)
                    else:
                        for j in range(4):
                            last = nc.tensor.matmul(b[:, j:j + 1], ada_accs[c % 2][:, j * P:(j + 1) * P], ones[:, 0:1],
                                                    start=True, stop=True)
                elif kind == "proj":
                    _, br, t, half = u
                    w = parts(("proj", br), D)
                    pe.wait_ge(y_split_done, Y_SPLITS.index(br) + 1)
                    for k in range(4):
                        wait_piece(n, ("proj", br), k)
                        y = [as_rounded(x[:, k, t * P:(t + 1) * P]) for x in (y_high[br], y_low[br])]
                        last = product(b, y, w(k, half * W512, W512), k == 0, k == 3)
                elif kind == "mT":
                    _, blk, t, half = u
                    pe.wait_ge(*evicted(("proj", "a" if blk == 1 else "s", t, half)))
                    for k in range(4):
                        f = (4 * half + k) * P
                        last = nc.tensor.transpose(b[:, k * P:(k + 1) * P], gate_tm[:, 0, t, f:f + P], ident)
                elif kind == "wout":
                    _, blk, t, half = u
                    w = parts(("wout", blk, half), W512)
                    pe.wait_ge(*evicted(("mT", blk, t, 1)))
                    for k in range(KD):
                        wait_piece(n, ("wout", blk, half), k // 2)
                        m = [as_rounded(x[:, i, t * P:(t + 1) * P]) for x, i in ((merged_hi, k), (merged_lo(blk, k // 4), k % 4))]
                        last = product(b, m, w(k, 0, W512), k == 0, k == KD - 1)
                elif kind == "FT":
                    pe.wait_ge(fox_ready, 1)
                    for t in range(TT):
                        last = nc.tensor.transpose(b[:, t * 8:(t + 1) * 8], fox[:, 2, t * P:(t + 1) * P],
                                                   ident[0:8, 0:8])
                elif kind == "logit":
                    t = u[1]
                    for k in range(KD):
                        if k % 4 == 0:
                            pe.wait_ge(*evicted(("hT", 2, t, k // 4)))
                        last = nc.tensor.matmul(b[:, 0:20], hT[:, k, t * P:(t + 1) * P], rt_w[:, k, :],
                                                start=k == 0, stop=k == KD - 1)
                elif kind == "rank":
                    pe.wait_ge(sel_ready, 1)
                    before = cs("before")
                    sel = rt[:, 0:32]
                    nc.tensor.matmul(b[:, 0:16], before, sel[:, 0:16], start=True, stop=True)
                    nc.tensor.matmul(b[:, 16:32], ones[:, 0:P], sel[:, 0:16], start=True, stop=False)
                    nc.tensor.matmul(b[:, 16:32], before, sel[:, 16:32], start=False, stop=True)
                    nc.tensor.matmul(b[:, 32:48], ones[:, 0:P], sel[:, 0:16], start=True, stop=False)
                    last = nc.tensor.matmul(b[:, 32:48], ones[:, 0:P], sel[:, 16:32], start=False, stop=True)
                if 1 in halves:
                    last.then_inc(unit_done, 1)

            def operands(h):
                if h < 8:
                    lo = HD * (h % 2)
                    return qm[lo:lo + HD, h // 2], km[lo:lo + HD, h // 2], [vm[:, t, h * HD:(h + 1) * HD] for t in range(TT)]
                if h < 16:
                    g = (h - 8) // 4
                    lo = HD * g
                    return (qs[lo:lo + HD, (h - 8) % 4], kvs[lo:lo + HD, 0:T],
                            [kvs[:, T + t * P + g * HD:T + t * P + (g + 1) * HD] for t in range(TT)])
                i = h % 8
                lo = HD * (i % 2)
                q, k, v = (qm, km, vm) if h < 24 else (qs, kb2, vb2)
                return q[lo:lo + HD, i // 2], k[lo:lo + HD, i // 2], [v[:, t, i * HD:(i + 1) * HD] for t in range(TT)]

            def wait_operands(h):
                if h in (0, 8, 16, 24):
                    for u in ((("fm", "cq", 1), ("fm", "ck", 1)), (("fm", "bq", 1), ("bkv",)),
                              (("fm", "qa", 1), ("fm", "ka", 1), ("FT",)), (("fm", "qb", 1), ("fm", "kb", 1)))[h // 8]:
                        pe.wait_ge(*evicted(u))

            def scores(h):
                wait_operands(h)
                if h >= 2:
                    pe.wait_ge(scores_masked, h - 1)
                b = score_bank[h % 2]
                q, k, _ = operands(h)
                if h < 24:
                    fox_head = 16 <= h
                    for t, (lo, n) in enumerate(((0, P), (P, T))):
                        last = nc.tensor.matmul(b[:, lo:lo + n], q[:, t * P:(t + 1) * P], k[:, 0:n],
                                                start=True, stop=not fox_head)
                        if fox_head:
                            row = fox_neg_ident[:, h - 16:h - 15].to_broadcast([8, P])
                            last = nc.tensor.matmul(b[:, lo:lo + n], row, fox[:, 2, 0:n], start=False, stop=True)
                else:
                    nc.tensor.matmul(b[:, 0:T], k[:, 0:P], q[:, 0:T], start=True, stop=True)
                    last = nc.tensor.matmul(b[:, T:T + P], k[:, P:T], q[:, P:T], start=True, stop=True)
                last.then_inc(scores_done, 1)

            def turn(h):
                b = trans_bank[h % 2]
                if h >= 2:
                    pe.wait_ge(pt_evicted, h - 1)
                pe.wait_ge(probs_ready, h + 1)
                if h == 24:
                    pe.wait_ge(late_loaded, 16)
                if h < 24:
                    for j in range(3):
                        last = nc.tensor.transpose(b[:, j * P:(j + 1) * P], score[:, h % 2, j * P:(j + 1) * P], ident)
                else:
                    nc.tensor.matmul(b[:, 0:384], cs("suffix"), soft[:, h % 2, :], start=True, stop=False,
                                     skip_group_check=True)
                    last = nc.tensor.matmul(b[:, P:T], ones[:, 0:P], soft[:, h % 2, T:T + P], start=False, stop=True,
                                            skip_group_check=True)
                last.then_inc(pt_done, 1)

            def values(h):
                if h in (0, 8, 16, 24):
                    pe.wait_ge(*evicted((("tm", "cv", 1), ("bkv",), ("tm", "va", 1), ("tm", "vb", 1))[h // 8]))
                if h % 2 == 0 and h >= 2:
                    pe.wait_ge(o_evicted, h // 2)
                pe.wait_ge(pt_evicted, h + 1)
                _, _, v = operands(h)
                o = o_bank[HD * (h % 2):HD * (h % 2) + HD, :]
                nc.tensor.matmul(o[:, 0:T], v[0], probT[:, h % 2, 0:T], start=True, stop=False,
                                 skip_group_check=True)
                nc.tensor.matmul(o[:, P:T], v[1], probT[:, h % 2, T:T + P], start=False, stop=True,
                                 skip_group_check=True).then_inc(o_done, 1)

            def residual(n):
                t, half = n // 2, n % 2
                nc.tensor.matmul(out_bank[n], ident, x_res[:, t, half * W512:(half + 1) * W512], start=True, stop=True,
                                 skip_group_check=True)

            rank_bank = (len(UNITS) - 1) % 3
            n, begun = 0, False
            for s in STEPS:
                if s == ("unit", "rank"):
                    pe.wait_ge(o_evicted, 16)
                    pe.wait_ge(act_evicted, evict_count([u for u in UNITS if evictor(u) == "act"][-1]))
                    pe.wait_ge(*evicted(("logit", 1)))
                    for i in range(4):
                        if i != rank_bank:
                            residual(i)
                if s[0] == "begin":
                    unit(n, s[1:], (0,))
                    begun = True
                elif s[0] == "unit":
                    unit(n, s[1:], (1,) if begun else (0, 1))
                    n, begun = n + 1, False
                elif s[0] == "S":
                    scores(s[1])
                elif s[0] == "T":
                    turn(s[1])
                elif s[0] == "V":
                    values(s[1])

            def scatter(t):
                for half in range(2):
                    last = nc.tensor.matmul(out_bank[2 * t + half], combT[:, t * P:(t + 1) * P],
                                            y_pair[:, half * W512:(half + 1) * W512], start=False, stop=True,
                                            skip_group_check=True)
                return last

            def gather(it, half):
                pe.wait_ge(onehot_ready, it + 1)
                for k in range(4):
                    for t in range(TT):
                        f = (4 * half + k) * P
                        last = nc.tensor.matmul(x_bank[half][:, k * P:(k + 1) * P], xn[:, t, f:f + P],
                                                onehot[:, t].rearrange("p e s -> p (e s)"),
                                                start=t == 0, stop=t == TT - 1)
                last.then_inc(gather_done, 1)

            pe.wait_ge(*evicted(("rank",)))
            gather(0, 0)
            gather(0, 1)
            residual(rank_bank)
            pe.wait_ge(rounds_ready, 1)
            rounds = pe.value_load(n_rounds[0:1, 0:1], min_val=1, max_val=T // SLOTS)
            def expert_pair(it, before, odd):
                def gate_up(e):
                    pair_loaded(pe, 2 * e, it, before, odd)
                    pair_loaded(pe, 2 * e + 1, it, before, odd)
                    for k in range(KD):
                        if (e, k) == (0, 0):
                            pe.wait_ge(xg_act, it + 1)
                        if (e, k) == (0, 4):
                            pe.wait_ge(xg_dve, it + 1)
                        for half in range(2):
                            last = nc.tensor.matmul(gu_bank[e][HD * half:HD * half + HD, :],
                                                    xg[:, k, e * SLOTS:(e + 1) * SLOTS],
                                                    pair_rows(2 * e + half, odd, k),
                                                    start=k == 0, stop=k == KD - 1, skip_group_check=True)
                    last.then_inc(gu_done, 1)

                pe.wait_ge(y_ready, it * 2 + 1)
                gate_up(0)
                gather(it + 1, 0)
                pe.wait_ge(y_ready, it * 2 + 2)
                gate_up(1)
                pe.wait_ge(combT_evicted, it + 1)
                scatter(0)
                scatter(1).then_inc(scatter_done, 1)
                pe.wait_ge(act_ready, it * 2 + 1)
                pe.wait_ge(combine_ready, it + 1)
                for t in range(TT):
                    last = nc.tensor.transpose(gu_bank[0][:, t * P:(t + 1) * P],
                                               combine[:, t].rearrange("p e s -> p (e s)"), ident)
                last.then_inc(combT_done, 1)
                pe.wait_ge(act_ready, it * 2 + 2)
                for k in range(4):
                    last = nc.tensor.transpose(gu_bank[1][:, k * P:(k + 1) * P], act[:, k * P:(k + 1) * P], ident)
                last.then_inc(actT_done, 1)
                gather(it + 1, 1)
                pe.wait_ge(combT_evicted, it + 2)
                pe.wait_ge(actT_evicted, it + 1)
                for e in range(2):
                    pair_loaded(pe, 4 + e, it, before, odd)
                    for k in range(4):
                        for half in range(2):
                            last = nc.tensor.matmul(gu_bank[e][HD * half:HD * half + HD, :],
                                                    actT[:, k, e * SLOTS:(e + 1) * SLOTS],
                                                    pair_rows(4 + e, odd, k)[:, half * W512:(half + 1) * W512],
                                                    start=k == 0, stop=k == 3, skip_group_check=True)
                    last.then_inc(down_done, 1)

            with pe.Fori(0, rounds) as r:
                with pe.Fori(0, PAIRS // 2) as two_pairs:
                    for odd in range(2):
                        expert_pair(r * PAIRS + two_pairs * 2 + odd, r * (PAIRS // 2) + two_pairs, odd)
            pe.wait_ge(y_ready, rounds * (2 * PAIRS) + 2)
            for t in range(TT):
                scatter(t).then_inc(tile_done, 1)

        @block.scalar
        def _(act_e):
            links = [0]

            def link(ins):
                links[0] += 1
                ins.then_inc(act_chain, 1)
                act_e.wait_ge(act_chain, links[0])

            def load_rest():
                for cols in (slice(P, late.start), slice(late.stop, N_CON)):
                    act_e.dma_start(con[:, cols], a["con"][:, cols]).then_inc(con_loaded, 16)
                with nc.allow_non_contiguous_dma(reason="few bytes"):
                    act_e.dma_start(pw[:, :, :], a["pool_w"][0].rearrange("g c d -> c g d")).then_inc(small_loaded, 16)
                    act_e.dma_start(fa_w[:, :, :], k_rows(w_in2, slice(IN2["fa"], IN2["fa"] + 8))).then_inc(small_loaded, 16)
                    act_e.dma_start(rt_w[:, :, :], a["router_w"].rearrange("(k p) n -> p k n", p=P)).then_inc(small_loaded, 16)
                act_e.dma_start(gate_rows[:, :, :], a["gate_b"]).then_inc(gate_rows_loaded, 16)

            act_e.dma_start(vec[:, :], a["vec"]).then_inc(vec_loaded, 16)
            act_e.dma_start(con[:, 0:P], a["con"][:, 0:P]).then_inc(ident_loaded, 16)
            nc.scalar.preload_act_table_set(LN_EXP)
            act_e.wait_ge(vec_loaded, 16)
            nc.scalar.activation(c_tmp[:, 0, :], vec[:, VEC["c"]], ACT.Exp, scale=-1.0).then_inc(c_exp, 1)

            def norm_half(n, t):
                if t == 0:
                    nc.scalar.preload_act_table_set(LN_EXP)
                act_e.wait_ge(*evicted(("wout", 1 if n == 1 else 2, t, 0)))
                nc.scalar.activation(junk[:, 0:W512], x_res[:, t, 0:W512], ACT.Square,
                                     accum_out=stat[:, NORMS.index((n, t)), 6:7]).then_inc(half_sumsq_ready, 1)

            def norm(n, t):
                i = NORMS.index((n, t))
                if (n, t) == (4, 0):
                    nc.scalar.preload_act_table_set(LN_EXP)
                if n == 0:
                    act_e.wait_ge(x_loaded[t], 16)
                elif n in (1, 3):
                    act_e.wait_ge(*evicted(("wout", 1 if n == 1 else 2, t, 1)))
                elif n == 2:
                    act_e.wait_ge(x1_ready, 2 * t + 2)
                else:
                    act_e.wait_ge(tile_done, t + 1)
                s = stat[:, i, :]
                x = x_res[:, t, :] if n < 4 else psum[:, 2 * t:2 * t + 2, :].rearrange("p h n -> p (h n)")
                eps = vec[:, VEC["eps"]]
                if (n, t) in HALF_NORMS:
                    x, eps = x[:, W512:D], s[:, 8:9]
                nc.scalar.activation(junk[:, 0:x.shape[1]], x, ACT.Square, accum_out=s[:, 0:1]).then_inc(sumsq_ready, 1)
                act_e.wait_ge(sumsq_ready, i + 1)
                if (n, t) in HALF_NORMS:
                    act_e.wait_ge(half_mean_ready, HALF_NORMS.index((n, t)) + 1)
                link(nc.scalar.activation(s[:, 2:3], s[:, 0:1], ACT.Ln, scale=1.0 / D, bias=eps))
                nc.scalar.activation(s[:, 3:4], s[:, 2:3], ACT.Exp, scale=-0.5).then_inc(guess_ready, 1)

            def unit(n, u):
                b = unit_bank[n % 3]
                kind = u[0]
                if evictor(u) == "dve":
                    if kind == "fm":
                        i = SILU_UNITS.index(u)
                        if i >= 2:
                            act_e.wait_ge(*evicted(SILU_UNITS[i - 2]))
                        act_e.wait_ge(unit_done, n + 1)
                        nc.scalar.activation(sig[:, i % 2, :], b, ACT.Sigmoid).then_inc(sig_ready, 1)
                    if u in HI_UNITS:
                        t, half = u[2:]
                        act_e.wait_ge(unit_done, n + 1)
                        if kind == "hT" and u[1] == 1:
                            act_e.wait_ge(mods_ready, 1)
                        for k in range(4):
                            f, src = 4 * half + k, b[:, k * P:(k + 1) * P]
                            if kind == "mT":
                                if k == 0:
                                    last = nc.scalar.activation(as_rounded(merged_hi[:, f:f + 4, t * P:(t + 1) * P]),
                                                                b.rearrange("p (k t) -> p k t", k=4), ACT.Copy)
                            elif u[1] == 0:
                                last = nc.scalar.activation(as_rounded(hT[:, f, t * P:(t + 1) * P]), src, ACT.Identity,
                                                            scale=vec[:, VEC["norm_g"]][:, f:f + 1])
                            else:
                                last = nc.scalar.activation(as_rounded(hT[:, f, t * P:(t + 1) * P]), src, ACT.Identity,
                                                            scale=aff[:, 0, f:f + 1], bias=mod[:, f // 4, f % 4:f % 4 + 1])
                        last.then_inc(hi_ready, 1)
                    return
                act_e.wait_ge(unit_done, n + 1)
                if kind == "fm":
                    dst = dict(cq=qm, ck=km, bq=qs, ax=pool_x, qa=qm, ka=km, qb=qs, kb=kb2)[u[1]]
                    scale = HD ** -0.5 if u[1] in ("cq", "bq", "qa", "qb") else 1.0
                    last = nc.scalar.activation(dst[:, 2 * u[2]:2 * u[2] + 2, :].rearrange("p n t -> p (n t)"), b,
                                                ACT.Copy, scale=scale)
                elif kind == "tm":
                    if u[1][0] in "gh":
                        i = int(u[1][1])
                        dst = gate_tm[:, i // 2, u[2], (i % 2) * W512:(i % 2 + 1) * W512]
                    else:
                        dst = dict(cv=vm, va=vm, vb=vb2)[u[1]][:, u[2], :]
                    last = nc.scalar.activation(dst, b, ACT.Copy)
                elif kind == "bkv":
                    last = nc.scalar.activation(kvs, b[:, :], ACT.Copy)
                elif kind == "fa":
                    last = nc.scalar.activation(fox[:, 0, :], b[0:8, 0:T], ACT.Identity,
                                                bias=vec[0:8, VEC["b_forget"]])
                elif kind == "hT":
                    act_e.wait_ge(mods_ready, 2)
                    for k in range(4):
                        last = nc.scalar.activation(hT[:, k, u[2] * P:(u[2] + 1) * P], b[:, k * P:(k + 1) * P], ACT.Identity,
                                                    scale=aff[:, 1, k:k + 1], bias=mod[:, 6, k:k + 1])
                elif kind == "FT":
                    last = nc.scalar.activation(foxT[:, :, :].rearrange("p t h -> p (t h)"), b[:, 0:16], ACT.Copy)
                last.then_inc(act_evicted, 1)

            def probs(h):
                s = score[:, h % 2, :]
                if h < 24:
                    st = hstat[:, h % 2, :]
                    act_e.wait_ge(max_ready, h + 1)
                    if 8 <= h < 16:
                        nc.scalar.activation(st[:, 4:6], st[:, 0:2], ACT.Exp, bias=vec[:, VEC["sink"]][:, h - 8:h - 7])
                    nc.scalar.activation(s[:, 0:P], s[:, 0:P], ACT.Exp, bias=st[:, 0:1], accum_out=st[:, 2:3])
                    nc.scalar.activation(s[:, P:384], s[:, P:384], ACT.Exp, bias=st[:, 1:2], accum_out=st[:, 3:4])\
                      .then_inc(exp_done, 1)
                else:
                    z = soft[:, h % 2, :]
                    act_e.wait_ge(scores_masked, h + 1)
                    if h >= 26:
                        act_e.wait_ge(pt_done, h - 1)
                    else:
                        act_e.wait_ge(unit_done, UNITS.index(("proj", "a", 1, 1)) + 1)
                    link(nc.scalar.activation(z, s, ACT.Abs))
                    link(nc.scalar.activation(z, z, ACT.Exp, scale=-1.0))
                    nc.scalar.activation(z, z, ACT.Ln, bias=1.0).then_inc(exp_done, 1)

            def turned(h):
                act_e.wait_ge(pt_done, h + 1)
                if h >= 2:
                    act_e.wait_ge(o_done, h - 1)
                if h < 24:
                    nc.scalar.activation(probT[:, h % 2, :], trans_bank[h % 2][:, 0:384], ACT.Copy)\
                      .then_inc(pt_evicted, 1)
                else:
                    act_e.wait_ge(stick_ready, h - 23)
                    nc.scalar.activation(probT[:, h % 2, :], score[:, h % 2, :], ACT.Exp).then_inc(pt_evicted, 1)

            def sigmoid(first_tile):
                block = 2 if first_tile < 16 and gates_made[0] >= 3 else 1
                units = [u for u in UNITS if u[0] == "tm" and u[1] in [f"{'gh'[block - 1]}{first_tile // 4 + i}" for i in range(2)]]
                act_e.wait_ge(act_evicted, max(map(evict_count, units)))
                g = gates[:, first_tile:first_tile + 8, :].rearrange("p n t -> p (n t)")
                nc.scalar.activation(g, g, ACT.Sigmoid).then_inc(gates_ready, 1)
                gates_made[0] += 1
                if block == 2:
                    nc.scalar.preload_act_table_set(LN_EXP)

            gates_made = [0]

            def split(c, q):
                m, src = SPLITS.index(c), wait_chunk(act_e, c)
                if m >= 2 and q == PIECES[0]:
                    act_e.wait_ge(unit_done, last_reader(SPLITS[m - 2])[1])
                piece = piece_of(c, q)
                nc.scalar.activation(as_rounded(high(c)[:, piece]), src[:, piece], ACT.Copy).then_inc(chunk_hi, 1)

            def y_split(br):
                if br == "a":
                    act_e.wait_ge(*evicted(("mix", 1)))
                act_e.wait_ge(o_evicted, dict(a=4, c=4, b=8, f=12, s=16)[br])
                nc.scalar.activation(as_rounded(y_high[br]), y_low[br], ACT.Copy).then_inc(y_hi, 1)

            def load_late():
                act_e.wait_ge(unit_done, UNITS.index(("mod", 2 * N_MOD - 1)) + 1)
                act_e.dma_start(con[:, late], a["con"][:, late]).then_inc(late_loaded, 16)

            def load_final_g(i):
                if i == 0:
                    act_e.wait_ge(*evicted(SILU_UNITS[-1]))
                    act_e.dma_start(fin_g, a["fin1"]).then_inc(fin1_loaded, 16)
                else:
                    act_e.wait_ge(scores_done, 24)
                    act_e.wait_ge(scores_masked, 24)
                    act_e.dma_start(fin_g, a["fin2"]).then_inc(fin2_loaded, 16)

            def fa_split():
                act_e.wait_ge(small_loaded, 16 * 3)
                nc.scalar.activation(as_rounded(fa_hi[:, :, :]), fa_w[:, :, :], ACT.Copy).then_inc(fa_hi_ready, 1)

            def logf():
                act_e.wait_ge(act_evicted, evict_count(("fa",)))
                link(nc.scalar.activation(fox[:, 1, :], fox[:, 0, :], ACT.Abs))
                link(nc.scalar.activation(fox[:, 2, :], fox[:, 1, :], ACT.Exp, scale=-1.0))
                nc.scalar.activation(fox[:, 1, :], fox[:, 2, :], ACT.Ln, bias=1.0).then_inc(fox_log, 1)

            n = 0
            for s in STEPS:
                if s[0] == "unit":
                    unit(n, s[1:])
                    n += 1
                elif s[0] == "norm":
                    norm(s[1], s[2])
                    if s[1:] == (0, 1):
                        load_rest()
                elif s[0] in ("norm_half", "sigmoid", "split", "y_split", "fa_split", "load_final_g", "load_late"):
                    dict(norm_half=norm_half, load_final_g=load_final_g, load_late=load_late, sigmoid=sigmoid, split=split, y_split=y_split, fa_split=fa_split)[s[0]](*s[1:])
                elif s[0] == "S":
                    probs(s[1])
                elif s[0] == "T":
                    turned(s[1])
                elif s[0] == "logf":
                    logf()
                elif s[0] == "route":
                    act_e.wait_ge(group_shifted, 1)
                    nc.scalar.activation(rt[:, 100:140], rt[:, 100:140], ACT.Exp).then_inc(group_exp, 1)
            def xg_half(it):
                act_e.wait_ge(gather_done, it * 2 + 1)
                for k in range(4):
                    last = nc.scalar.activation(xg[:, k, :], x_bank[0][:, k * P:(k + 1) * P], ACT.Identity,
                                                scale=aff[:, 1, k:k + 1],
                                                bias=mod[:, 6:8, :].rearrange("p c j -> p (c j)")[:, k:k + 1])
                last.then_inc(xg_act, 1)

            xg_half(0)
            nc.scalar.preload_act_table_set(SILU_SET)
            act_e.wait_ge(rounds_ready, 1)
            rounds = act_e.value_load(n_rounds[0:1, 0:1], min_val=1, max_val=T // SLOTS)
            with act_e.Fori(0, rounds) as r:
                with act_e.Fori(0, PAIRS) as pair:
                    it = r * PAIRS + pair
                    for e in range(2):
                        act_e.wait_ge(gu_done, it * 2 + e + 1)
                        nc.scalar.activation(sil[HD:P, e, :], gu_bank[e][0:HD, :], ACT.Silu).then_inc(silu_done, 1)
                    act_e.wait_ge(actT_done, it + 1)
                    nc.scalar.activation(actT.rearrange("p k s -> p (k s)"), gu_bank[1], ACT.Copy)\
                      .then_inc(actT_evicted, 1)
                    xg_half(it + 1)
            for t in range(TT):
                norm(4, t)

        @block.gpsimd
        def _(pool_e):
            for s in STEPS:
                if s[0] == "split" and s[2] >= POOL_FROM:
                    _, c, q = s
                    pool_e.wait_ge(chunk_hi, SPLIT * SPLITS.index(c) + PIECES.index(q) + 1)
                    w, piece = ring[CHUNKS.index(c) % RING][:, :], piece_of(c, q)
                    nc.gpsimd.tensor_tensor(as_rounded(w[:, piece]), w[:, piece], was_rounded(high(c)[:, piece]), ALU.subtract)\
                      .then_inc(chunk_split_pool, 1)

        @block.vector
        def _(dve):
            v = nc.vector
            links = [0]

            def link(ins):
                links[0] += 1
                ins.then_inc(dve_chain, 1)
                dve.wait_ge(dve_chain, links[0])

            dve.wait_ge(c_exp, 1)
            link(v.tensor_scalar(c_tmp[:, 1, :], c_tmp[:, 0, :], 1.0, None, ALU.add))
            link(v.reciprocal(c_tmp[:, 0, :], c_tmp[:, 1, :]))
            link(v.tensor_tensor(c_act[:, :], c_tmp[:, 0, :], vec[:, VEC["c"]], ALU.mult))
            dve.wait_ge(ident_loaded, 16)
            v.tensor_scalar(fox_neg_ident[:, :], ident[0:8, 0:8], -1.0, None, ALU.mult)
            norms_on_xn = [0]

            def norm_half(n, t):
                s = stat[:, NORMS.index((n, t)), :]
                dve.wait_ge(half_sumsq_ready, HALF_NORMS.index((n, t)) + 1)
                v.tensor_scalar(s[:, 8:9], s[:, 6:7], 1.0 / D, EPS, ALU.mult, ALU.add).then_inc(half_mean_ready, 1)

            def norm(n, t):
                i = NORMS.index((n, t))
                s = stat[:, i, :]
                dve.wait_ge(sumsq_ready, i + 1)
                eps = EPS
                if (n, t) in HALF_NORMS:
                    dve.wait_ge(half_mean_ready, HALF_NORMS.index((n, t)) + 1)
                    eps = s[:, 8:9]
                v.tensor_scalar(s[:, 1:2], s[:, 0:1], 1.0 / D, eps, ALU.mult, ALU.add).then_inc(ms_ready, 1)
                dve.wait_ge(guess_ready, i + 1)
                y = s[:, 3:4]
                dve.wait_ge(ms_ready, i + 1)
                link(v.tensor_scalar(s[:, 4:5], y, y, s[:, 1:2], ALU.mult, ALU.mult))
                link(v.tensor_scalar(s[:, 5:6], s[:, 4:5], -0.5, 1.5, ALU.mult, ALU.add))
                link(v.tensor_tensor(s[:, 7:8], y, s[:, 5:6], ALU.mult))
                rstd = s[:, 7:8]
                if n in (1, 4):
                    dve.wait_ge(fin1_loaded if n == 1 else fin2_loaded, 16)
                    x = x_res[:, t, :] if n == 1 else psum[:, 2 * t:2 * t + 2, :].rearrange("p h n -> p (h n)")
                    for half in range(2):
                        cols = slice(half * W512, (half + 1) * W512)
                        v.scalar_tensor_tensor(x_res[:, t, cols], x[:, cols], rstd, fin_g[:, cols], ALU.mult, ALU.mult)\
                         .then_inc(x1_ready if n == 1 else out_ready, 1)
                else:
                    if n == 2:
                        dve.wait_ge(x1_ready, 2 * t + 2)
                    v.tensor_scalar(xn[:, t, :], x_res[:, t, :], rstd, None, ALU.mult).then_inc(xn_ready, 1)

            def unit(n, u):
                if evictor(u) != "dve":
                    return
                b = unit_bank[n % 3]
                kind = u[0]
                flat = lambda ap: ap.rearrange("p n t -> p (n t)")
                if kind == "fm":
                    i = SILU_UNITS.index(u)
                    dve.wait_ge(sig_ready, i + 1)
                    z = mixed[:, "cba".index(u[1][0]), 2 * u[2]:2 * u[2] + 2, :]
                    v.tensor_tensor(flat(z), b, sig[:, i % 2, :], ALU.mult).then_inc(dve_evicted, 1)
                    return
                dve.wait_ge(unit_done, n + 1)
                if u in HI_UNITS:
                    dve.wait_ge(hi_ready, HI_UNITS.index(u) + 1)
                if kind == "hT":
                    _, norm_i, t, half = u
                    if norm_i == 1 and (t, half) == (0, 0):
                        dve.wait_ge(mods_ready, 1)
                    if norm_i == 2 and t == 0:
                        dve.wait_ge(mods_ready, 2)
                    for k in range(4):
                        f = 4 * half + k
                        dst, src = hT[:, f, t * P:(t + 1) * P], b[:, k * P:(k + 1) * P]
                        if norm_i < 2:
                            dst = hT_lo[:, f, t * P:(t + 1) * P]
                        if norm_i == 0:
                            last = v.scalar_tensor_tensor(as_rounded(dst), src, vec[:, VEC["norm_g"]][:, f:f + 1],
                                                          was_rounded(hT[:, f, t * P:(t + 1) * P]), ALU.mult, ALU.subtract)
                        else:
                            shift = mod[:, (0 if norm_i == 1 else 6) + f // 4, f % 4:f % 4 + 1]
                            last = v.tensor_scalar(dst, src, aff[:, norm_i - 1, f:f + 1], shift, ALU.mult, ALU.add)
                    if norm_i == 1:
                        link(last)
                        rows = slice(4 * half, 4 * half + 4), slice(t * P, (t + 1) * P)
                        last = v.tensor_tensor(as_rounded(hT_lo[:, rows[0], rows[1]]), hT_lo[:, rows[0], rows[1]],
                                               was_rounded(hT[:, rows[0], rows[1]]), ALU.subtract)
                elif kind == "mT":
                    _, blk, t, half = u
                    last = v.tensor_tensor(as_rounded(merged_lo(blk, half)[:, :, t * P:(t + 1) * P]),
                                           b.rearrange("p (k t) -> p k t", k=4),
                                           was_rounded(merged_hi[:, 4 * half:4 * half + 4, t * P:(t + 1) * P]),
                                           ALU.subtract)
                elif kind == "mix":
                    dve.wait_ge(*evicted(("fm", "az", 1)))
                    for j in range(2):
                        g = 2 * u[1] + j
                        y = mixed[:, 2, g, :]
                        last = v.scalar_tensor_tensor(y, b[:, j * T:(j + 1) * T], vec[:, VEC["pool_scale"]][:, g:g + 1],
                                                      y, ALU.mult, ALU.mult)
                elif kind == "mod":
                    c = u[1]
                    if c // 2 in (2, 5):
                        dve.wait_ge(gate_rows_loaded, 16)
                        row = gate_rows[:, c // 2 == 5, (c % 2) * W512:(c % 2 + 1) * W512]
                        last = v.tensor_tensor(row, b[:, :], row, ALU.add)
                    else:
                        bias = vec[:, VEC["ada_b"]][:, 4 * c:4 * c + 4]
                        last = v.tensor_tensor(mod[:, c, :], b[:, 0:4], bias, ALU.add)
                elif kind == "proj":
                    _, br, t, half = u
                    place = dict(c=2, b=1, a=0, f=0, s=1)
                    at = lambda br: gate_tm[:, place[br], t, half * W512:(half + 1) * W512]
                    dve.wait_ge(gates_ready, sigmoids(8 * place[br], 1 if br in "abc" else 2))
                    last = v.tensor_tensor(at(br), b, at(br), ALU.mult)
                    if br not in "cf":
                        link(last)
                        dst, one, two = dict(b="bbc", a="aab", s="ffs")[br]
                        last = v.tensor_tensor(at(dst), at(one), at(two), ALU.add)
                elif kind == "wout":
                    _, blk, t, half = u
                    x = x_res[:, t, half * W512:(half + 1) * W512]
                    if blk == 1:
                        last = v.tensor_tensor(x, b[:, :], x, ALU.add)
                    else:
                        dve.wait_ge(dve_evicted, evict_count(u) - 1)
                        link(v.tensor_tensor(tmp, b[:, :], gate_rows[:, 0, half * W512:(half + 1) * W512], ALU.mult))
                        last = v.tensor_tensor(x, x, tmp, ALU.add)
                elif kind == "logit":
                    t = u[1]
                    rb = vec[:, VEC["router_b"]]
                    if t == 0:
                        dve.wait_ge(o_done, 32)
                    v.tensor_tensor(rt[:, 32 + 4 * t:36 + 4 * t], b[:, 0:4], rb[:, 0:4], ALU.add)
                    last = v.tensor_tensor(rt[:, 40 + 16 * t:56 + 16 * t], b[:, 4:20], rb[:, 4:20], ALU.add)
                elif kind == "rank":
                    pos = rt[:, 300:336].rearrange("p (t e) -> p t e", t=TT)
                    sel = rt[:, 0:32].rearrange("p (t e) -> p t e", t=TT)
                    link(v.scalar_tensor_tensor(pos[:, :, 0:16], b[:, 0:32].rearrange("p (t e) -> p t e", t=TT), 1.0,
                                                sel, ALU.add, ALU.mult))
                    link(v.tensor_scalar(pos[:, :, 0:16], pos[:, :, 0:16], -1.0, None, ALU.add))
                    v.tensor_scalar(pos[:, :, 16:18], pos[:, :, 0:2], -float(SLOTS), None, ALU.add)
                    last = v.tensor_reduce(rt[:, 340:341], b[:, 32:48], X, ALU.max)
                last.then_inc(dve_evicted, 1)

            def pool():
                dve.wait_ge(*evicted(("fm", "ax", 1)))
                src = pool_x
                for i, w in enumerate(WINDOWS):
                    dst, h = (pool_a, pool_b)[i % 2], w // 2
                    v.tensor_copy(dst[:, i:4, 0:h], src[:, i:4, 0:h])
                    link(v.tensor_tensor(dst[:, i:4, h:T], src[:, i:4, h:T], src[:, i:4, 0:T - h], ALU.add))
                    src = dst
                inv = cs("inv_count").rearrange("p (g t) -> p g t", g=4)
                for g, w in enumerate(WINDOWS):
                    s = (pool_a, pool_b)[g % 2][:, g, :]
                    link(v.tensor_tensor(s[:, 0:16], s[:, 0:16], inv[:, g, :], ALU.mult))
                    v.tensor_tensor(pool_a[:, g, 0:16], s[:, 0:16], pool_x[:, g, 0:16], ALU.subtract)
                    last = v.scalar_tensor_tensor(pool_a[:, g, 16:T], s[:, 16:T], 1.0 / w, pool_x[:, g, 16:T],
                                                  ALU.mult, ALU.subtract)
                last.then_inc(pooled_ready, 1)

            def ada(c, part):
                w = wait_chunk(dve, ("ada", c)).rearrange("p (k n) -> p k n", n=W512)
                acc, n = ada_accs[c % 2], KD // ADA_PARTS
                if c >= 2 and part == 0:
                    dve.wait_ge(unit_done, UNITS.index(("mod", c - 2)) + 1)
                for k in range(n * part, n * part + n):
                    if k == 0:
                        ins = v.tensor_scalar(acc, w[:, 0, :], c_act[:, 0:1], None, ALU.mult)
                    else:
                        ins = v.scalar_tensor_tensor(acc, w[:, k, :], c_act[:, k:k + 1], acc, ALU.mult, ALU.add)
                    if k < KD - 1:
                        link(ins)
                    else:
                        ins.then_inc(ada_done, 1)

            def split_low(c, q):
                dve.wait_ge(chunk_hi, SPLIT * SPLITS.index(c) + PIECES.index(q) + 1)
                w, piece = ring[CHUNKS.index(c) % RING][:, :], piece_of(c, q)
                v.tensor_tensor(as_rounded(w[:, piece]), w[:, piece], was_rounded(high(c)[:, piece]), ALU.subtract)\
                 .then_inc(chunk_split, 1)

            def y_split_low(br):
                dve.wait_ge(y_hi, Y_SPLITS.index(br) + 1)
                v.tensor_tensor(as_rounded(y_low[br]), y_low[br], was_rounded(y_high[br]), ALU.subtract).then_inc(y_split_done, 1)

            def fa_split():
                dve.wait_ge(fa_hi_ready, 1)
                v.tensor_tensor(as_rounded(fa_w[:, :, :]), fa_w[:, :, :], was_rounded(fa_hi[:, :, :]), ALU.subtract).then_inc(fa_split_done, 1)

            def mods(i):
                c = (2, 8)[i]
                dve.wait_ge(*evicted(("mod", c + 1)))
                g = vec[:, VEC["norm1_g" if i == 0 else "norm2_g"]]
                v.scalar_tensor_tensor(aff[:, i, :], mod[:, c:c + 2, :].rearrange("p c j -> p (c j)"), 1.0, g,
                                       ALU.add, ALU.mult).then_inc(mods_ready, 1)

            def probs(h):
                s = score[:, h % 2, :]
                st = hstat[:, h % 2, :]
                b = score_bank[h % 2]
                dve.wait_ge(scores_done, h + 1)
                if h == 0:
                    dve.wait_ge(con_loaded, 16 * 2)
                if h == 24:
                    dve.wait_ge(late_loaded, 16)
                if h >= 2:
                    if h - 2 < 24:
                        dve.wait_ge(pt_done, h - 1)
                    else:
                        dve.wait_ge(pt_evicted, h - 1)
                mask = cs("mask_causal" if h < 8 or 16 <= h < 24 else "mask_swa" if h < 16 else "mask_strict")
                if 16 <= h < 24:
                    v.scalar_tensor_tensor(s[:, 0:P], b[:, 0:P], foxT[:, 0, h - 16:h - 15], mask[:, 0:P], ALU.add, ALU.add)
                    v.scalar_tensor_tensor(s[:, P:384], b[:, P:384], foxT[:, 1, h - 16:h - 15], mask[:, P:384], ALU.add, ALU.add)\
                     .then_inc(scores_masked, 1)
                else:
                    v.tensor_tensor(s, b[:, 0:384], mask, ALU.add).then_inc(scores_masked, 1)
                dve.wait_ge(scores_masked, h + 1)
                if h < 24:
                    ins = v.tensor_reduce(st[:, 0:1], s[:, 0:P], X, ALU.max, negate=True)
                    ins = v.tensor_reduce(st[:, 1:2], s[:, P:384], X, ALU.max, negate=True)
                    if 8 <= h < 16:
                        link(ins)
                        link(v.tensor_scalar(st[:, 8:9], vec[:, VEC["sink"]][:, h - 8:h - 7], -1.0, None, ALU.mult))
                        ins = v.tensor_scalar(st[:, 0:2], st[:, 0:2], st[:, 8:9], None, ALU.min)
                    ins.then_inc(max_ready, 1)
                    dve.wait_ge(exp_done, h + 1)
                    if 8 <= h < 16:
                        link(v.tensor_tensor(st[:, 2:4], st[:, 2:4], st[:, 4:6], ALU.add))
                    link(v.reciprocal(st[:, 6:8], st[:, 2:4]))
                    v.tensor_scalar(s[:, 0:P], s[:, 0:P], st[:, 6:7], None, ALU.mult)
                    v.tensor_scalar(s[:, P:384], s[:, P:384], st[:, 7:8], None, ALU.mult).then_inc(probs_ready, 1)
                else:
                    dve.wait_ge(exp_done, h + 1)
                    z = soft[:, h % 2, :]
                    v.scalar_tensor_tensor(z, s, 0.0, z, ALU.max, ALU.add).then_inc(probs_ready, 1)

            def turned(h):
                if h >= 24:
                    dve.wait_ge(pt_done, h + 1)
                    s = score[:, h % 2, :]
                    v.tensor_tensor(s, s, trans_bank[h % 2][:, 0:384], ALU.subtract).then_inc(stick_ready, 1)

            def outputs(h):
                if h % 2 == 0:
                    return
                dve.wait_ge(o_done, h + 1)
                mixer = (0, 1, 0, 1)[h // 8]
                y = mixed[:, mixer, (h % 8) // 2, :]
                if h < 16:
                    if h in (1, 9):
                        dve.wait_ge(*evicted(("fm", "cz" if h == 1 else "bz", 1)))
                    v.tensor_tensor(y, o_bank[:, 0:T], y, ALU.mult).then_inc(o_evicted, 1)
                else:
                    v.tensor_copy(y, o_bank[:, 0:T]).then_inc(o_evicted, 1)

            def logf():
                dve.wait_ge(fox_log, 1)
                link(v.scalar_tensor_tensor(fox[:, 3, :], fox[:, 0, :], 0.0, fox[:, 1, :], ALU.min, ALU.subtract))
                v.tensor_tensor_scan(fox[:, 2, :], ones[0:8, 0:T], fox[:, 3, :], 0.0, ALU.mult, ALU.add)\
                 .then_inc(fox_ready, 1)

            def ranks(dst, logits, n, scratch):
                other = logits.unsqueeze(2).to_broadcast([P, n, 4, 4])
                own = logits.unsqueeze(3).to_broadcast([P, n, 4, 4])
                more = rt[:, scratch:scratch + 16 * n].rearrange("p (n i j) -> p n i j", n=n, i=4)
                same = rt[:, scratch + 16 * n:scratch + 32 * n].rearrange("p (n i j) -> p n i j", n=n, i=4)
                tie = cs("tie").rearrange("p (i j) -> p i j", i=4).unsqueeze(1).to_broadcast([P, n, 4, 4])
                v.tensor_tensor(more, other, own, ALU.is_gt)
                link(v.tensor_tensor(same, other, own, ALU.is_equal))
                link(v.tensor_tensor(same, same, tie, ALU.mult))
                link(v.tensor_tensor(more, more, same, ALU.add))
                link(v.tensor_reduce(dst, more, X, ALU.add))

            def route():
                v.memset(y_pair, 0.0).then_inc(y_ready, 2)
                v.memset(combT, 0.0).then_inc(combT_evicted, 1)
                dve.wait_ge(*evicted(("logit", 1)))
                fours = TT + TT * 4
                logits = rt[:, 32:72].rearrange("p (n e) -> p n e", e=4)
                shifted = rt[:, 100:140].rearrange("p (n e) -> p n e", e=4)
                gd, ed = shifted[:, 0:TT], shifted[:, TT:fours]
                most = rt[:, 80:90]
                link(v.tensor_reduce(most, logits, X, ALU.max))
                v.tensor_tensor(shifted, logits, most.unsqueeze(2).to_broadcast([P, fours, 4]), ALU.subtract)\
                 .then_inc(group_shifted, 1)
                rank = rt[:, 150:190].rearrange("p (n e) -> p n e", e=4)
                ranks(rank, logits, fours, 400)
                erank = rank[:, TT:fours]
                top = rt[:, 200:208]
                two = rt[:, 210:242].rearrange("p (n e) -> p n e", e=4)
                v.tensor_scalar(top, rt[:, 150:158], 0.5, None, ALU.is_lt)
                link(v.tensor_scalar(two, erank, 1.5, None, ALU.is_lt))
                sel = rt[:, 0:32].rearrange("p (n e) -> p n e", e=4)
                v.tensor_tensor(sel, two, top.unsqueeze(2).to_broadcast([P, 8, 4]), ALU.mult).then_inc(sel_ready, 1)
                dve.wait_ge(group_exp, 1)
                gsum, esum, f = rt[:, 250:252], rt[:, 254:262], rt[:, 264:272]
                v.tensor_reduce(gsum, gd, X, ALU.add)
                link(v.tensor_tensor(ed, ed, two, ALU.mult))
                link(v.tensor_reduce(esum, ed, X, ALU.add))
                v.reciprocal(gsum, gsum)
                link(v.reciprocal(f, esum))
                link(v.tensor_tensor(f, f, top, ALU.mult))
                link(v.tensor_tensor(f.rearrange("p (t g) -> p t g", t=TT), f.rearrange("p (t g) -> p t g", t=TT),
                                     gsum.unsqueeze(2).to_broadcast([P, TT, 4]), ALU.mult))
                comb = rt[:, 1000:1036].rearrange("p (t e) -> p t e", t=TT)
                for t in range(TT):
                    last = v.tensor_tensor(comb[:, t, 0:16].rearrange("p (g e) -> p g e", e=4), ed[:, 4 * t:4 * t + 4, :],
                                           f[:, 4 * t:4 * t + 4].unsqueeze(2).to_broadcast([P, 4, 4]), ALU.mult)
                link(last)
                link(v.tensor_copy(comb[:, :, 16:18], comb[:, :, 0:2]))

            def slots():
                dve.wait_ge(*evicted(("rank",)))
                v.tensor_tensor(onehot, iota, columns(pos, 0), ALU.is_equal).then_inc(onehot_ready, 1)
                r = rt[:, 344:348]
                for i in range(3):
                    last = v.tensor_scalar(r[:, i:i + 1], rt[:, 340:341], SLOTS * (i + 1) + 0.5, None, ALU.is_gt)
                link(last)
                link(v.tensor_reduce(r[:, 3:4], r[:, 0:3], X, ALU.add))
                v.tensor_scalar(n_rounds[:, :], r[:, 3:4], 1.0, None, ALU.add).then_inc(rounds_ready, 1)

            pos = rt[:, 300:336].rearrange("p (t e) -> p t e", t=TT)
            comb = rt[:, 1000:1036].rearrange("p (t e) -> p t e", t=TT)
            iota = cs("iota").unsqueeze(1).unsqueeze(1).to_broadcast([P, TT, 2, SLOTS])

            def columns(ap, pair):
                return ap[:, :, bass.ds(pair * 2, 2)].unsqueeze(3).to_broadcast([P, TT, 2, SLOTS])

            n = 0
            for s in STEPS:
                if s[0] == "unit":
                    unit(n, s[1:])
                    n += 1
                elif s[0] not in ("begin", "split", "y_split", "sigmoid", "load_final_g", "load_late"):
                    dict(norm_half=norm_half, split_low=split_low, y_split_low=y_split_low, fa_split=fa_split, norm=norm, ada=ada, S=probs, T=turned, V=outputs, pool=pool, mods=mods, logf=logf,
                         route=route, slots=slots)[s[0]](*s[1:])

            def xg_half(it):
                dve.wait_ge(gather_done, it * 2 + 2)
                for k in range(4, KD):
                    last = v.tensor_scalar(xg[:, k, :], x_bank[1][:, (k - 4) * P:(k - 3) * P], aff[:, 1, k:k + 1],
                                           mod[:, 7, k - 4:k - 3], ALU.mult, ALU.add)
                last.then_inc(xg_dve, 1)

            xg_half(0)
            dve.wait_ge(rounds_ready, 1)
            rounds = dve.value_load(n_rounds[0:1, 0:1], min_val=1, max_val=T // SLOTS)
            with dve.Fori(0, rounds) as r:
                with dve.Fori(0, PAIRS) as pair:
                    it = r * PAIRS + pair
                    dve.wait_ge(onehot_ready, it + 1)
                    v.tensor_tensor(combine, onehot, columns(comb, pair), ALU.mult).then_inc(combine_ready, 1)
                    dve.wait_ge(gather_done, it * 2 + 2)
                    dve.wait_ge(combine_ready, it + 1)
                    v.tensor_tensor(onehot, iota, columns(pos, pair + 1), ALU.is_equal).then_inc(onehot_ready, 1)
                    for e in range(2):
                        dve.wait_ge(silu_done, it * 2 + e + 1)
                        v.tensor_tensor(act[e * SLOTS:(e + 1) * SLOTS, :], sil[HD:P, e, :], gu_bank[e][HD:P, :], ALU.mult)\
                         .then_inc(act_ready, 1)
                    dve.wait_ge(combT_done, it + 1)
                    dve.wait_ge(scatter_done, it + 1)
                    v.tensor_copy(combT, gu_bank[0][:, 0:T]).then_inc(combT_evicted, 1)
                    xg_half(it + 1)
                    for e in range(2):
                        dve.wait_ge(down_done, it * 2 + e + 1)
                        rows = slice(e * SLOTS, (e + 1) * SLOTS)
                        v.tensor_tensor(y_pair[rows, 0:W512], gu_bank[e][0:HD, :], gate_rows[0:HD, 1, 0:W512], ALU.mult)
                        v.tensor_tensor(y_pair[rows, W512:D], gu_bank[e][HD:P, :], gate_rows[HD:P, 1, W512:D], ALU.mult)\
                         .then_inc(y_ready, 1)
                dve.wait_ge(onehot_ready, r * PAIRS + PAIRS + 1)
                v.tensor_scalar(pos, pos, -float(SLOTS), None, ALU.add)
            for t in range(TT):
                norm(4, t)


_MATRICES = ["x", "w_in", "pool_w", "w_proj_a", "w_proj_b", "w_proj_c", "w_out", "ada_w_2", "w_in_2",
             "w_branch_fox_2", "w_branch_sb_2", "w_out_2", "expert_w_gate_2", "expert_w_up_2", "expert_w_down_2"]


def kernel(**inputs):
    import concourse.bacc as bacc
    from concourse.bass_utils import run_bass_kernel_spmd

    inp = {k: np.asarray(v) for k, v in inputs.items()}
    columns = lambda v: v.reshape(-1, P).T
    rows = lambda v: np.broadcast_to(v.reshape(1, -1), (P, v.size))
    forget = np.zeros((P, 1), np.float32)
    forget[0:8, 0] = inp["b_forget_2"][0]
    router_b = np.concatenate([inp["router_group_b_2"][0], inp["router_expert_b_2"][0]])
    vec = np.concatenate([np.full((P, 1), EPS, np.float32), columns(inp["norm_g"]), columns(inp["norm1_g_2"]), columns(inp["norm2_g_2"]),
                          columns(inp["c_2"]), columns(inp["pool_scale"]), columns(inp["ada_b_2"]), forget,
                          rows(inp["sink_logits"]), rows(router_b)], 1)
    ada_b = inp["ada_b_2"].reshape(N_MOD, D)
    arrays = {n: np.ascontiguousarray(inp[n]) for n in _MATRICES}
    arrays["con"] = constants()
    w_bq = inp["w_in"][0][:, IN1["bq"]:IN1["bq"] + W512]
    arrays["w_bq"] = np.ascontiguousarray(w_bq.reshape(D, 2, 4, HD).transpose(0, 2, 1, 3).reshape(D, W512))
    arrays["vec"] = np.ascontiguousarray(vec)
    arrays["fin1"] = np.ascontiguousarray(rows(inp["final_norm_g"]))
    arrays["fin2"] = np.ascontiguousarray(rows(inp["final_g_2"]))
    arrays["gate_b"] = np.ascontiguousarray(np.stack([rows(ada_b[2]), rows(ada_b[5])], 1))
    arrays["router_w"] = np.ascontiguousarray(np.concatenate([inp["router_group_w_2"][0], inp["router_expert_w_2"][0]], 1))

    nc = bacc.Bacc("TRN2", target_bir_lowering=False, num_devices=1, dynamic_dma_scratch_size=1024)
    aps = {n: nc.dram_tensor("in_" + n, v.shape, mybir.dt.from_np(v.dtype), kind="ExternalInput").ap()
           for n, v in arrays.items()}
    out = nc.dram_tensor("out", (1, T, D), F32, kind="ExternalOutput").ap()
    two_block_kernel(nc, aps, out)
    result = run_bass_kernel_spmd(nc, [{"in_" + n: v for n, v in arrays.items()}], core_ids=[0])
    return result.results[0]["out"]
```
